# Optimizing a Trainium2 kernel written in Bass

```python
import jax, jax.numpy as jnp
from jax import lax
import numpy as np

D_MODEL = 1024
BATCH = 1
SEQ = 1024
DEPTH = 1

HEAD_DIM = 64
N_ATTN_HEADS = 8
N_KV_HEADS = 2
GQA_GROUP = N_ATTN_HEADS // N_KV_HEADS
ATTN_WIDTH = N_ATTN_HEADS * HEAD_DIM
KV_WIDTH = N_KV_HEADS * HEAD_DIM
N_RWKV_HEADS = 8
RWKV_WIDTH = N_RWKV_HEADS * HEAD_DIM
MIX_WIDTH = ATTN_WIDTH + RWKV_WIDTH
WINDOW = 128
BLOCK = 128
DECAY_LORA = 64
ICLR_LORA = 64
GATE_LORA = 128
RWKV_SHIFT_WIDTH = 3 * RWKV_WIDTH + DECAY_LORA + ICLR_LORA + GATE_LORA
IN_WIDTH = ATTN_WIDTH + 2 * KV_WIDTH + RWKV_SHIFT_WIDTH
D_FF = 4 * D_MODEL
RMS_EPS = 1e-6
GN_EPS = 64e-5
L2_EPS = 1e-12
NEG_INF = -1e30

kernel_name = 'hybrid_swa_sink_alibi_rwkv7_block'

def rms_norm(x, g):
    xf = x.astype(jnp.float32)
    y = xf * lax.rsqrt(jnp.mean(xf * xf, axis=-1, keepdims=True) + RMS_EPS)
    return (y * g.astype(jnp.float32)).astype(x.dtype)

def alibi_slopes():
    h = jnp.arange(1, N_ATTN_HEADS + 1, dtype=jnp.float32)
    return jnp.exp2(-8.0 * h / N_ATTN_HEADS)

def sliding_window_attention(q, k, v, sinks):
    B, T = q.shape[0], q.shape[1]
    nb = T // BLOCK
    qb = q.reshape(B, nb, BLOCK, N_KV_HEADS, GQA_GROUP, HEAD_DIM)

    def band(t):
        tp = jnp.pad(t, ((0, 0), (BLOCK, 0), (0, 0), (0, 0)))
        tp = tp.reshape(B, nb + 1, BLOCK, N_KV_HEADS, HEAD_DIM)
        return jnp.concatenate([tp[:, :-1], tp[:, 1:]], axis=2)

    kb, vb = band(k), band(v)
    s = jnp.einsum('bnqkgd,bnskd->bnkgqs', qb, kb).astype(jnp.float32) * (HEAD_DIM ** -0.5)
    qi = jnp.arange(BLOCK)[:, None]
    kj = jnp.arange(2 * BLOCK)[None, :]
    dist = qi - kj + BLOCK
    bias = -alibi_slopes().reshape(N_KV_HEADS, GQA_GROUP, 1, 1) * dist.astype(jnp.float32)
    key_pos = jnp.arange(nb)[:, None] * BLOCK + jnp.arange(2 * BLOCK)[None, :] - BLOCK
    valid = ((dist >= 0) & (dist < WINDOW))[None] & (key_pos >= 0)[:, None, :]
    s = jnp.where(valid[None, :, None, None], s + bias, NEG_INF)
    sink = sinks.astype(jnp.float32).reshape(1, 1, N_KV_HEADS, GQA_GROUP, 1, 1)
    m = jnp.maximum(jnp.max(s, axis=-1, keepdims=True), sink)
    e = jnp.exp(s - m)
    p = e / (jnp.sum(e, axis=-1, keepdims=True) + jnp.exp(sink - m))
    o = jnp.einsum('bnkgqs,bnskd->bnqkgd', p.astype(vb.dtype), vb)
    return o.reshape(B, T, ATTN_WIDTH)

def rwkv7_recurrence(r, w, k, v, a, b):
    B, _, H, N = r.shape

    def step(S, inp):
        rt, wt, kt, vt, at, bt = inp
        sa = jnp.einsum('bhij,bhj->bhi', S, at)
        S = S * wt[:, :, None, :] + sa[..., None] * bt[:, :, None, :] + vt[..., None] * kt[:, :, None, :]
        return S, jnp.einsum('bhij,bhj->bhi', S, rt)

    xs = tuple(jnp.moveaxis(t, 1, 0) for t in (r, w, k, v, a, b))
    S0 = jnp.zeros((B, H, N, N), jnp.float32)
    _, y = lax.scan(step, S0, xs)
    return jnp.moveaxis(y, 0, 1)

def rwkv7_time_mix(xr, xk, xv, xw, xa, xg, w0, w2, a0, a2, g2, k_k, k_a, r_k, ln_w, ln_b):
    out_dtype = xr.dtype
    f = lambda t: t.astype(jnp.float32)
    xr, xk, xv, xw, xa, xg = f(xr), f(xk), f(xv), f(xw), f(xa), f(xg)
    B, T, _ = xr.shape
    heads = lambda t: t.reshape(B, T, N_RWKV_HEADS, HEAD_DIM)
    w_log = -jax.nn.softplus(-(f(w0) + jnp.tanh(xw) @ f(w2))) - 0.5
    decay = jnp.exp(-jnp.exp(w_log))
    a = jax.nn.sigmoid(f(a0) + xa @ f(a2))
    g = jax.nn.sigmoid(xg) @ f(g2)
    kk = heads(xk * f(k_k))
    kk = kk / jnp.maximum(jnp.sqrt(jnp.sum(kk * kk, axis=-1, keepdims=True)), L2_EPS)
    k = xk * (1.0 + (a - 1.0) * f(k_a))
    r_h, k_h, v_h, a_h = heads(xr), heads(k), heads(xv), heads(a)
    y = rwkv7_recurrence(r_h, heads(decay), k_h, v_h, -kk, kk * a_h)
    mu = jnp.mean(y, axis=-1, keepdims=True)
    var = jnp.mean(jnp.square(y - mu), axis=-1, keepdims=True)
    y = ((y - mu) * lax.rsqrt(var + GN_EPS)).reshape(B, T, RWKV_WIDTH) * f(ln_w) + f(ln_b)
    bonus = jnp.sum(r_h * k_h * f(r_k).reshape(N_RWKV_HEADS, HEAD_DIM), axis=-1, keepdims=True) * v_h
    y = (y + bonus.reshape(B, T, RWKV_WIDTH)) * g
    return y.astype(out_dtype)

def setup_inputs(seed: int = 0) -> dict:
    key = jax.random.key(seed)
    ks = jax.random.split(key, 20)
    f32 = jnp.float32
    L = DEPTH

    def nrm(k, shape, scale):
        return jax.random.normal(k, shape, f32) * scale

    return {
        'x': nrm(ks[0], (BATCH, SEQ, D_MODEL), 1.0),
        'attn_norm_g': 1.0 + nrm(ks[1], (L, D_MODEL), 0.02),
        'w_in': nrm(ks[2], (L, D_MODEL, IN_WIDTH), D_MODEL ** -0.5),
        'attn_sinks': nrm(ks[3], (L, N_ATTN_HEADS), 1.0),
        'rwkv_mu': jax.random.uniform(ks[4], (L, RWKV_SHIFT_WIDTH), f32),
        'w0': jax.random.uniform(ks[5], (L, RWKV_WIDTH), f32, -4.0, 0.0),
        'w2': nrm(ks[6], (L, DECAY_LORA, RWKV_WIDTH), 0.5 * DECAY_LORA ** -0.5),
        'a0': nrm(ks[7], (L, RWKV_WIDTH), 0.1),
        'a2': nrm(ks[8], (L, ICLR_LORA, RWKV_WIDTH), ICLR_LORA ** -0.5),
        'g2': nrm(ks[9], (L, GATE_LORA, RWKV_WIDTH), GATE_LORA ** -0.5),
        'k_k': 0.85 + nrm(ks[10], (L, RWKV_WIDTH), 0.02),
        'k_a': 1.0 + nrm(ks[11], (L, RWKV_WIDTH), 0.02),
        'r_k': nrm(ks[12], (L, RWKV_WIDTH), 0.1),
        'ln_x_w': 1.0 + nrm(ks[13], (L, RWKV_WIDTH), 0.02),
        'ln_x_b': nrm(ks[14], (L, RWKV_WIDTH), 0.02),
        'w_out': nrm(ks[15], (L, MIX_WIDTH, D_MODEL), MIX_WIDTH ** -0.5),
        'mlp_norm_g': 1.0 + nrm(ks[16], (L, D_MODEL), 0.02),
        'w_up': nrm(ks[17], (L, D_MODEL, D_FF), D_MODEL ** -0.5),
        'w_down': nrm(ks[18], (L, D_FF, D_MODEL), D_FF ** -0.5),
        'final_norm_g': 1.0 + nrm(ks[19], (D_MODEL,), 0.02),
    }

def reference(x, attn_norm_g, w_in, attn_sinks, rwkv_mu, w0, w2, a0, a2, g2, k_k, k_a, r_k,
              ln_x_w, ln_x_b, w_out, mlp_norm_g, w_up, w_down, final_norm_g):
    B, T, _ = x.shape
    c1 = ATTN_WIDTH
    c2 = c1 + KV_WIDTH
    c3 = c2 + KV_WIDTH
    r1 = RWKV_WIDTH
    r2 = 2 * RWKV_WIDTH
    r3 = 3 * RWKV_WIDTH
    r4 = r3 + DECAY_LORA
    r5 = r4 + ICLR_LORA
    for l in range(DEPTH):
        h = rms_norm(x, attn_norm_g[l])
        z = h @ w_in[l]
        q = z[..., :c1].reshape(B, T, N_ATTN_HEADS, HEAD_DIM)
        ka = z[..., c1:c2].reshape(B, T, N_KV_HEADS, HEAD_DIM)
        va = z[..., c2:c3].reshape(B, T, N_KV_HEADS, HEAD_DIM)
        attn_out = sliding_window_attention(q, ka, va, attn_sinks[l])
        zr = z[..., c3:]
        zr_prev = jnp.pad(zr, ((0, 0), (1, 0), (0, 0)))[:, :-1]
        zs = zr + (zr_prev - zr) * rwkv_mu[l]
        rwkv_out = rwkv7_time_mix(zs[..., :r1], zs[..., r1:r2], zs[..., r2:r3],
                                  zs[..., r3:r4], zs[..., r4:r5], zs[..., r5:],
                                  w0[l], w2[l], a0[l], a2[l], g2[l], k_k[l], k_a[l], r_k[l],
                                  ln_x_w[l], ln_x_b[l])
        x = x + jnp.concatenate([attn_out, rwkv_out], axis=-1) @ w_out[l]
        h = rms_norm(x, mlp_norm_g[l])
        x = x + jnp.square(jax.nn.relu(h @ w_up[l])) @ w_down[l]
    return rms_norm(x, final_norm_g)


_drawn_inputs = setup_inputs


def setup_inputs(seed=0):
    import zlib

    import numpy as np

    out = dict(_drawn_inputs(seed))
    spreads = {}
    factors = {'attn_norm_g': 3.44,
     'w2': 3.881,
     'a0': 3.799,
     'k_k': 200.0,
     'k_a': 6.749,
     'ln_x_w': 196.383,
     'ln_x_b': 200.0,
     'mlp_norm_g': 15.977,
     'final_norm_g': 23.154,
     'attn_sinks': 64.0}
    for name, (base, spread) in spreads.items():
        noise = np.random.default_rng([zlib.crc32(name.encode()), seed]).standard_normal(out[name].shape)
        drawn = base * np.exp(spread * noise) if base else spread * noise
        out[name] = __import__('jax').numpy.asarray(drawn.astype(out[name].dtype))
    for name, factor in factors.items():
        out[name] = (out[name] * factor).astype(out[name].dtype)
    return out
```

```python
from contextlib import ExitStack
import math

import concourse.bass as bass
from concourse import mybir

F32 = mybir.dt.float32
F32R = mybir.dt.float32r
ALU = mybir.AluOpType
ACT = mybir.ActivationFunctionType
AX = mybir.AxisListType

P = 128
SEQ = 1024
D = 1024
KT = D // P
HEAD = 64
HEADS = 8
KV = 2
PAIRS = HEADS // 2
CHUNK = 64
TILES = SEQ // P
CHUNKS = P // CHUNK
HALF = 512
D_FF = 4 * D
Q0, K0, V0, R0 = 0, 4, 5, 6
RK0, RV0, RWA, RG = 10, 14, 18, 19
N_IN = 20
N_SHIFT = N_IN - R0
N_OUT = 8
GROUPS = 4
UNITS = N_IN + N_OUT + GROUPS * 16
RMS_EPS = 1e-6
GN_EPS = 64e-5
L2_EPS = 1e-12
LOG_DECAY = math.exp(-0.5)
SCALE = HEAD ** -0.5
FAR = 1.0e32
LEVELS = CHUNK.bit_length() - 1

C_MU, C_W0, C_A0, C_KK, C_KA, C_RK = 0, 14, 18, 22, 26, 30
C_G1, C_G2, N_VEC = 34, 42, 50

BANK_USES = {
    0: ["lab0", "xt0", "y0_1", "y0_2", "y0_3", "y0_4", "y0_5", "rq", "outT"],
    1: ["lab1", "xt1", "y1_1", "y1_2", "y1_3", "y1_4", "y1_5", "st0", "st1"],
    2: ["mrb0", "mrk0", "z0_1", "z0_2", "z0_3", "z0_4", "w", "yy"],
    3: ["mrb1", "mrk1", "z1_1", "z1_2", "z1_3", "z1_4", "g", "gate"],
    4: ["lak0", "lv", "zt0_1", "zt0_2", "zt0_3", "zt0_4", "zt0_5", "c0"],
    5: ["lak1", "zt1_1", "zt1_2", "zt1_3", "zt1_4", "zt1_5", "c1"],
    6: ["lora_w", "ss", "tr_a", "tr_k", "bonus", "vt", "sc00", "sc01", "pt00", "pt01", "o"],
    7: ["lora_a", "tr_b", "tr_v", "sc10", "sc11", "pt10", "pt11", "oT"],
}
READER = {
    "lora_w": ("xw0", 1, 1), "lora_a": ("aa0", 1, 1), "ss": ("ssm", 1, 1), "bonus": ("bonus", 1, 1),
    "tr_a": ("A_tok", 1, 1), "tr_b": ("B_tok", 1, 1), "tr_k": ("K_tok", 1, 1), "tr_v": ("V_tok", 1, 1),
    "vt": ("va_tok", 1, 1), "o": ("o", 1, 1), "oT": ("oT", 1, 1), "lv": ("LV", 1, 1), "w": ("W", 1, 1),
    "g": ("G", 1, 1), "rq": ("QT", 1, 1), "yy": ("y", 1, 1), "gate": ("gate", 1, 1), "outT": ("rw", 1, 1),
}
for _i, _n in enumerate(("00", "10", "01", "11")):
    READER["sc" + _n] = ("sc", 8, 2 * _i + 2)
    READER["pt" + _n] = ("pT", 4, _i + 1)
for _g in range(2):
    READER[f"lab{_g}"] = ("LT", 2, _g + 1)
    READER[f"lak{_g}"] = ("LakT", 2, _g + 1)
    READER[f"mrb{_g}"] = ("MrbT", 2, _g + 1)
    READER[f"mrk{_g}"] = ("MrkR", 2, _g + 1)
    READER[f"xt{_g}"] = ("X", 2 * (LEVELS - 1), _g + 1)
    READER[f"c{_g}"] = ("phi", 4, 2 * _g + 2)
    READER[f"st{_g}"] = ("state", 2, _g + 1)
    for _k in range(1, LEVELS):
        READER[f"y{_g}_{_k}"] = ("IY", 2 * (LEVELS - 1), 2 * (_k - 1) + _g + 1)
        READER[f"z{_g}_{_k}"] = ("X", 2 * (LEVELS - 1), 2 * _k + _g + 1)
        READER[f"zt{_g}_{_k}"] = ("XT", 2 * (LEVELS - 1), 2 * (_k - 1) + _g + 1)

USE = {name: (b, i) for b, names in BANK_USES.items() for i, name in enumerate(names)}



def build(nc, x, w_all, vec, sinks, w2a2, g2, ln_w, ln_b, fin_g, out):
    with ExitStack() as ctx:
        def sb(name, shape, dt=F32):
            return ctx.enter_context(nc.sbuf_tensor(name, shape, dt))

        vecs = sb("vecs", [P, N_VEC])
        ident = sb("ident", [P, P])
        ones = sb("ones", [P, P])
        w_raw = [sb(f"w_raw{i}", [P, KT, P]) for i in range(2)]
        neg_half = sb("neg_half", [P, 8])
        BASE = -(-nc.sbuf_base // 64) * 64
        TOP = nc.sbuf_usable_end // 64 * 64
        KB4 = 4 * SEQ

        class Region:

            def __init__(self, base, end=TOP):
                self.at, self.end = base, end

            def __call__(self, name, shape, dt=F32):
                t = nc.alloc_sbuf_tensor_at(name, shape, dt, offset=self.at)
                self.at += -(-4 * math.prod(shape[1:]) // 32) * 32
                assert self.at <= self.end, (name, self.at, self.end)
                return t

        r = Region(TOP - 4 * KB4)
        w_hi = [r(f"w_hi{i}", [P, KT, P], F32R) for i in range(2)]
        w_lo = [r(f"w_lo{i}", [P, KT, P], F32R) for i in range(2)]
        W_AT = TOP - 4 * KB4

        r = Region(BASE)
        zT = r("zT", [P, N_IN, SEQ])
        w2a2_s = r("w2a2_s", [P, 512])
        g2_s = r("g2_s", [P, 512])
        lnw_s = r("lnw_s", [P, 512])
        lnb_s = r("lnb_s", [P, 512])
        strict = r("strict", [P, P])
        incl = r("incl", [P, P])
        level = [r(f"level{k}", [P, P]) for k in range(LEVELS)]
        dist = r("dist", [P, 2 * P])
        pair_ones = r("pair_ones", [P, P])
        ident64 = r("ident64", [P, HEAD])
        rk_w = r("rk_w", [P, PAIRS, 2])
        keep = r("keep", [P, 512])
        sink_s = r("sink_s", [P, HEADS])
        CONST_END = r.at

        r = Region(CONST_END, W_AT)
        h_hi = r("h_hi", [P, KT, SEQ], F32R)
        h_lo = r("h_lo", [P, KT, SEQ], F32R)
        xs = [r(f"xs{i}", [P, D]) for i in range(2)]
        h_raw = [r(f"h_raw{i}", [P, 4, P]) for i in range(2)]
        z_tmp = [r(f"z_tmp{i}", [P, 1 + SEQ]) for i in range(2)]
        ss1 = r("ss1", [P, TILES])
        rs1 = r("rs1", [P, TILES])

        r = Region(CONST_END)
        block = [P, PAIRS, P]
        toks = [P, HEADS, HEAD]
        at = r("at", block)
        rt = r("rt", block)
        bt = r("bt", block)
        kt = r("kt", block)
        rq = r("rq", block)
        A_tok = [r(f"A_tok{i}", toks) for i in range(2)]
        B_tok = [r(f"B_tok{i}", toks) for i in range(2)]
        K_tok = [r(f"K_tok{i}", toks) for i in range(2)]
        V_tok = [r(f"V_tok{i}", toks) for i in range(2)]
        va_tok = [r(f"va_tok{i}", [P, P]) for i in range(2)]
        xw = r("xw", block)
        aa = r("aa", block)
        kk = r("kk", block)
        cs = r("cs", block)
        dm = r("dm", block)
        e1 = r("e1", block)
        e2 = r("e2", block)
        k2 = r("k2", block)
        tw = r("tw", [P, P])
        gs = [r(f"gs{i}", [P, P]) for i in range(2)]
        sc = [r(f"sc{i}", [P, 2, 2 * P]) for i in range(4)]
        LT = [r(f"LT{i}", block) for i in range(2)]
        MrbT = [r(f"MrbT{i}", block) for i in range(2)]
        MrkT = [r(f"MrkT{i}", block) for i in range(2)]
        LakT = [r(f"LakT{i}", block) for i in range(2)]
        LTk = [r(f"LTk{i}", block) for i in range(2)]
        X = [r(f"X{i}", block) for i in range(2)]
        XT = [r(f"XT{i}", block) for i in range(2)]
        W_s = r("W_s", toks)
        G_s = r("G_s", toks)
        QT = r("QT", block)
        phi = [r(f"phi{i}", block) for i in range(2)]
        psi = [r(f"psi{i}", block) for i in range(2)]
        state = [r(f"state{i}", block) for i in range(2)]
        LV = QT[:].rearrange("p a b -> p (a b)").rearrange("p (h d) -> p h d", d=HEAD)
        IY = LakT
        diag = X[0][:].rearrange("p a b -> p (a b)").rearrange("p (h d) -> p h d", d=HEAD)
        y_s, yc, y_sq, gate = LTk[0], LTk[1], LT[0], LT[1]
        pm = [r(f"pm{i}", [P, 2 * PAIRS]) for i in range(2)]
        pe_ = [r(f"pe{i}", [P, 2 * PAIRS]) for i in range(2)]
        pc = [r(f"pc{i}", [P, 2 * PAIRS]) for i in range(2)]
        bonus = [r(f"bonus{i}", [P, HEADS]) for i in range(2)]
        mx, nm, es, sums, den = (r(n, [P, HEADS]) for n in ("mx", "nm", "es", "sums", "den"))
        mu8, var8, rstd8 = (r(n, [P, HEADS]) for n in ("mu8", "var8", "rstd8"))

        r = Region(BASE + 10 * KB4)
        xs3 = [r(f"xs3_{i}", [P, D]) for i in range(2)]
        x2 = r("x2", [P, KT, SEQ])
        assert r.at == BASE + N_IN * KB4
        ACT_AT = W_AT - 16 * KB4
        r = Region(ACT_AT, W_AT)
        m_hi = r("m_hi", [P, KT, SEQ], F32R)
        m_lo = r("m_lo", [P, KT, SEQ], F32R)
        r = Region(BASE + N_IN * KB4, ACT_AT)
        sq3 = [r(f"sq3_{i}", [P, SEQ]) for i in range(2)]
        acc3 = r("acc3", [P, SEQ])
        rs3 = r("rs3", [P, SEQ])
        h3 = [r(f"h3_{i}", [P, SEQ]) for i in range(2)]
        r = Region(BASE)
        u_hi = r("u_hi", [P, KT, SEQ], F32R)
        u_r = [r(f"u_r{i}", [P, SEQ]) for i in range(2)]
        u_f = [r(f"u_f{i}", [P, SEQ]) for i in range(2)]
        r = Region(BASE + N_IN * KB4, ACT_AT)
        u_lo = r("u_lo", [P, KT, SEQ], F32R)
        r = Region(BASE)
        fg_s = r("fg_s", [P, D])
        o_s = [r(f"o_s{i}", [P, D]) for i in range(TILES)]
        sq5 = r("sq5", [P, D])
        ss5 = r("ss5", [P, 2 * TILES])
        rs5 = r("rs5", [P, TILES])

        ps = [ctx.enter_context(nc.psum_tensor(f"bank{i}", [P, 512], F32)) for i in range(8)]

        def sem(name):
            return ctx.enter_context(nc.semaphore(name))

        consts_in = sem("consts_in")
        w_in = [sem(f"w_in{i}") for i in range(2)]
        w_hi_ok, w_lo_ok = sem("w_hi_ok"), sem("w_lo_ok")
        proj_full = sem("proj_full")
        act_read, dve_read = sem("act_read"), sem("dve_read")
        x_in = [sem(f"x_in{i}") for i in range(2)]
        x_sq, x_rs, x_root, x_n = sem("x_sq"), sem("x_rs"), sem("x_root"), sem("x_n")
        tr_full, x2_in = sem("tr_full"), sem("x2_in")
        h_raw_ok, h_hi_ok, h_lo_ok = sem("h_raw_ok"), sem("h_hi_ok"), sem("h_lo_ok")
        masks_ok, mask_step = sem("masks_ok"), sem("mask_step")
        z_zero, z_copied, z_diff, z_ok = sem("z_zero"), sem("z_copied"), sem("z_diff"), sem("z_ok")
        bank_full = [sem(f"bank_full{b}") for b in range(8)]
        NAMES = """tw gs gg xw0 aa0 xw1 aa1 xw2 aa2 cs dm dp dpe pm pe e1 e2 pc kx ksq ssm root rn kk t1 t2 k2 at kka bt kt
            rt rk ah bh kh A_tok B_tok K_tok V_tok bonus va_tok sc mx m nm dsink es p den rden pT o oT
            LT MrbT LakT MrkR MrkT xt1 XT1 XT X LTk IY LV W G rq QT diag phi psi state
            y mu yc ysq var rs rstd yn1 yn2 yn3 yn4 bv gate yn5 rw zero""".split()
        done = {n: sem("s_" + n) for n in NAMES}
        m_hi_ok, m_lo_ok = sem("m_hi_ok"), sem("m_lo_ok")
        x2_sq, x2_acc = sem("x2_sq"), sem("x2_acc")
        ss3_full, rs3_ok, h3_raw = sem("ss3_full"), sem("rs3_ok"), sem("h3_raw")
        u_sq = sem("u_sq")
        fin_sq, fin_rs, fin_root, fin_y, fin_in, out_sent = (
            sem(n) for n in ("fin_sq", "fin_rs", "fin_root", "fin_y", "fin_in", "out_sent"))

        xv = x.rearrange("b (t p) d -> p (b t) d", p=P)
        ov = out.rearrange("b (t p) d -> p (b t) d", p=P)
        MIX_UNITS = N_IN
        U_UP = N_IN + N_OUT

        def bank(name):
            return ps[USE[name][0]]

        def wait_read(pe, name, t):
            key, each, i = READER[name]
            pe.wait_ge(done[key], each * t + i)

        def wait_bank(pe, name, t):
            b, i = USE[name]
            if i:
                wait_read(pe, BANK_USES[b][i - 1], t)
            elif t:
                wait_read(pe, BANK_USES[b][-1], t - 1)

        def wait_full(eng, name, t):
            b, i = USE[name]
            eng.wait_ge(bank_full[b], t * len(BANK_USES[b]) + i + 1)

        def filled(name):
            return bank_full[USE[name][0]]

        def tile(t):
            return slice(t * P, (t + 1) * P)

        def slot(g, i):
            return 2 * (2 * (g // 2) + i) + g % 2

        def halves(ap, g):
            return ap[HEAD * g:HEAD * (g + 1)]

        def per_chunk(ap):
            return ap.rearrange("p a (c t) -> p (a c) t", c=CHUNKS)

        def spread(ap, n):
            return ap.unsqueeze(2).to_broadcast([P, ap.shape[1], n])

        def across(ap, m):
            return ap.unsqueeze(1).to_broadcast([ap.shape[0], m, ap.shape[1]])

        def view(ap, m):
            return ap.rearrange("p (m n) -> p m n", m=m)

        def interleave(main, side):
            for _ in main:
                next(side, None)
            for _ in side:
                pass

        block_ = ctx.enter_context(nc.Block())

        @block_.sync
        def _(sp):
            sp.dma_start(vecs[:], vec).then_inc(consts_in, 16)

            def load_x(i, bufs, base):
                if i >= 2:
                    sp.wait_ge(tr_full, base + 2 * (i - 1))
                sp.dma_start(bufs[i % 2][:], xv[:, i, :]).then_inc(x_in[i % 2], 16)

            for i in range(2):
                load_x(i, xs, 0)
            for p in range(2):
                sp.dma_start(w_raw[p][:], w_all[p]).then_inc(w_in[p], 16)
            for i in range(2, TILES):
                load_x(i, xs, 0)
            for dst, src in ((w2a2_s, w2a2), (g2_s, g2), (lnw_s, ln_w.to_broadcast([P, 512])),
                             (lnb_s, ln_b.to_broadcast([P, 512])), (sink_s, sinks.to_broadcast([P, HEADS]))):
                sp.dma_start(dst[:], src).then_inc(consts_in, 16)

            def load_w(i):
                for p in range(2):
                    sp.wait_ge(w_hi_ok, 2 * i + p - 1)
                    sp.wait_ge(w_lo_ok, 2 * i + p - 1)
                    sp.dma_start(w_raw[p][:], w_all[2 * i + p]).then_inc(w_in[p], 16)

            with sp.Fori(1, MIX_UNITS // 2 + 1) as i:
                load_w(i)
            sp.wait_ge(done["oT"], TILES)
            sp.wait_ge(done["rw"], TILES)
            for i in range(TILES):
                load_x(i, xs3, 2 * TILES)
            with sp.Fori(MIX_UNITS // 2 + 1, UNITS // 2) as i:
                load_w(i)
            sp.wait_ge(proj_full, 2 * UNITS)
            sp.dma_start(fg_s[:], fin_g.to_broadcast([P, D])).then_inc(fin_in, 16)
            for i in range(TILES):
                sp.wait_ge(fin_y, 2 * (i + 1))
                sp.dma_start(ov[:, i, :], o_s[i][:]).then_inc(out_sent, 16)
            sp.wait_ge(out_sent, 16 * TILES)

        @block_.scalar
        def _(act):
            def A(o, i, f=ACT.Copy, **kw):
                return nc.scalar.activation(o, i, f, **kw)

            def need(name, n):
                if n > 0:
                    act.wait_ge(done[name], n)

            def split_w(m, p, first=False):
                n = 2 * m + p
                act.wait_ge(w_in[p], 16 * m + 16)
                if not first:
                    act.wait_ge(proj_full, 2 * n - 2)
                    act.wait_ge(w_lo_ok, n - 1)
                A(w_hi[p][:], w_raw[p][:]).then_inc(w_hi_ok, 1)

            def h_high(i):
                for j in range(2):
                    act.wait_ge(h_raw_ok, 2 * i + j + 1)
                    A(h_hi[:, 4 * j:4 * j + 4, tile(i)], h_raw[j][:]).then_inc(h_hi_ok, 1)

            for i in range(TILES):
                act.wait_ge(x_in[i % 2], 16 * (i // 2 + 1))
                if i:
                    act.wait_ge(x_sq, i)
                A(z_tmp[0][:, 1:], xs[i % 2][:], ACT.Square, accum_out=ss1[:, i:i + 1]).then_inc(x_sq, 1)
                if i == 0:
                    split_w(0, 0, first=True)
                    split_w(0, 1, first=True)
                else:
                    h_high(i - 1)
            h_high(TILES - 1)
            act.wait_ge(x_sq, TILES)

            def z_plain(m):
                for p in range(2):
                    n = 2 * m + p
                    for h in range(2):
                        act.wait_ge(proj_full, 2 * n + h + 1)
                        A(zT[:, bass.ds(n, 1), h * HALF:(h + 1) * HALF], ps[2 * p + h][:]).then_inc(act_read, 1)
                    split_w(m + 1, p)

            def z_shift(m, first=False, last=False):
                for p in range(2):
                    n = 2 * m + p
                    if first:
                        act.wait_ge(z_zero, 2)
                    else:
                        act.wait_ge(z_ok, n - R0 - 1)
                    for h in range(2):
                        act.wait_ge(proj_full, 2 * n + h + 1)
                        A(z_tmp[p][:, 1 + h * HALF:1 + (h + 1) * HALF], ps[2 * p + h][:])\
                            .then_inc(act_read, 1)
                    if not last:
                        split_w(m + 1, p)

            with act.Fori(0, R0 // 2) as i:
                z_plain(i)
            z_shift(R0 // 2, first=True)
            with act.Fori(R0 // 2 + 1, N_IN // 2 - 1) as i:
                z_shift(i)
            z_shift(N_IN // 2 - 1, last=True)

            act.wait_ge(z_ok, N_SHIFT)
            act.wait_ge(consts_in, 96)

            def side(t):
                b = t % 2
                T = tile(t)
                if t:
                    wait_full(act, "lora_w", t - 1)
                A(tw[0:64], zT[0:64, RWA, T], ACT.Tanh).then_inc(done["tw"], 1)
                if t > 1:
                    wait_full(act, "gate", t - 2)
                A(gs[b][:], zT[:, RG, T], ACT.Tanh, scale=0.5).then_inc(done["gs"], 1)
                need("kx", t + 1)
                need("kt", t)
                need("rk", t)
                A(k2[:], kk[:], ACT.Square).then_inc(done["ksq"], 1)
                need("xw0", t + 1)
                A(xw[:], xw[:], ACT.Tanh, scale=0.5).then_inc(done["xw1"], 1)
                need("aa0", t + 1)
                A(aa[:], aa[:], ACT.Tanh, scale=0.5).then_inc(done["aa1"], 1)
                yield
                need("ssm", t + 1)
                A(k2[:], k2[:], ACT.Sqrt).then_inc(done["root"], 1)
                need("cs", t + 1)
                A(pm[b][:], per_chunk(cs[:])[:, :, CHUNK // 2 - 1], ACT.Exp, scale=-LOG_DECAY).then_inc(done["pm"], 1)
                need("dm", t + 1)
                A(pe_[b][:], per_chunk(dm[:])[:, :, CHUNK - 1], ACT.Exp, scale=-LOG_DECAY).then_inc(done["pe"], 1)
                if t:
                    wait_full(act, "tr_k", t - 1)
                    wait_full(act, "bonus", t - 1)
                A(e2[:], dm[:], ACT.Exp, scale=LOG_DECAY).then_inc(done["e2"], 1)
                A(e1[:], dm[:], ACT.Exp, scale=-LOG_DECAY).then_inc(done["e1"], 1)
                need("dp", t + 1)
                A(xw[:], xw[:], ACT.Exp, scale=-LOG_DECAY).then_inc(done["dpe"], 1)
                yield
                for name, dst, key in (("tr_a", A_tok, "A_tok"), ("tr_b", B_tok, "B_tok"),
                                       ("tr_k", K_tok, "K_tok"), ("tr_v", V_tok, "V_tok")):
                    wait_full(act, name, t)
                    A(dst[b][:], view(bank(name)[:], HEADS)).then_inc(done[key], 1)
                wait_full(act, "bonus", t)
                A(bonus[b][:], bank("bonus")[:, 0:HEADS]).then_inc(done["bonus"], 1)
                wait_full(act, "vt", t)
                A(va_tok[b][:], bank("vt")[:, 0:P]).then_inc(done["va_tok"], 1)
                yield
                lo = P if t == 0 else 0
                need("dsink", t + 1)
                A(es[:], es[:], ACT.Exp).then_inc(done["es"], 1)
                need("nm", t + 1)
                for g in range(4):
                    for i in range(2):
                        c = slot(g, i)
                        A(sc[g][:, i, lo:], sc[g][:, i, lo:], ACT.Exp, bias=nm[:, c:c + 1], scale=SCALE,
                          accum_out=sums[:, c:c + 1]).then_inc(done["p"], 1)
                yield
                yield
                for g, name in enumerate(("pt00", "pt10", "pt01", "pt11")):
                    wait_full(act, name, t)
                    A(view(sc[g][:].rearrange("p a b -> p (a b)"), 4)[:, (1 if t == 0 else 0)::(2 if t == 0 else 1), :],
                      view(bank(name)[:], 4)[:, (1 if t == 0 else 0)::(2 if t == 0 else 1), :])\
                        .then_inc(done["pT"], 1)
                yield
                wait_full(act, "oT", t)
                A(zT[:, Q0:Q0 + PAIRS, T], view(bank("oT")[:], PAIRS)).then_inc(done["oT"], 1)
                yield

            def main(t):
                T = tile(t)
                yield
                for g in range(2):
                    wait_full(act, f"mrk{g}", t)
                    A(MrkT[g][:], view(bank(f"mrk{g}")[:], PAIRS)).then_inc(done["MrkR"], 1)
                need("phi", 4 * t)
                for g in range(2):
                    wait_full(act, f"xt{g}", t)
                    A(X[g][:], view(bank(f"xt{g}")[:], PAIRS)).then_inc(done["X"], 1)
                wait_full(act, "lv", t)
                A(LV, view(bank("lv")[:], HEADS)).then_inc(done["LV"], 1)
                yield
                for k in range(1, LEVELS):
                    for g in range(2):
                        for dst, key, n in ((X, "X", f"z{g}_{k}"), (XT, "XT", f"zt{g}_{k}")):
                            if n in USE:
                                wait_full(act, n, t)
                                A(dst[g][:], view(bank(n)[:], PAIRS)).then_inc(done[key], 1)
                    yield
                wait_full(act, "w", t)
                A(W_s[:], view(bank("w")[:], HEADS)).then_inc(done["W"], 1)
                yield
                need("state", 2 * t)
                for c in range(CHUNKS):
                    wait_full(act, f"c{c}", t)
                    for g in range(2):
                        src = halves(view(bank(f"c{c}")[:], PAIRS), g)[:, :, HEAD:]
                        A(halves(psi[c], g)[:, :, HEAD * g:HEAD * (g + 1)], src).then_inc(done["psi"], 1)
                yield
                wait_full(act, "yy", t)
                A(y_s[:], view(bank("yy")[:], PAIRS)).then_inc(done["y"], 1)
                wait_full(act, "gate", t)
                A(gate[:], view(bank("gate")[:], PAIRS)).then_inc(done["gate"], 1)
                need("yc", t + 1)
                A(y_sq[:], yc[:], ACT.Square).then_inc(done["ysq"], 1)
                yield
                wait_full(act, "outT", t)
                A(zT[:, R0:R0 + PAIRS, T], view(bank("outT")[:], PAIRS)).then_inc(done["rw"], 1)
                yield

            for _ in side(0):
                pass
            for t in range(TILES):
                interleave(main(t), side(t + 1) if t + 1 < TILES else iter(()))

            need("oT", TILES)
            need("rw", TILES)
            need("state", 2 * TILES)
            split_w(N_IN // 2, 0)
            split_w(N_IN // 2, 1)
            for k in range(KT):
                A(m_hi[:, k, :], zT[:, k if k < PAIRS else R0 + k - PAIRS, :]).then_inc(m_hi_ok, 1)
            for j in range(N_OUT):
                act.wait_ge(dve_read, 2 * j + 2)
                if j >= 2:
                    act.wait_ge(x2_acc, j - 1)
                A(sq3[j % 2][:], x2[:, j, :], ACT.Square).then_inc(x2_sq, 1)
                n = N_IN + j + 2
                split_w(n // 2, n % 2)
            act.wait_ge(rs3_ok, 2)
            A(rs3[:], rs3[:], ACT.Sqrt).then_inc(rs3_ok, 1)
            for k in range(KT):
                act.wait_ge(h3_raw, k + 1)
                A(m_hi[:, k, :], h3[k % 2][:]).then_inc(m_hi_ok, 1)

            def group(g, last=False):
                with act.Fori(0, 4) as i:
                    for p in range(2):
                        m = U_UP // 2 + 8 * g + i
                        n = 2 * m + p
                        for h in range(2):
                            act.wait_ge(proj_full, 2 * n + h + 1)
                            A(u_r[p][:, h * HALF:(h + 1) * HALF], ps[2 * p + h][:], ACT.Relu)\
                                .then_inc(act_read, 1)
                        split_w(m + 1, p)
                        act.wait_ge(u_sq, 8 * g + 2 * i + p + 1)
                        A(u_hi[:, bass.ds(2 * i + p, 1), :], u_f[p][:]).then_inc(m_hi_ok, 1)
                m = U_UP // 2 + 8 * g + 4
                with act.Fori(0, 3 if last else 4) as i:
                    for p in range(2):
                        split_w(m + i + 1, p)

            with act.Fori(0, GROUPS - 1) as g:
                group(g)
            group(GROUPS - 1, last=True)

            for i in range(TILES):
                for j in range(2):
                    f = 4 * TILES + 2 * i + j
                    act.wait_ge(tr_full, f + 1)
                    if f > 4 * TILES:
                        act.wait_ge(fin_sq, f - 4 * TILES)
                    A(sq5[:, 0:HALF], ps[4 + f % 4][:], ACT.Square, accum_out=ss5[:, 2 * i + j:2 * i + j + 1])\
                        .then_inc(fin_sq, 1)

        @block_.gpsimd
        def _(pool):
            G = nc.gpsimd
            steps = [0]

            def step(ins):
                steps[0] += 1
                ins.then_inc(mask_step, 1)
                pool.wait_ge(mask_step, steps[0])

            def select(ap, pattern, base, mult, fill, op=ALU.is_ge):
                step(G.affine_select(out=ap, in_=ap, compare_op=op, fill=fill, base=base, pattern=pattern,
                                     channel_multiplier=mult))

            step(G.memset(ident[:], 0.0))
            select(ident[:], [[-1, P]], 0, 1, 1.0, ALU.not_equal)
            step(G.memset(ones[:], 1.0))
            step(G.memset(neg_half[:], -0.5))
            for p in range(2):
                G.memset(z_tmp[p][:, 0:1], 0.0).then_inc(z_zero, 1)

            def high_h(i):
                for j in range(2):
                    n = 2 * i + j
                    pool.wait_ge(h_hi_ok, n + 1)
                    o = h_hi[:, 4 * j:4 * j + 4, tile(i)]
                    G.tensor_tensor(h_lo[:, 4 * j:4 * j + 4, tile(i)], h_raw[j][:], o.bitcast(F32), ALU.subtract)\
                        .then_inc(h_lo_ok, 1)

            def split_w(m, p):
                pool.wait_ge(w_hi_ok, 2 * m + p + 1)
                G.tensor_tensor(w_lo[p][:], w_raw[p][:], w_hi[p][:].bitcast(F32), ALU.subtract).then_inc(w_lo_ok, 1)

            split_w(0, 0)
            split_w(0, 1)
            def root(ap, ready, n, out_sem):
                pool.wait_ge(ready, n)
                G.tensor_tensor(ap, ap, neg_half[:, 0:1], ALU.pow).then_inc(out_sem, 1)

            for i in range(TILES):
                root(rs1[:, i:i + 1], x_rs, i + 1, x_root)
                if i:
                    high_h(i - 1)
            high_h(TILES - 1)
            for mask, first in ((strict, -1), (incl, 0)):
                step(G.memset(mask[:], 1.0))
                select(view(mask[:], CHUNKS), [[CHUNK, CHUNKS], [1, CHUNK]], first, -1, 0.0)
                select(view(mask[:], CHUNKS), [[-CHUNK, CHUNKS], [0, CHUNK]], 0, 1, 0.0)
            for k in range(LEVELS):
                w = 1 << k
                mk = view(level[k][:], P // (2 * w))
                step(G.memset(level[k][:], 1.0))
                step(G.memset(mk[:, :, 0:w], 0.0))
                select(mk, [[-2 * w, P // (2 * w)], [0, 2 * w]], 0, 1, 0.0)
                select(mk, [[2 * w, P // (2 * w)], [0, 2 * w]], w - 1, -1, 0.0)
            step(G.iota(dist[:], pattern=[[-1, 2 * P]], base=P, channel_multiplier=1,
                        allow_small_or_imprecise_dtypes=True))
            select(dist[:], [[-1, 2 * P]], P, 1, FAR)
            select(dist[:], [[1, 2 * P]], -1, -1, FAR)
            step(G.memset(pair_ones[:], 1.0))
            select(view(pair_ones[:], 2), [[-HEAD, 2], [0, HEAD]], 0, 1, 0.0)
            select(view(pair_ones[:], 2), [[HEAD, 2], [0, HEAD]], HEAD - 1, -1, 0.0)
            step(G.tensor_tensor(ident64[:], ident[:, 0:HEAD], ident[:, HEAD:P], ALU.add))
            step(G.memset(keep[:], 1.0))
            step(G.memset(view(keep[:], 2 * PAIRS)[:, :, 0:1], 0.0))
            step(G.memset(rk_w[:], 0.0))
            pool.wait_ge(consts_in, 96)
            for g in range(2):
                step(G.tensor_copy(halves(rk_w, g)[:, :, g], halves(vecs, g)[:, C_RK:C_RK + PAIRS]))

            with pool.Fori(1, N_IN // 2) as i:
                for p in range(2):
                    split_w(i, p)

            def need(name, n):
                if n > 0:
                    pool.wait_ge(done[name], n)

            def TT(o, a, b, op=ALU.mult):
                return G.tensor_tensor(o, a, b, op)

            def channels(c):
                return spread(vecs[:, c:c + PAIRS], P)

            pool.wait_ge(z_ok, N_SHIFT)
            for i in range(2):
                for tns in (phi[i], psi[i], state[i]):
                    o = G.memset(tns[:], 0.0)
            o.then_inc(done["zero"], 1)

            def side(t):
                b = t % 2
                T = tile(t)
                need("at", t)
                TT(kk[:], zT[:, RK0:RK0 + PAIRS, T], channels(C_KK)).then_inc(done["kx"], 1)
                need("gs", t + 1)
                G.tensor_scalar(gs[b][:], gs[b][:], 0.5, 0.5, ALU.mult, ALU.add).then_inc(done["gg"], 1)
                need("xw1", t + 1)
                G.tensor_scalar(xw[:], xw[:], 0.5, 0.5, ALU.mult, ALU.add).then_inc(done["xw2"], 1)
                need("aa1", t + 1)
                G.tensor_scalar(aa[:], aa[:], 0.5, 0.5, ALU.mult, ALU.add).then_inc(done["aa2"], 1)
                yield
                need("dm", t + 1)
                need("cs", t + 1)
                TT(xw[:], dm[:], xw[:], ALU.subtract).then_inc(done["dp"], 1)
                need("pm", t + 1)
                need("pe", t + 1)
                TT(pc[b][:], pm[b][:], pe_[b][:]).then_inc(done["pc"], 1)
                need("kk", t + 1)
                need("aa2", t + 1)
                G.tensor_scalar(k2[:], aa[:], -1.0, None, ALU.add).then_inc(done["t1"], 1)
                need("t1", t + 1)
                TT(k2[:], k2[:], channels(C_KA)).then_inc(done["t2"], 1)
                yield
                TT(aa[:], aa[:], kk[:]).then_inc(done["kka"], 1)
                need("kka", t + 1)
                need("e2", t + 1)
                if t:
                    wait_full(pool, "mrk1", t - 1)
                TT(bt[:], aa[:], e2[:]).then_inc(done["bt"], 1)
                need("e1", t + 1)
                TT(rt[:], zT[:, R0:R0 + PAIRS, T], e1[:]).then_inc(done["rt"], 1)
                need("bt", t + 1)
                TT(per_chunk(dm[:]), per_chunk(bt[:]), spread(pe_[b][:], CHUNK)).then_inc(done["bh"], 1)
                need("rt", t + 1)
                need("k2", t + 1)
                TT(e1[:], zT[:, R0:R0 + PAIRS, T], k2[:]).then_inc(done["rk"], 1)
                yield
                yield
                yield
                yield
                yield

            def main(t):
                b = t % 2
                T = tile(t)
                need("rt", t + 1)
                need("QT", t)
                TT(per_chunk(rq[:]), per_chunk(rt[:]), spread(pm[b][:], CHUNK)).then_inc(done["rq"], 1)
                yield
                for g in range(2):
                    need("LT", 2 * t + g + 1)
                    TT(XT[g][:], LT[g][:], across(level[0][:], PAIRS)).then_inc(done["xt1"], 1)
                    need("xt1", 2 * t + g + 1)
                    TT(XT[g][:], XT[g][:], across(ident[:], PAIRS), ALU.add).then_inc(done["XT1"], 1)
                need("ysq", t)
                if t:
                    wait_full(pool, "outT", t - 1)
                for g in range(2):
                    TT(LTk[g][:], LT[g][:], across(level[1][:], PAIRS)).then_inc(done["LTk"], 1)
                for g in range(2):
                    need("MrkR", 2 * t + g + 1)
                    TT(MrkT[g][:], MrkT[g][:], across(incl[:], PAIRS)).then_inc(done["MrkT"], 1)
                yield
                for k in range(1, LEVELS):
                    if k + 1 < LEVELS:
                        for g in range(2):
                            wait_full(pool, f"y{g}_{k}", t)
                            TT(LTk[g][:], LT[g][:], across(level[k + 1][:], PAIRS)).then_inc(done["LTk"], 1)
                    yield
                wait_full(pool, f"y0_{LEVELS - 1}", t)
                need("pc", t + 1)
                TT(diag, across(ident64[:], 2 * PAIRS), spread(pc[b][:], HEAD)).then_inc(done["diag"], 1)
                yield
                yield
                need("rs", t + 1)
                TT(rstd8[:], var8[:], neg_half[:], ALU.pow).then_inc(done["rstd"], 1)
                need("rstd", t + 1)
                TT(view(yc[:].rearrange("p a b -> p (a b)"), HEADS), view(yc[:].rearrange("p a b -> p (a b)"), HEADS),
                   spread(rstd8[:], HEAD)).then_inc(done["yn1"], 1)
                TT(view(y_s[:].rearrange("p a b -> p (a b)"), HEADS), V_tok[b][:], spread(bonus[b][:], HEAD))\
                    .then_inc(done["bv"], 1)
                need("yn1", t + 1)
                TT(yc[:], yc[:], view(lnw_s[:], PAIRS)).then_inc(done["yn2"], 1)
                need("yn2", t + 1)
                TT(yc[:], yc[:], view(lnb_s[:], PAIRS), ALU.add).then_inc(done["yn3"], 1)
                need("yn3", t + 1)
                need("bv", t + 1)
                TT(yc[:], yc[:], y_s[:], ALU.add).then_inc(done["yn4"], 1)
                need("yn4", t + 1)
                need("gate", t + 1)
                TT(yc[:], yc[:], gate[:]).then_inc(done["yn5"], 1)
                yield
                yield

            for _ in side(0):
                pass
            for t in range(TILES):
                interleave(main(t), side(t + 1) if t + 1 < TILES else iter(()))

            split_w(N_IN // 2, 0)
            split_w(N_IN // 2, 1)
            for k in range(KT):
                pool.wait_ge(m_hi_ok, k + 1)
                TT(m_lo[:, k, :], zT[:, k if k < PAIRS else R0 + k - PAIRS, :], m_hi[:, k, :].bitcast(F32), ALU.subtract)\
                    .then_inc(m_lo_ok, 1)
            for j in range(N_OUT):
                n = N_IN + j + 2
                split_w(n // 2, n % 2)
            for k in range(KT):
                pool.wait_ge(m_hi_ok, KT + k + 1)
                TT(m_lo[:, k, :], h3[k % 2][:], m_hi[:, k, :].bitcast(F32), ALU.subtract).then_inc(m_lo_ok, 1)

            def group(g, last=False):
                with pool.Fori(0, 4) as i:
                    for p in range(2):
                        split_w(U_UP // 2 + 8 * g + i + 1, p)
                        pool.wait_ge(m_hi_ok, 2 * KT + 8 * g + 2 * i + p + 1)
                        c = bass.ds(2 * i + p, 1)
                        TT(u_lo[:, c, :], u_f[p][:].unsqueeze(1), u_hi[:, c, :].bitcast(F32), ALU.subtract)\
                            .then_inc(m_lo_ok, 1)
                with pool.Fori(0, 3 if last else 4) as i:
                    for p in range(2):
                        split_w(U_UP // 2 + 8 * g + 4 + i + 1, p)

            with pool.Fori(0, GROUPS - 1) as g:
                group(g)
            group(GROUPS - 1, last=True)
            for i in range(TILES):
                root(rs5[:, i:i + 1], fin_rs, 2 * i + 2, fin_root)

        @block_.vector
        def _(dve):
            V = nc.vector

            def need(name, n):
                if n > 0:
                    dve.wait_ge(done[name], n)

            dve.wait_ge(consts_in, 16)
            def scale_x(i):
                dve.wait_ge(x_sq, i + 1)
                c = slice(i, i + 1)
                V.tensor_scalar(rs1[:, c], ss1[:, c], 1.0 / D, RMS_EPS, ALU.mult, ALU.add).then_inc(x_rs, 1)
                dve.wait_ge(x_root, i + 1)
                V.tensor_scalar(xs[i % 2][:], xs[i % 2][:], rs1[:, c], None, ALU.mult).then_inc(x_n, 1)

            def gain_h(i):
                for j in range(2):
                    n = 2 * i + j
                    dve.wait_ge(tr_full, n + 1)
                    if i:
                        dve.wait_ge(h_lo_ok, n - 1)
                    V.tensor_tensor(h_raw[j][:], view(ps[4 + n % 4][:], 4),
                                    spread(vecs[:, C_G1 + 4 * j:C_G1 + 4 * j + 4], P), ALU.mult)\
                        .then_inc(h_raw_ok, 1)

            for i in range(TILES):
                scale_x(i)
                if i:
                    gain_h(i - 1)
            gain_h(TILES - 1)

            def shift(m):
                for p in range(2):
                    n = 2 * m + p
                    zn = zT[:, bass.ds(n, 1), :]
                    before, now = z_tmp[p][:, 0:SEQ].unsqueeze(1), z_tmp[p][:, 1:].unsqueeze(1)
                    dve.wait_ge(act_read, 2 * n + 2)
                    V.tensor_tensor(zn, before, now, ALU.subtract).then_inc(z_diff, 1)
                    dve.wait_ge(z_diff, n - R0 + 1)
                    V.scalar_tensor_tensor(out=zn, in0=zn, scalar=vecs[:, bass.ds(n - R0 + C_MU, 1)], in1=now,
                                           op0=ALU.mult, op1=ALU.add).then_inc(z_ok, 1)

            dve.wait_ge(z_zero, 2)
            with dve.Fori(R0 // 2, N_IN // 2) as i:
                shift(i)

            def TT(o, a, b, op=ALU.mult):
                return V.tensor_tensor(o, a, b, op)

            def channels(c):
                return spread(vecs[:, c:c + PAIRS], P)

            dve.wait_ge(z_ok, N_SHIFT)
            dve.wait_ge(consts_in, 96)
            dve.wait_ge(done["zero"], 1)

            def side(t):
                b = t % 2
                T = tile(t)
                wait_full(dve, "lora_w", t)
                TT(xw[:], view(bank("lora_w")[:], PAIRS), channels(C_W0), ALU.add)\
                    .then_inc(done["xw0"], 1)
                wait_full(dve, "lora_a", t)
                need("bt", t)
                TT(aa[:], view(bank("lora_a")[:], PAIRS), channels(C_A0), ALU.add)\
                    .then_inc(done["aa0"], 1)
                yield
                wait_full(dve, "ss", t)
                V.tensor_scalar(k2[:], view(bank("ss")[:], PAIRS), L2_EPS ** 2, None, ALU.max).then_inc(done["ssm"], 1)
                need("xw2", t + 1)
                if t:
                    wait_full(dve, "tr_a", t - 1)
                V.tensor_tensor_scan(cs[:].rearrange("p a b -> p (a b)"), keep[:], xw[:].rearrange("p a b -> p (a b)"),
                                     0.0, ALU.mult, ALU.add).then_inc(done["cs"], 1)
                need("cs", t + 1)
                if t:
                    wait_full(dve, "tr_b", t - 1)
                TT(per_chunk(dm[:]), per_chunk(cs[:]),
                   per_chunk(cs[:])[:, :, CHUNK // 2 - 1:CHUNK // 2].to_broadcast([P, 2 * PAIRS, CHUNK]), ALU.subtract)\
                    .then_inc(done["dm"], 1)
                need("root", t + 1)
                V.reciprocal(k2[:], k2[:]).then_inc(done["rn"], 1)
                need("rn", t + 1)
                TT(kk[:], kk[:], k2[:]).then_inc(done["kk"], 1)
                need("t2", t + 1)
                V.scalar_tensor_tensor(out=k2[:], in0=k2[:], scalar=1.0, in1=zT[:, RK0:RK0 + PAIRS, T],
                                       op0=ALU.add, op1=ALU.mult).then_inc(done["k2"], 1)
                yield
                need("kk", t + 1)
                need("dpe", t + 1)
                if t:
                    wait_full(dve, "mrk1", t - 1)
                V.scalar_tensor_tensor(out=at[:], in0=kk[:], scalar=-1.0, in1=xw[:],
                                       op0=ALU.mult, op1=ALU.mult).then_inc(done["at"], 1)
                need("k2", t + 1)
                need("e2", t + 1)
                TT(kt[:], k2[:], e2[:]).then_inc(done["kt"], 1)
                need("at", t + 1)
                need("pm", t + 1)
                TT(per_chunk(cs[:]), per_chunk(at[:]), spread(pm[b][:], CHUNK)).then_inc(done["ah"], 1)
                need("kt", t + 1)
                need("pe", t + 1)
                need("bt", t + 1)
                TT(per_chunk(e2[:]), per_chunk(kt[:]), spread(pe_[b][:], CHUNK)).then_inc(done["kh"], 1)
                yield
                lo = P if t == 0 else 0
                if t:
                    wait_full(dve, "oT", t - 1)
                need("rden", t)
                for g, name in enumerate(("sc00", "sc10", "sc01", "sc11")):
                    wait_full(dve, name, t)
                    for i in range(2):
                        head = 2 * (g // 2) + i + PAIRS * (g % 2)
                        slope = 2.0 ** -(head + 1)
                        V.scalar_tensor_tensor(out=sc[g][:, i, lo:], in0=dist[:, lo:], scalar=-slope / SCALE,
                                               in1=bank(name)[:, 2 * P * i + lo:2 * P * (i + 1)],
                                               op0=ALU.mult, op1=ALU.add).then_inc(done["sc"], 1)
                    need("sc", 8 * t + 2 * g + 2)
                    V.tensor_reduce(mx[:, slot(g, 0):slot(g, 1) + 1:2], sc[g][:, :, lo:], AX.X, ALU.max).then_inc(done["mx"], 1)
                need("mx", 4 * t + 4)
                V.scalar_tensor_tensor(out=mx[:], in0=mx[:], scalar=SCALE, in1=sink_s[:], op0=ALU.mult, op1=ALU.max)\
                    .then_inc(done["m"], 1)
                need("m", t + 1)
                TT(es[:], sink_s[:], mx[:], ALU.subtract).then_inc(done["dsink"], 1)
                need("p", 8 * t)
                V.tensor_scalar(nm[:], mx[:], -1.0, None, ALU.mult).then_inc(done["nm"], 1)
                yield
                need("es", t + 1)
                need("p", 8 * t + 8)
                TT(den[:], es[:], sums[:], ALU.add).then_inc(done["den"], 1)
                need("den", t + 1)
                V.reciprocal(den[:], den[:]).then_inc(done["rden"], 1)
                yield
                yield
                wait_full(dve, "o", t)
                need("rden", t + 1)
                TT(view(sc[0][:].rearrange("p a b -> p (a b)"), HEADS), view(bank("o")[:], HEADS), spread(den[:], HEAD))\
                    .then_inc(done["o"], 1)
                yield

            def main(t):
                b = t % 2
                need("yn5", t)
                need("rstd", t)
                for name, dst, mask, key in (("lab", LT, strict, "LT"), ("lak", LakT, strict, "LakT"),
                                             ("mrb", MrbT, incl, "MrbT")):
                    for g in range(2):
                        n = f"{name}{g}"
                        wait_full(dve, n, t)
                        TT(dst[g][:], view(bank(n)[:], PAIRS), across(mask[:], PAIRS))\
                            .then_inc(done[key], 1)
                yield
                yield
                for k in range(1, LEVELS):
                    for g in range(2):
                        n = f"y{g}_{k}"
                        wait_full(dve, n, t)
                        TT(IY[g][:], view(bank(n)[:], PAIRS), across(ident[:], PAIRS), ALU.add)\
                            .then_inc(done["IY"], 1)
                    yield
                wait_full(dve, "g", t)
                V.tensor_copy(G_s[:], view(bank("g")[:], HEADS)).then_inc(done["G"], 1)
                yield
                wait_full(dve, "rq", t)
                need("rq", t + 1)
                TT(QT[:], view(bank("rq")[:], PAIRS), rq[:], ALU.add).then_inc(done["QT"], 1)
                need("diag", t + 1)
                dg = diag.rearrange("p (a c) d -> p a c d", c=CHUNKS)
                for c in range(CHUNKS):
                    need("psi", 4 * t + 2 * c + 2)
                    for g in range(2):
                        TT(halves(phi[c], g)[:, :, HEAD * g:HEAD * (g + 1)],
                           halves(view(bank(f"c{c}")[:], PAIRS), g)[:, :, 0:HEAD], halves(dg, g)[:, :, c, :],
                           ALU.add).then_inc(done["phi"], 1)
                yield
                for c in range(CHUNKS):
                    wait_full(dve, f"st{c}", t)
                    need("psi", 4 * t + 2 * c + 2)
                    TT(state[1 - c][:], view(bank(f"st{c}")[:], PAIRS), psi[c][:], ALU.add)\
                        .then_inc(done["state"], 1)
                need("y", t + 1)
                yh = view(y_s[:].rearrange("p a b -> p (a b)"), HEADS)
                V.tensor_reduce(mu8[:], yh, AX.X, ALU.add).then_inc(done["mu"], 1)
                need("mu", t + 1)
                V.scalar_tensor_tensor(out=view(yc[:].rearrange("p a b -> p (a b)"), HEADS), in0=spread(mu8[:], HEAD),
                                       scalar=-1.0 / HEAD, in1=yh, op0=ALU.mult, op1=ALU.add).then_inc(done["yc"], 1)
                need("ysq", t + 1)
                V.tensor_reduce(var8[:], view(y_sq[:].rearrange("p a b -> p (a b)"), HEADS), AX.X, ALU.add)\
                    .then_inc(done["var"], 1)
                need("var", t + 1)
                V.tensor_scalar(var8[:], var8[:], 1.0 / HEAD, GN_EPS, ALU.mult, ALU.add).then_inc(done["rs"], 1)
                yield
                yield

            for _ in side(0):
                pass
            for t in range(TILES):
                interleave(main(t), side(t + 1) if t + 1 < TILES else iter(()))

            for f in range(2 * TILES):
                i, j = divmod(f, 2)
                dve.wait_ge(tr_full, 2 * TILES + f + 1)
                V.tensor_copy(x2[:, 4 * j:4 * j + 4, tile(i)], view(ps[4 + f % 4][:], 4)).then_inc(x2_in, 1)
            dve.wait_ge(x2_in, 2 * TILES)

            for j in range(N_OUT):
                for h in range(2):
                    n = N_IN + j
                    dve.wait_ge(proj_full, 2 * n + h + 1)
                    o = x2[:, j, h * HALF:(h + 1) * HALF]
                    V.tensor_tensor(o, o, ps[2 * (n % 2) + h][:], ALU.add).then_inc(dve_read, 1)
                dve.wait_ge(x2_sq, j + 1)
                if j:
                    dve.wait_ge(x2_acc, j)
                    V.tensor_tensor(acc3[:], acc3[:], sq3[j % 2][:], ALU.add).then_inc(x2_acc, 1)
                else:
                    V.tensor_copy(acc3[:], sq3[0][:]).then_inc(x2_acc, 1)
            for h in range(2):
                c = slice(h * HALF, (h + 1) * HALF)
                dve.wait_ge(ss3_full, h + 1)
                V.tensor_scalar(rs3[:, c], ps[4 + h][:], 1.0 / D, RMS_EPS, ALU.mult, ALU.add).then_inc(rs3_ok, 1)
            dve.wait_ge(rs3_ok, 3)
            V.reciprocal(rs3[:], rs3[:]).then_inc(rs3_ok, 1)
            dve.wait_ge(rs3_ok, 4)
            for k in range(KT):
                if k >= 2:
                    dve.wait_ge(m_lo_ok, KT + k - 1)
                V.scalar_tensor_tensor(out=h3[k % 2][:], in0=x2[:, k, :], scalar=vecs[:, C_G2 + k:C_G2 + k + 1],
                                       in1=rs3[:], op0=ALU.mult, op1=ALU.mult).then_inc(h3_raw, 1)

            with dve.Fori(0, GROUPS) as g:
                with dve.Fori(0, 4) as i:
                    for p in range(2):
                        e = 8 * g + 2 * i + p
                        dve.wait_ge(act_read, 2 * (N_IN + e) + 2)
                        dve.wait_ge(m_lo_ok, 2 * KT + e - 1)
                        V.tensor_tensor(u_f[p][:], u_r[p][:], u_r[p][:], ALU.mult).then_inc(u_sq, 1)
                with dve.Fori(0, 4) as i:
                    for p in range(2):
                        n = U_UP + 16 * g + 8 + 2 * i + p
                        for h in range(2):
                            dve.wait_ge(proj_full, 2 * n + h + 1)
                            o = x2[:, bass.ds(2 * i + p, 1), h * HALF:(h + 1) * HALF]
                            V.tensor_tensor(o, o, ps[2 * p + h][:].unsqueeze(1), ALU.add)\
                                .then_inc(dve_read, 1)

            dve.wait_ge(fin_in, 16)
            for i in range(TILES):
                c = slice(i, i + 1)
                dve.wait_ge(fin_sq, 2 * i + 2)
                V.tensor_tensor(rs5[:, c], ss5[:, 2 * i:2 * i + 1], ss5[:, 2 * i + 1:2 * i + 2], ALU.add).then_inc(fin_rs, 1)
                dve.wait_ge(fin_rs, 2 * i + 1)
                V.tensor_scalar(rs5[:, c], rs5[:, c], 1.0 / D, RMS_EPS, ALU.mult, ALU.add).then_inc(fin_rs, 1)
                dve.wait_ge(fin_root, i + 1)
                for j in range(2):
                    f = 4 * TILES + 2 * i + j
                    V.scalar_tensor_tensor(out=o_s[i][:, j * HALF:(j + 1) * HALF], in0=ps[4 + f % 4][:],
                                           scalar=rs5[:, c], in1=fg_s[:, j * HALF:(j + 1) * HALF],
                                           op0=ALU.mult, op1=ALU.mult).then_inc(fin_y, 1)

        @block_.tensor
        def _(pe):
            M = nc.tensor.matmul

            def need(name, n):
                if n > 0:
                    pe.wait_ge(done[name], n)

            def turn(read, source, i):
                for j in range(2):
                    f = 2 * i + j
                    if f >= 4:
                        pe.wait_ge(read, f - 3)
                    for k in range(4):
                        o = nc.tensor.transpose(ps[4 + f % 4][:, k * P:(k + 1) * P], source(4 * j + k), ident[:])
                    o.then_inc(tr_full, 1)

            def unit(m, p, hi, lo):
                n = 2 * m + p
                pe.wait_ge(w_hi_ok, n + 1)
                pe.wait_ge(w_lo_ok, n + 1)
                for k in range(KT):
                    for s, (w, a) in enumerate(((w_hi, hi), (w_hi, lo), (w_lo, hi))):
                        for h in range(2):
                            o = M(ps[2 * p + h][:], w[p][:, k, :], a[:, k, h * HALF:(h + 1) * HALF],
                                  start=k == 0 and s == 0, stop=k == KT - 1 and s == 2)
                            if k == KT - 1 and s == 2:
                                o.then_inc(proj_full, 1)

            pe.wait_ge(mask_step, 3)
            for i in range(TILES):
                pe.wait_ge(x_n, i + 1)
                turn(h_raw_ok, lambda k: xs[i % 2][:, k * P:(k + 1) * P], i)
            pe.wait_ge(h_hi_ok, 2 * TILES)
            pe.wait_ge(h_lo_ok, 2 * TILES)
            unit(0, 0, h_hi, h_lo)
            unit(0, 1, h_hi, h_lo)
            with pe.Fori(1, N_IN // 2) as i:
                for p in range(2):
                    pe.wait_ge(act_read, 4 * i + 2 * p - 2)
                    unit(i, p, h_hi, h_lo)

            pe.wait_ge(h_raw_ok, 2 * TILES)
            pe.wait_ge(act_read, 2 * N_IN)
            pe.wait_ge(z_ok, N_SHIFT)
            pe.wait_ge(consts_in, 96)
            pe.wait_ge(done["zero"], 1)

            def side(t):
                b = t % 2
                T = tile(t)
                need("tw", t + 1)
                wait_bank(pe, "lora_w", t)
                for a in range(PAIRS):
                    c = slice(a * P, (a + 1) * P)
                    o = M(bank("lora_w")[:, c], w2a2_s[0:64, c], tw[0:64, :], start=True, stop=True)
                o.then_inc(filled("lora_w"), 1)
                wait_bank(pe, "lora_a", t)
                for a in range(PAIRS):
                    c = slice(a * P, (a + 1) * P)
                    o = M(bank("lora_a")[:, c], w2a2_s[64:P, c], zT[64:P, RWA, T], start=True, stop=True)
                o.then_inc(filled("lora_a"), 1)
                need("ksq", t + 1)
                wait_bank(pe, "ss", t)
                M(bank("ss")[:], pair_ones[:], k2[:].rearrange("p a b -> p (a b)"), start=True, stop=True)\
                    .then_inc(filled("ss"), 1)
                yield
                yield
                for name, key, src in (("tr_a", "ah", cs), ("tr_b", "bh", dm), ("tr_k", "kh", e2), ("tr_v", None, None)):
                    if key:
                        need(key, t + 1)
                    wait_bank(pe, name, t)
                    for a in range(PAIRS):
                        o = nc.tensor.transpose(bank(name)[:, a * P:(a + 1) * P],
                                                src[:, a, :] if key else zT[:, RV0 + a, T], ident[:])
                    o.then_inc(filled(name), 1)
                need("rk", t + 1)
                wait_bank(pe, "bonus", t)
                for a in range(PAIRS):
                    o = M(bank("bonus")[:, 2 * a:2 * a + 2], e1[:, a, :], rk_w[:, a, :], start=True, stop=True)
                o.then_inc(filled("bonus"), 1)
                wait_bank(pe, "vt", t)
                nc.tensor.transpose(bank("vt")[:, 0:P], zT[:, V0, T], ident[:]).then_inc(filled("vt"), 1)
                yield
                lo = P if t == 0 else 0
                for g, name in enumerate(("sc00", "sc10", "sc01", "sc11")):
                    wait_bank(pe, name, t)
                    par = g % 2
                    for i in range(2):
                        o = M(bank(name)[:, 2 * P * i + lo:2 * P * (i + 1)], halves(zT, par)[:, Q0 + 2 * (g // 2) + i, T],
                              halves(zT, par)[:, K0, t * P - P + lo:t * P + P], start=True, stop=True)
                    o.then_inc(filled(name), 1)
                yield
                yield
                for g, name in enumerate(("pt00", "pt10", "pt01", "pt11")):
                    need("p", 8 * t + 2 * g + 2)
                    wait_bank(pe, name, t)
                    for i in range(2):
                        for k in range(1 if t == 0 else 0, 2):
                            q = 2 * i + k
                            o = nc.tensor.transpose(bank(name)[:, q * P:(q + 1) * P], sc[g][:, i, k * P:(k + 1) * P], ident[:])
                    o.then_inc(filled(name), 1)
                wait_bank(pe, "o", t)
                for g in range(4):
                    need("pT", 4 * t + g + 1)
                    for i in range(2):
                        c = slot(g, i)
                        kv = g % 2
                        for k in range(1 if t == 0 else 0, 2):
                            o = M(bank("o")[:, c * HEAD:(c + 1) * HEAD], sc[g][:, i, k * P:(k + 1) * P],
                                  va_tok[(t - 1 + k) % 2][:, kv * HEAD:(kv + 1) * HEAD],
                                  start=k == 0 or t == 0, stop=k == 1)
                o.then_inc(filled("o"), 1)
                yield
                need("o", t + 1)
                wait_bank(pe, "oT", t)
                o_tok = view(sc[0][:].rearrange("p a b -> p (a b)"), PAIRS)
                for a in range(PAIRS):
                    o = nc.tensor.transpose(bank("oT")[:, a * P:(a + 1) * P], o_tok[:, a, :], ident[:])
                o.then_inc(filled("oT"), 1)
                yield

            def main(t):
                b = t % 2

                def four(name, f, last=True):
                    wait_bank(pe, name, t)
                    for a in range(PAIRS):
                        o = f(a)
                    o.then_inc(filled(name), 1)

                def scores(name, g, keys, queries):
                    bk = bank(f"{name}{g}")
                    four(f"{name}{g}", lambda a: M(bk[:, a * P:(a + 1) * P], halves(keys, g)[:, a, :],
                                                   halves(queries, g)[:, a, :], start=True, stop=True))

                need("at", t + 1)
                need("bt", t + 1)
                for g in range(2):
                    scores("lab", g, bt, at)
                need("kt", t + 1)
                for g in range(2):
                    scores("lak", g, kt, at)
                need("rt", t + 1)
                for g in range(2):
                    scores("mrb", g, bt, rt)
                yield
                for g in range(2):
                    scores("mrk", g, kt, rt)
                for g in range(2):
                    need("XT1", 2 * t + g + 1)
                    four(f"xt{g}", lambda a: nc.tensor.transpose(bank(f"xt{g}")[:, a * P:(a + 1) * P], XT[g][:, a, :], ident[:]))
                wait_bank(pe, "lv", t)
                need("LakT", 2 * t + 2)
                for c in range(HEADS):
                    a, g = divmod(c, 2)
                    o = M(bank("lv")[:, c * HEAD:(c + 1) * HEAD], LakT[g][:, a, :], V_tok[b][:, c, :], start=True, stop=True)
                o.then_inc(filled("lv"), 1)
                yield
                for k in range(1, LEVELS):
                    turns = LEVELS - 1
                    for g in range(2):
                        need("LTk", 2 * turns * t + 2 * (k - 1) + g + 1)
                        need("X", 2 * turns * t + 2 * (k - 1) + g + 1)
                        n = f"y{g}_{k}"
                        four(n, lambda a: M(bank(n)[:, a * P:(a + 1) * P], LTk[g][:, a, :], X[g][:, a, :], start=True, stop=True))
                    for g in range(2):
                        need("IY", 2 * turns * t + 2 * (k - 1) + g + 1)
                        if k > 1:
                            need("XT", 2 * turns * t + 2 * (k - 2) + g + 1)
                        n = f"z{g}_{k}"
                        if n in USE:
                            four(n, lambda a: M(bank(n)[:, a * P:(a + 1) * P], XT[g][:, a, :], IY[g][:, a, :], start=True, stop=True))
                        nt = f"zt{g}_{k}"
                        four(nt, lambda a: M(bank(nt)[:, a * P:(a + 1) * P], IY[g][:, a, :], XT[g][:, a, :], start=True, stop=True))
                    yield
                need("XT", 2 * turns * t + 2 * turns)
                need("LV", t + 1)
                for name, rhs in (("w", A_tok[b][:]), ("g", LV)):
                    wait_bank(pe, name, t)
                    for c in range(HEADS):
                        a, g = divmod(c, 2)
                        o = M(bank(name)[:, c * HEAD:(c + 1) * HEAD], XT[g][:, a, :], rhs[:, c, :], start=True, stop=True)
                    o.then_inc(filled(name), 1)
                yield
                need("W", t + 1)
                need("MrbT", 2 * t + 2)
                wait_bank(pe, "rq", t)
                for c in range(HEADS):
                    a, g = divmod(c, 2)
                    o = M(halves(bank("rq"), g)[:, a * P:(a + 1) * P], W_s[:, c, :], MrbT[g][:, a, :], start=True, stop=True)
                o.then_inc(filled("rq"), 1)
                need("G", t + 1)
                for c in range(CHUNKS):
                    wait_bank(pe, f"c{c}", t)
                    for h in range(HEADS):
                        a, g = divmod(h, 2)
                        to = halves(bank(f"c{c}"), g)[:, a * P:(a + 1) * P]
                        row = slice(c * CHUNK, (c + 1) * CHUNK)
                        M(to[:, 0:HEAD], W_s[row, h, :], B_tok[b][row, h, :], start=True, stop=True)
                        M(to[:, HEAD:], B_tok[b][row, h, :], G_s[row, h, :], start=True, stop=False)
                        o = M(to[:, HEAD:], K_tok[b][row, h, :], V_tok[b][row, h, :], start=False, stop=True)
                    o.then_inc(filled(f"c{c}"), 1)
                yield
                def advance(c):
                    need("phi", 4 * t + 2 * c + 2)
                    need("state", 2 * t + c)
                    four(f"st{c}", lambda a: M(bank(f"st{c}")[:, a * P:(a + 1) * P], phi[c][:, a, :], state[c][:, a, :],
                                               start=True, stop=True))

                advance(0)
                need("gg", t + 1)
                wait_bank(pe, "gate", t)
                M(bank("gate")[:], gs[b][:], g2_s[:], start=True, stop=True).then_inc(filled("gate"), 1)
                need("QT", t + 1)
                need("MrkT", 2 * t + 2)
                need("state", 2 * t + 1)
                wait_bank(pe, "yy", t)
                for a in range(PAIRS):
                    for c in range(CHUNKS):
                        row = slice(c * CHUNK, (c + 1) * CHUNK)
                        M(bank("yy")[row, a * P:(a + 1) * P], QT[:, a, row], state[c][:, a, :], start=True, stop=False,
                          skip_group_check=True)
                    for g in range(2):
                        h = 2 * a + g
                        to = bank("yy")[:, h * HEAD:(h + 1) * HEAD]
                        M(to, MrbT[g][:, a, :], G_s[:, h, :], start=False, stop=False, skip_group_check=True)
                        o = M(to, MrkT[g][:, a, :], V_tok[b][:, h, :], start=False, stop=g == 1, skip_group_check=True)
                o.then_inc(filled("yy"), 1)
                advance(1)
                yield
                need("yn5", t + 1)
                four("outT", lambda a: nc.tensor.transpose(bank("outT")[:, a * P:(a + 1) * P], yc[:, a, :], ident[:]))
                yield

            for _ in side(0):
                pass
            for t in range(TILES):
                interleave(main(t), side(t + 1) if t + 1 < TILES else iter(()))

            for uses in BANK_USES.values():
                wait_read(pe, uses[-1], TILES - 1)
            for i in range(TILES):
                pe.wait_ge(x_in[i % 2], 16 * (TILES // 2 + i // 2 + 1))
                turn(x2_in, lambda k: xs3[i % 2][:, k * P:(k + 1) * P], i)
            pe.wait_ge(m_hi_ok, KT)
            pe.wait_ge(m_lo_ok, KT)
            unit(N_IN // 2, 0, m_hi, m_lo)
            unit(N_IN // 2, 1, m_hi, m_lo)
            with pe.Fori(1, N_OUT // 2) as i:
                for p in range(2):
                    pe.wait_ge(dve_read, 4 * i + 2 * p - 2)
                    unit(N_IN // 2 + i, p, m_hi, m_lo)
            pe.wait_ge(x2_acc, N_OUT)
            pe.wait_ge(x2_in, 2 * TILES)
            for h in range(2):
                M(ps[4 + h][:], ones[:], acc3[:, h * HALF:(h + 1) * HALF], start=True, stop=True).then_inc(ss3_full, 1)
            pe.wait_ge(m_hi_ok, 2 * KT)
            pe.wait_ge(m_lo_ok, 2 * KT)
            with pe.Fori(0, GROUPS) as g:
                with pe.Fori(0, 4) as i:
                    for p in range(2):
                        pe.wait_ge(dve_read, 2 * (N_OUT + 8 * g) - 2 * (1 - p))
                        pe.wait_ge(act_read, 2 * (N_IN + 8 * g + 2 * i + p - 1))
                        unit(U_UP // 2 + 8 * g + i, p, m_hi, m_lo)
                with pe.Fori(0, 4) as i:
                    for p in range(2):
                        pe.wait_ge(m_hi_ok, 2 * KT + 8 * g + 8)
                        pe.wait_ge(m_lo_ok, 2 * KT + 8 * g + 8)
                        pe.wait_ge(act_read, 2 * (N_IN + 8 * g + 8) - 2 * (1 - p))
                        pe.wait_ge(dve_read, 2 * (N_OUT + 8 * g + 2 * i + p - 1))
                        unit(U_UP // 2 + 8 * g + 4 + i, p, u_hi, u_lo)
            pe.wait_ge(dve_read, 2 * N_OUT * (1 + GROUPS))
            for i in range(TILES):
                turn(fin_y, lambda k: x2[:, k, tile(i)], i)


def kernel(x, attn_norm_g, w_in, attn_sinks, rwkv_mu, w0, w2, a0, a2, g2, k_k, k_a, r_k,
           ln_x_w, ln_x_b, w_out, mlp_norm_g, w_up, w_down, final_norm_g):
    import numpy as np
    import concourse.bacc as bacc
    from concourse.bass_utils import run_bass_kernel_spmd as run

    def arr(a):
        return np.ascontiguousarray(a)

    def blocks(v):
        return np.asarray(v).reshape(-1, P).T

    def units(w):
        n = w.shape[1] // P
        return w.reshape(KT, P, n, P).transpose(2, 1, 0, 3).reshape(n, P, KT * P)

    wi = np.asarray(w_in)[0]
    q = wi[:, :512].reshape(D, 2, 4, HEAD).transpose(0, 2, 1, 3).reshape(D, 512)
    wo = np.asarray(w_out)[0]
    o = wo[:512].reshape(2, 4, HEAD, D).transpose(1, 0, 2, 3).reshape(512, D)
    wu, wd = np.asarray(w_up)[0], np.asarray(w_down)[0]
    parts = [units(np.concatenate([q, wi[:, 512:]], 1)), units(np.concatenate([o, wo[512:]], 0))]
    for g in range(GROUPS):
        parts += [units(wu[:, g * 1024:(g + 1) * 1024]), units(wd[g * 1024:(g + 1) * 1024])]
    vec = np.concatenate([blocks(v) for v in (rwkv_mu, w0, a0, k_k, k_a, r_k, attn_norm_g, mlp_norm_g)], 1)
    ins = {
        "x": arr(x),
        "w_all": arr(np.concatenate(parts, 0)),
        "vec": arr(vec),
        "sinks": arr(np.asarray(attn_sinks).reshape(2, 4).T.reshape(1, HEADS)),
        "w2a2": arr(np.concatenate([np.asarray(w2)[0], np.asarray(a2)[0]], 0)),
        "g2": arr(np.asarray(g2)[0]),
        "ln_w": arr(ln_x_w), "ln_b": arr(ln_x_b),
        "fin_g": arr(np.asarray(final_norm_g).reshape(1, D)),
    }
    nc = bacc.Bacc("TRN2", target_bir_lowering=False, num_devices=1)
    aps = [nc.dram_tensor(f"in_{n}", a.shape, F32, kind="ExternalInput").ap() for n, a in ins.items()]
    out = nc.dram_tensor("out_0", x.shape, F32, kind="ExternalOutput").ap()
    build(nc, *aps, out)
    r = run(nc, [{f"in_{n}": a for n, a in ins.items()}], core_ids=[0])
    return r.results[0]["out_0"]
```

```python
from contextlib import ExitStack
import math

import concourse.bass as bass
from concourse import mybir

F32 = mybir.dt.float32
F32R = mybir.dt.float32r
ALU = mybir.AluOpType
ACT = mybir.ActivationFunctionType
AX = mybir.AxisListType

P = 128
SEQ = 1024
D = 1024
KT = D // P
HEAD = 64
HEADS = 8
KV = 2
PAIRS = HEADS // 2
CHUNK = 64
TILES = SEQ // P
CHUNKS = P // CHUNK
HALF = 512
D_FF = 4 * D
Q0, K0, V0, R0 = 0, 4, 5, 6
RK0, RV0, RWA, RG = 10, 14, 18, 19
N_IN = 20
N_SHIFT = N_IN - R0
N_OUT = 8
GROUPS = 4
UNITS = N_IN + N_OUT + GROUPS * 16
RMS_EPS = 1e-6
GN_EPS = 64e-5
L2_EPS = 1e-12
LOG_DECAY = math.exp(-0.5)
SCALE = HEAD ** -0.5
FAR = 1.0e32
LEVELS = CHUNK.bit_length() - 1

C_MU, C_W0, C_A0, C_KK, C_KA, C_RK = 0, 14, 18, 22, 26, 30
C_G1, C_G2, N_VEC = 34, 42, 50

SCHEDULE = [
    ("tanh", 1), ("lab", 0), ("li", 0), ("lora", 1), ("lak", 0), ("yy", -1), ("st1", -1), ("mu", -1),
    ("mrb", 0), ("sig", 1), ("ssq", 1), ("mrk", 0), ("bv", -1), ("xt", 0), ("pt", 0), ("lv", 0),
    ("y1", 0), ("o", 0), ("var", -1), ("cum", 1), ("z1", 0),
    ("y2", 0), ("rnT", 1), ("oT", 0), ("mid", 1), ("mrk_m", 0), ("yn", -1), ("z2", 0),
    ("y3", 0), ("rx", 1), ("gate", -1), ("exps", 1), ("gs", 1), ("z3", 0),
    ("y4", 0), ("outT", -1), ("dpe", 1), ("sc_a", 1), ("abk", 1), ("z4", 0),
    ("y5", 0), ("sc_b", 1), ("hats", 1), ("z5", 0),
    ("wg", 0), ("tr_ab", 1), ("rq", 0), ("c", 0), ("tr_kv", 1), ("st0", 0), ("p", 1), ("den", 1),
]
ORDER = [(step, i + lag) for i in range(-1, TILES + 1) for step, lag in SCHEDULE if 0 <= i + lag < TILES]

MAKES = {
    "lora": [("lora_w", 6), ("lora_a", 7)], "ssq": [("ss", 6)], "rnT": [("rnT", 6)], "rx": [("rx", 6)],
    "tr_ab": [("tr_a", 6), ("tr_b", 7)], "tr_kv": [("tr_k", 6), ("tr_v", 7), ("bonus", 6), ("vt", 7)],
    "sc_a": [("sc00", 6), ("sc10", 7)], "sc_b": [("sc01", 6), ("sc11", 7)],
    "pt": [("pt00", 6), ("pt10", 7), ("pt01", 6), ("pt11", 7)], "o": [("o", 6)], "oT": [("oT", 7)],
    "lab": [("lab0", 0), ("lab1", 1)], "lak": [("lak0", 4), ("lak1", 5)],
    "mrb": [("mrb0", 0), ("mrb1", 1)], "mrk": [("mrk0", 4), ("mrk1", 5)],
    "xt": [("xt0", 0), ("xt1", 1)], "lv": [("lv", 4)],
    "wg": [("w", 2), ("g", 3)], "rq": [("rq", 0)], "c": [("c0", 4), ("c1", 5)],
    "st0": [("st0", 2)], "st1": [("st1", 2)], "yy": [("yy", 3)], "gate": [("gate", 7)], "outT": [("outT", 7)],
}
for _k in range(1, LEVELS):
    MAKES[f"y{_k}"] = [(f"y{_g}_{_k}", _g) for _g in range(2)]
    MAKES[f"z{_k}"] = [(f"zt{_g}_{_k}", 4 + _g) for _g in range(2)]
    if _k < LEVELS - 1:
        MAKES[f"z{_k}"] = [(f"z{_g}_{_k}", 2 + _g) for _g in range(2)] + MAKES[f"z{_k}"]
BANK = {name: b for makes in MAKES.values() for name, b in makes}
BANK_USES = {b: [(name, t) for step, t in ORDER for name, to in MAKES.get(step, ()) if to == b] for b in range(8)}
USE = {use: i for uses in BANK_USES.values() for i, use in enumerate(uses)}

READER = {
    "lora_w": ("xw0", 1, 1), "lora_a": ("aa0", 1, 1), "ss": ("ssm", 1, 1), "rnT": ("rnT", 1, 1), "rx": ("kk", 1, 1),
    "bonus": ("bonus", 1, 1),
    "tr_a": ("A_tok", 1, 1), "tr_b": ("B_tok", 1, 1), "tr_k": ("K_tok", 1, 1), "tr_v": ("V_tok", 1, 1),
    "vt": ("va_tok", 1, 1), "o": ("o", 1, 1), "oT": ("oT", 1, 1), "lv": ("LV", 1, 1), "w": ("W", 1, 1),
    "g": ("G", 1, 1), "rq": ("QT", 1, 1), "yy": ("yc", 1, 1), "gate": ("yn5", 1, 1), "outT": ("rw", 1, 1),
}
for _i, _n in enumerate(("00", "10", "01", "11")):
    READER["sc" + _n] = ("sc", 8, 2 * _i + 2)
    READER["pt" + _n] = ("pT", 4, _i + 1)
for _g in range(2):
    READER[f"lab{_g}"] = ("LT", 2, _g + 1)
    READER[f"lak{_g}"] = ("LakT", 2, _g + 1)
    READER[f"mrb{_g}"] = ("MrbT", 2, _g + 1)
    READER[f"mrk{_g}"] = ("MrkR", 2, _g + 1)
    READER[f"xt{_g}"] = ("X", 2 * (LEVELS - 1), _g + 1)
    READER[f"c{_g}"] = ("phi", 4, 2 * _g + 2)
    READER[f"st{_g}"] = ("state", 2, _g + 1)
    for _k in range(1, LEVELS):
        READER[f"y{_g}_{_k}"] = ("IY", 2 * (LEVELS - 1), 2 * (_k - 1) + _g + 1)
        READER[f"z{_g}_{_k}"] = ("X", 2 * (LEVELS - 1), 2 * _k + _g + 1)
        READER[f"zt{_g}_{_k}"] = ("XT", 2 * (LEVELS - 1), 2 * (_k - 1) + _g + 1)


def build(nc, x, w_all, vec, sinks, w2a2, g2, ln_w, ln_b, fin_g, out):
    with ExitStack() as ctx:
        def sb(name, shape, dt=F32):
            return ctx.enter_context(nc.sbuf_tensor(name, shape, dt))

        vecs = sb("vecs", [P, N_VEC])
        ident = sb("ident", [P, P])
        ones = sb("ones", [P, P])
        w_raw = [sb(f"w_raw{i}", [P, KT, P]) for i in range(2)]
        neg_half = sb("neg_half", [P, 8])
        BASE = -(-nc.sbuf_base // 64) * 64
        TOP = nc.sbuf_usable_end // 64 * 64
        KB4 = 4 * SEQ

        class Region:

            def __init__(self, base, end=TOP):
                self.at, self.end = base, end

            def __call__(self, name, shape, dt=F32):
                t = nc.alloc_sbuf_tensor_at(name, shape, dt, offset=self.at)
                self.at += -(-4 * math.prod(shape[1:]) // 32) * 32
                assert self.at <= self.end, (name, self.at, self.end)
                return t

        r = Region(TOP - 4 * KB4)
        w_hi = [r(f"w_hi{i}", [P, KT, P], F32R) for i in range(2)]
        w_lo = [r(f"w_lo{i}", [P, KT, P], F32R) for i in range(2)]
        W_AT = TOP - 4 * KB4

        r = Region(BASE)
        zT = r("zT", [P, N_IN, SEQ])
        w2a2_s = r("w2a2_s", [P, 512])
        g2_s = r("g2_s", [P, 512])
        lnw_s = r("lnw_s", [P, 512])
        lnb_s = r("lnb_s", [P, 512])
        strict = r("strict", [P, P])
        incl = r("incl", [P, P])
        level = [r(f"level{k}", [P, P]) for k in range(LEVELS)]
        dist = r("dist", [P, 2 * P])
        pair_sel = r("pair_sel", [P, 2])
        head_up = r("head_up", [P, 512])
        ident64 = r("ident64", [P, HEAD])
        rk_w = r("rk_w", [P, PAIRS, 2])
        keep = r("keep", [P, 512])
        sink_s = r("sink_s", [P, HEADS])
        CONST_END = r.at

        r = Region(CONST_END, W_AT)
        h_hi = r("h_hi", [P, KT, SEQ], F32R)
        h_lo = r("h_lo", [P, KT, SEQ], F32R)
        xs = [r(f"xs{i}", [P, D]) for i in range(2)]
        h_raw = [r(f"h_raw{i}", [P, 4, P]) for i in range(2)]
        z_tmp = [r(f"z_tmp{i}", [P, 1 + SEQ]) for i in range(2)]
        ss1 = r("ss1", [P, TILES])
        rs1 = r("rs1", [P, TILES])

        r = Region(CONST_END)
        block = [P, PAIRS, P]
        toks = [P, HEADS, HEAD]
        at = r("at", block)
        rt = r("rt", block)
        bt = r("bt", block)
        kt = r("kt", block)
        rq = r("rq", block)
        A_tok = [r(f"A_tok{i}", toks) for i in range(2)]
        B_tok = [r(f"B_tok{i}", toks) for i in range(2)]
        K_tok = [r(f"K_tok{i}", toks) for i in range(2)]
        V_tok = [r(f"V_tok{i}", toks) for i in range(2)]
        va_tok = [r(f"va_tok{i}", [P, P]) for i in range(2)]
        xw = r("xw", block)
        aa = r("aa", block)
        kk = r("kk", block)
        cs = r("cs", block)
        dm = r("dm", block)
        e1 = r("e1", block)
        e2 = r("e2", block)
        k2 = r("k2", block)
        tw = r("tw", [P, P])
        gs = [r(f"gs{i}", [P, P]) for i in range(2)]
        sc = [r(f"sc{i}", [P, 2, 2 * P]) for i in range(4)]
        LT = [r(f"LT{i}", block) for i in range(2)]
        MrbT = [r(f"MrbT{i}", block) for i in range(2)]
        MrkT = [r(f"MrkT{i}", block) for i in range(2)]
        LakT = [r(f"LakT{i}", block) for i in range(2)]
        X = [r(f"X{i}", block) for i in range(2)]
        XT = [r(f"XT{i}", block) for i in range(2)]
        W_s = r("W_s", toks)
        G_s = r("G_s", toks)
        QT = r("QT", block)
        phi = [r(f"phi{i}", block) for i in range(2)]
        psi = [r(f"psi{i}", block) for i in range(2)]
        state = [r(f"state{i}", block) for i in range(2)]
        LV = QT[:].rearrange("p a b -> p (a b)").rearrange("p (h d) -> p h d", d=HEAD)
        IY = LakT
        diag = X[0][:].rearrange("p a b -> p (a b)").rearrange("p (h d) -> p h d", d=HEAD)
        yc, y_sq, bv = r("yc", block), r("y_sq", block), r("bv", toks)
        rn8 = r("rn8", [P, HEADS])
        rn_T = k2[0:HEADS, 0, :]
        pm = [r(f"pm{i}", [P, 2 * PAIRS]) for i in range(2)]
        pe_ = [r(f"pe{i}", [P, 2 * PAIRS]) for i in range(2)]
        pc = [r(f"pc{i}", [P, 2 * PAIRS]) for i in range(2)]
        bonus = [r(f"bonus{i}", [P, HEADS]) for i in range(2)]
        mx, nm, es, sums, den = (r(n, [P, HEADS]) for n in ("mx", "nm", "es", "sums", "den"))
        mu8, var8, rstd8 = (r(n, [P, HEADS]) for n in ("mu8", "var8", "rstd8"))

        r = Region(BASE + 10 * KB4)
        xs3 = [r(f"xs3_{i}", [P, D]) for i in range(2)]
        x2 = r("x2", [P, KT, SEQ])
        assert r.at == BASE + N_IN * KB4
        ACT_AT = W_AT - 16 * KB4
        r = Region(ACT_AT, W_AT)
        m_hi = r("m_hi", [P, KT, SEQ], F32R)
        m_lo = r("m_lo", [P, KT, SEQ], F32R)
        r = Region(BASE + N_IN * KB4, ACT_AT)
        sq3 = [r(f"sq3_{i}", [P, SEQ]) for i in range(2)]
        acc3 = r("acc3", [P, SEQ])
        rs3 = r("rs3", [P, SEQ])
        h3 = [r(f"h3_{i}", [P, SEQ]) for i in range(2)]
        r = Region(BASE)
        u_hi = r("u_hi", [P, KT, SEQ], F32R)
        u_r = [r(f"u_r{i}", [P, SEQ]) for i in range(2)]
        u_f = [r(f"u_f{i}", [P, SEQ]) for i in range(2)]
        r = Region(BASE + N_IN * KB4, ACT_AT)
        u_lo = r("u_lo", [P, KT, SEQ], F32R)
        r = Region(BASE)
        fg_s = r("fg_s", [P, D])
        o_s = [r(f"o_s{i}", [P, D]) for i in range(TILES)]
        sq5 = r("sq5", [P, D])
        ss5 = r("ss5", [P, 2 * TILES])
        rs5 = r("rs5", [P, TILES])

        ps = [ctx.enter_context(nc.psum_tensor(f"bank{i}", [P, 512], F32)) for i in range(8)]

        def sem(name):
            return ctx.enter_context(nc.semaphore(name))

        consts_in = sem("consts_in")
        w_in = [sem(f"w_in{i}") for i in range(2)]
        w_hi_ok, w_lo_ok = sem("w_hi_ok"), sem("w_lo_ok")
        proj_full = sem("proj_full")
        act_read, dve_read = sem("act_read"), sem("dve_read")
        x_in = [sem(f"x_in{i}") for i in range(2)]
        x_sq, x_rs, x_root, x_n = sem("x_sq"), sem("x_rs"), sem("x_root"), sem("x_n")
        tr_full, x2_in = sem("tr_full"), sem("x2_in")
        h_raw_ok, h_hi_ok, h_lo_ok = sem("h_raw_ok"), sem("h_hi_ok"), sem("h_lo_ok")
        masks_ok, mask_step = sem("masks_ok"), sem("mask_step")
        z_zero, z_copied, z_diff, z_ok = sem("z_zero"), sem("z_copied"), sem("z_diff"), sem("z_ok")
        bank_full = [sem(f"bank_full{b}") for b in range(8)]
        NAMES = """tw gs gg xw0 aa0 xw1 aa1 xw2 aa2 cs dm dp dpe pm pe e1 e2 pc kx ksq ssm rn rnT kk t2 k2 at kka bt kt
            rt rk ah bh kh A_tok B_tok K_tok V_tok bonus va_tok sc mx m nm dsink es p den rden pT o oT
            LT LI0 LI1 MrbT LakT MrkR MrkT XT1_0 XT1_1 XT X IY LV W G rq QT diag phi psi state
            mu yc ysq var rs rstd yn1 yn2 yn3 bv bvb yn5 rw zero""".split()
        done = {n: sem("s_" + n) for n in NAMES}
        m_hi_ok, m_lo_ok = sem("m_hi_ok"), sem("m_lo_ok")
        x2_sq, x2_acc = sem("x2_sq"), sem("x2_acc")
        ss3_full, rs3_ok, h3_raw = sem("ss3_full"), sem("rs3_ok"), sem("h3_raw")
        u_sq = sem("u_sq")
        fin_sq, fin_rs, fin_root, fin_y, fin_in, out_sent = (
            sem(n) for n in ("fin_sq", "fin_rs", "fin_root", "fin_y", "fin_in", "out_sent"))

        xv = x.rearrange("b (t p) d -> p (b t) d", p=P)
        ov = out.rearrange("b (t p) d -> p (b t) d", p=P)
        MIX_UNITS = N_IN
        U_UP = N_IN + N_OUT

        def bank(name):
            return ps[BANK[name]]

        def wait_read(pe, name, t):
            key, each, i = READER[name]
            pe.wait_ge(done[key], each * t + i)

        def wait_bank(pe, name, t):
            i = USE[name, t]
            if i:
                wait_read(pe, *BANK_USES[BANK[name]][i - 1])

        def wait_full(eng, name, t):
            eng.wait_ge(bank_full[BANK[name]], USE[name, t] + 1)

        def filled(name):
            return bank_full[BANK[name]]

        def tile(t):
            return slice(t * P, (t + 1) * P)

        def slot(g, i):
            return 2 * (2 * (g // 2) + i) + g % 2

        def halves(ap, g):
            return ap[HEAD * g:HEAD * (g + 1)]

        def per_chunk(ap):
            return ap.rearrange("p a (c t) -> p (a c) t", c=CHUNKS)

        def spread(ap, n):
            return ap.unsqueeze(2).to_broadcast([P, ap.shape[1], n])

        def across(ap, m):
            return ap.unsqueeze(1).to_broadcast([ap.shape[0], m, ap.shape[1]])

        def view(ap, m):
            return ap.rearrange("p (m n) -> p m n", m=m)

        def run(steps):
            for step, t in ORDER:
                if step in steps:
                    steps[step](t)

        block_ = ctx.enter_context(nc.Block())

        @block_.sync
        def _(sp):
            sp.dma_start(vecs[:], vec).then_inc(consts_in, 16)

            def load_x(i, bufs, base):
                if i >= 2:
                    sp.wait_ge(tr_full, base + 2 * (i - 1))
                sp.dma_start(bufs[i % 2][:], xv[:, i, :]).then_inc(x_in[i % 2], 16)

            for i in range(2):
                load_x(i, xs, 0)
            for p in range(2):
                sp.dma_start(w_raw[p][:], w_all[p]).then_inc(w_in[p], 16)
            for i in range(2, TILES):
                load_x(i, xs, 0)
            for dst, src in ((w2a2_s, w2a2), (g2_s, g2), (lnw_s, ln_w.to_broadcast([P, 512])),
                             (lnb_s, ln_b.to_broadcast([P, 512])), (sink_s, sinks.to_broadcast([P, HEADS]))):
                sp.dma_start(dst[:], src).then_inc(consts_in, 16)

            def load_w(i):
                for p in range(2):
                    sp.wait_ge(w_hi_ok, 2 * i + p - 1)
                    sp.wait_ge(w_lo_ok, 2 * i + p - 1)
                    sp.dma_start(w_raw[p][:], w_all[2 * i + p]).then_inc(w_in[p], 16)

            with sp.Fori(1, MIX_UNITS // 2 + 1) as i:
                load_w(i)
            sp.wait_ge(done["oT"], TILES)
            sp.wait_ge(done["rw"], TILES)
            for i in range(TILES):
                load_x(i, xs3, 2 * TILES)
            with sp.Fori(MIX_UNITS // 2 + 1, UNITS // 2) as i:
                load_w(i)
            sp.wait_ge(proj_full, 2 * UNITS)
            sp.dma_start(fg_s[:], fin_g.to_broadcast([P, D])).then_inc(fin_in, 16)
            for i in range(TILES):
                sp.wait_ge(fin_y, 2 * (i + 1))
                sp.dma_start(ov[:, i, :], o_s[i][:]).then_inc(out_sent, 16)
            sp.wait_ge(out_sent, 16 * TILES)

        @block_.scalar
        def _(act):
            def A(o, i, f=ACT.Copy, **kw):
                return nc.scalar.activation(o, i, f, **kw)

            def need(name, n):
                if n > 0:
                    act.wait_ge(done[name], n)

            def split_w(m, p, first=False):
                n = 2 * m + p
                act.wait_ge(w_in[p], 16 * m + 16)
                if not first:
                    act.wait_ge(proj_full, 2 * n - 2)
                    act.wait_ge(w_lo_ok, n - 1)
                A(w_hi[p][:], w_raw[p][:]).then_inc(w_hi_ok, 1)

            def h_high(i):
                for j in range(2):
                    act.wait_ge(h_raw_ok, 2 * i + j + 1)
                    A(h_hi[:, 4 * j:4 * j + 4, tile(i)], h_raw[j][:]).then_inc(h_hi_ok, 1)

            for i in range(TILES):
                act.wait_ge(x_in[i % 2], 16 * (i // 2 + 1))
                if i:
                    act.wait_ge(x_sq, i)
                A(z_tmp[0][:, 1:], xs[i % 2][:], ACT.Square, accum_out=ss1[:, i:i + 1]).then_inc(x_sq, 1)
                if i == 0:
                    split_w(0, 0, first=True)
                    split_w(0, 1, first=True)
                else:
                    h_high(i - 1)
            h_high(TILES - 1)
            act.wait_ge(x_sq, TILES)

            def z_plain(m):
                for p in range(2):
                    n = 2 * m + p
                    for h in range(2):
                        act.wait_ge(proj_full, 2 * n + h + 1)
                        A(zT[:, bass.ds(n, 1), h * HALF:(h + 1) * HALF], ps[2 * p + h][:]).then_inc(act_read, 1)
                    split_w(m + 1, p)

            def z_shift(m, first=False, last=False):
                for p in range(2):
                    n = 2 * m + p
                    if first:
                        act.wait_ge(z_zero, 2)
                    else:
                        act.wait_ge(z_ok, n - R0 - 1)
                    for h in range(2):
                        act.wait_ge(proj_full, 2 * n + h + 1)
                        A(z_tmp[p][:, 1 + h * HALF:1 + (h + 1) * HALF], ps[2 * p + h][:])\
                            .then_inc(act_read, 1)
                    if not last:
                        split_w(m + 1, p)

            with act.Fori(0, R0 // 2) as i:
                z_plain(i)
            z_shift(R0 // 2, first=True)
            with act.Fori(R0 // 2 + 1, N_IN // 2 - 1) as i:
                z_shift(i)
            z_shift(N_IN // 2 - 1, last=True)

            act.wait_ge(z_ok, N_SHIFT)
            act.wait_ge(consts_in, 96)

            def tanh(t):
                if t:
                    wait_full(act, "lora_w", t - 1)
                A(tw[0:64], zT[0:64, RWA, tile(t)], ACT.Tanh).then_inc(done["tw"], 1)

            def lora(t):
                need("kx", t + 1)
                need("kt", t)
                need("rk", t)
                A(k2[:], kk[:], ACT.Square).then_inc(done["ksq"], 1)

            def gs_(t):
                if t > 1:
                    wait_full(act, "gate", t - 2)
                A(gs[t % 2][:], zT[:, RG, tile(t)], ACT.Tanh, scale=0.5).then_inc(done["gs"], 1)

            def sig(t):
                need("xw0", t + 1)
                A(xw[:], xw[:], ACT.Tanh, scale=0.5).then_inc(done["xw1"], 1)
                need("aa0", t + 1)
                A(aa[:], aa[:], ACT.Tanh, scale=0.5).then_inc(done["aa1"], 1)

            def norm_T(t):
                wait_full(act, "rnT", t)
                A(rn_T, bank("rnT")[0:HEADS, 0:P]).then_inc(done["rnT"], 1)

            def exps(t):
                b = t % 2
                need("cs", t + 1)
                A(pm[b][:], per_chunk(cs[:])[:, :, CHUNK // 2 - 1], ACT.Exp, scale=-LOG_DECAY).then_inc(done["pm"], 1)
                need("dm", t + 1)
                A(pe_[b][:], per_chunk(dm[:])[:, :, CHUNK - 1], ACT.Exp, scale=-LOG_DECAY).then_inc(done["pe"], 1)
                if t:
                    wait_full(act, "tr_k", t - 1)
                    wait_full(act, "bonus", t - 1)
                A(e2[:], dm[:], ACT.Exp, scale=LOG_DECAY).then_inc(done["e2"], 1)
                A(e1[:], dm[:], ACT.Exp, scale=-LOG_DECAY).then_inc(done["e1"], 1)

            def dpe(t):
                need("dp", t + 1)
                A(xw[:], xw[:], ACT.Exp, scale=-LOG_DECAY).then_inc(done["dpe"], 1)

            def tr_ab(t):
                for name, dst, key in (("tr_a", A_tok, "A_tok"), ("tr_b", B_tok, "B_tok")):
                    wait_full(act, name, t)
                    A(dst[t % 2][:], view(bank(name)[:], HEADS)).then_inc(done[key], 1)

            def tr_kv(t):
                b = t % 2
                if t > 1:
                    need("bv", t - 1)
                for name, dst, key in (("tr_k", K_tok, "K_tok"), ("tr_v", V_tok, "V_tok")):
                    wait_full(act, name, t)
                    A(dst[b][:], view(bank(name)[:], HEADS)).then_inc(done[key], 1)
                wait_full(act, "bonus", t)
                A(bonus[b][:], bank("bonus")[:, 0:HEADS]).then_inc(done["bonus"], 1)
                wait_full(act, "vt", t)
                if t:
                    wait_full(act, "o", t - 1)
                A(va_tok[b][:], bank("vt")[:, 0:P]).then_inc(done["va_tok"], 1)

            def probs(t):
                lo = P if t == 0 else 0
                need("dsink", t + 1)
                A(es[:], es[:], ACT.Exp).then_inc(done["es"], 1)
                need("nm", t + 1)
                need("den", t)
                for g in range(4):
                    for i in range(2):
                        c = slot(g, i)
                        A(sc[g][:, i, lo:], sc[g][:, i, lo:], ACT.Exp, bias=nm[:, c:c + 1], scale=SCALE,
                          accum_out=sums[:, c:c + 1]).then_inc(done["p"], 1)

            def probs_T(t):
                first, by = (1, 2) if t == 0 else (0, 1)
                for g, name in enumerate(("pt00", "pt10", "pt01", "pt11")):
                    wait_full(act, name, t)
                    A(view(sc[g][:].rearrange("p a b -> p (a b)"), 4)[:, first::by, :],
                      view(bank(name)[:], 4)[:, first::by, :]).then_inc(done["pT"], 1)

            def o_T(t):
                wait_full(act, "oT", t)
                A(zT[:, Q0:Q0 + PAIRS, tile(t)], view(bank("oT")[:], PAIRS)).then_inc(done["oT"], 1)

            def mrk(t):
                wait_full(act, "mrk0", t)
                if t:
                    wait_full(act, "yy", t - 1)
                for g in range(2):
                    wait_full(act, f"mrk{g}", t)
                    A(MrkT[g][:], view(bank(f"mrk{g}")[:], PAIRS)).then_inc(done["MrkR"], 1)

            def xt(t):
                need("phi", 4 * t)
                for g in range(2):
                    wait_full(act, f"xt{g}", t)
                    A(X[g][:], view(bank(f"xt{g}")[:], PAIRS)).then_inc(done["X"], 1)

            def lv(t):
                wait_full(act, "lv", t)
                A(LV, view(bank("lv")[:], HEADS)).then_inc(done["LV"], 1)

            def z(k):
                def level_z(t):
                    for dst, key, n in ((X, "X", "z"), (XT, "XT", "zt")):
                        for g in range(2):
                            name = f"{n}{g}_{k}"
                            if name in BANK:
                                wait_full(act, name, t)
                                A(dst[g][:], view(bank(name)[:], PAIRS)).then_inc(done[key], 1)
                return level_z

            def wg(t):
                need("var", t)
                for name, dst, key in (("w", W_s, "W"), ("g", G_s, "G")):
                    wait_full(act, name, t)
                    A(dst[:], view(bank(name)[:], HEADS)).then_inc(done[key], 1)

            def c_(t):
                need("state", 2 * t)
                for c in range(CHUNKS):
                    wait_full(act, f"c{c}", t)
                    for g in range(2):
                        src = halves(view(bank(f"c{c}")[:], PAIRS), g)[:, :, HEAD:]
                        A(halves(psi[c], g)[:, :, HEAD * g:HEAD * (g + 1)], src).then_inc(done["psi"], 1)

            def bv_(t):
                need("yc", t + 1)
                need("var", t)
                A(y_sq[:], yc[:], ACT.Square).then_inc(done["ysq"], 1)

            def out_T(t):
                wait_full(act, "outT", t)
                A(zT[:, R0:R0 + PAIRS, tile(t)], view(bank("outT")[:], PAIRS)).then_inc(done["rw"], 1)

            run({"tanh": tanh, "lora": lora, "gs": gs_, "sig": sig, "rnT": norm_T, "exps": exps, "dpe": dpe,
                 "tr_ab": tr_ab, "tr_kv": tr_kv, "p": probs, "pt": probs_T, "oT": o_T, "mrk": mrk, "xt": xt,
                 "lv": lv, "wg": wg, "c": c_, "bv": bv_, "outT": out_T}
                | {f"z{k}": z(k) for k in range(1, LEVELS)})

            need("oT", TILES)
            need("rw", TILES)
            need("state", 2 * TILES)
            split_w(N_IN // 2, 0)
            split_w(N_IN // 2, 1)
            for k in range(KT):
                A(m_hi[:, k, :], zT[:, k if k < PAIRS else R0 + k - PAIRS, :]).then_inc(m_hi_ok, 1)
            for j in range(N_OUT):
                act.wait_ge(dve_read, 2 * j + 2)
                if j >= 2:
                    act.wait_ge(x2_acc, j - 1)
                A(sq3[j % 2][:], x2[:, j, :], ACT.Square).then_inc(x2_sq, 1)
                n = N_IN + j + 2
                split_w(n // 2, n % 2)
            act.wait_ge(rs3_ok, 2)
            A(rs3[:], rs3[:], ACT.Sqrt).then_inc(rs3_ok, 1)
            for k in range(KT):
                act.wait_ge(h3_raw, k + 1)
                A(m_hi[:, k, :], h3[k % 2][:]).then_inc(m_hi_ok, 1)

            def group(g, last=False):
                with act.Fori(0, 4) as i:
                    for p in range(2):
                        m = U_UP // 2 + 8 * g + i
                        n = 2 * m + p
                        for h in range(2):
                            act.wait_ge(proj_full, 2 * n + h + 1)
                            A(u_r[p][:, h * HALF:(h + 1) * HALF], ps[2 * p + h][:], ACT.Relu)\
                                .then_inc(act_read, 1)
                        split_w(m + 1, p)
                        act.wait_ge(u_sq, 8 * g + 2 * i + p + 1)
                        A(u_hi[:, bass.ds(2 * i + p, 1), :], u_f[p][:]).then_inc(m_hi_ok, 1)
                m = U_UP // 2 + 8 * g + 4
                with act.Fori(0, 3 if last else 4) as i:
                    for p in range(2):
                        split_w(m + i + 1, p)

            with act.Fori(0, GROUPS - 1) as g:
                group(g)
            group(GROUPS - 1, last=True)

            for i in range(TILES):
                for j in range(2):
                    f = 4 * TILES + 2 * i + j
                    act.wait_ge(tr_full, f + 1)
                    if f > 4 * TILES:
                        act.wait_ge(fin_sq, f - 4 * TILES)
                    A(sq5[:, 0:HALF], ps[4 + f % 4][:], ACT.Square, accum_out=ss5[:, 2 * i + j:2 * i + j + 1])\
                        .then_inc(fin_sq, 1)

        @block_.gpsimd
        def _(pool):
            G = nc.gpsimd
            steps = [0]

            def step(ins):
                steps[0] += 1
                ins.then_inc(mask_step, 1)
                pool.wait_ge(mask_step, steps[0])

            def select(ap, pattern, base, mult, fill, op=ALU.is_ge):
                step(G.affine_select(out=ap, in_=ap, compare_op=op, fill=fill, base=base, pattern=pattern,
                                     channel_multiplier=mult))

            step(G.memset(ident[:], 0.0))
            select(ident[:], [[-1, P]], 0, 1, 1.0, ALU.not_equal)
            step(G.memset(ones[:], 1.0))
            step(G.memset(neg_half[:], -0.5))
            for p in range(2):
                G.memset(z_tmp[p][:, 0:1], 0.0).then_inc(z_zero, 1)

            def high_h(i):
                for j in range(2):
                    n = 2 * i + j
                    pool.wait_ge(h_hi_ok, n + 1)
                    o = h_hi[:, 4 * j:4 * j + 4, tile(i)]
                    G.tensor_tensor(h_lo[:, 4 * j:4 * j + 4, tile(i)], h_raw[j][:], o.bitcast(F32), ALU.subtract)\
                        .then_inc(h_lo_ok, 1)

            def split_w(m, p):
                pool.wait_ge(w_hi_ok, 2 * m + p + 1)
                G.tensor_tensor(w_lo[p][:], w_raw[p][:], w_hi[p][:].bitcast(F32), ALU.subtract).then_inc(w_lo_ok, 1)

            split_w(0, 0)
            split_w(0, 1)
            def root(ap, ready, n, out_sem):
                pool.wait_ge(ready, n)
                G.tensor_tensor(ap, ap, neg_half[:, 0:1], ALU.pow).then_inc(out_sem, 1)

            for i in range(TILES):
                root(rs1[:, i:i + 1], x_rs, i + 1, x_root)
                if i:
                    high_h(i - 1)
            high_h(TILES - 1)
            for mask, first in ((strict, -1), (incl, 0)):
                step(G.memset(mask[:], 1.0))
                select(view(mask[:], CHUNKS), [[CHUNK, CHUNKS], [1, CHUNK]], first, -1, 0.0)
                select(view(mask[:], CHUNKS), [[-CHUNK, CHUNKS], [0, CHUNK]], 0, 1, 0.0)
            for k in range(LEVELS):
                w = 1 << k
                mk = view(level[k][:], P // (2 * w))
                rows, cols = (0, w) if k == 0 else (w, 0)
                step(G.memset(level[k][:], 0.0))
                step(G.memset(mk[:, :, cols:cols + w], 1.0))
                select(mk, [[-2 * w, P // (2 * w)], [0, 2 * w]], -rows, 1, 0.0)
                select(mk, [[2 * w, P // (2 * w)], [0, 2 * w]], rows + w - 1, -1, 0.0)
                step(G.tensor_tensor(level[k][:], level[k][:], ident[:], ALU.add))
            step(G.iota(dist[:], pattern=[[-1, 2 * P]], base=P, channel_multiplier=1,
                        allow_small_or_imprecise_dtypes=True))
            select(dist[:], [[-1, 2 * P]], P, 1, FAR)
            select(dist[:], [[1, 2 * P]], -1, -1, FAR)
            step(G.memset(pair_sel[:], 0.0))
            for g in range(2):
                step(G.memset(halves(pair_sel, g)[:, g:g + 1], 1.0))
            step(G.memset(head_up[:], 1.0))
            select(view(head_up[:], HEADS), [[-1, HEADS], [0, HEAD]], 0, 1, 0.0, ALU.is_equal)
            step(G.tensor_tensor(ident64[:], ident[:, 0:HEAD], ident[:, HEAD:P], ALU.add))
            step(G.memset(keep[:], 1.0))
            step(G.memset(view(keep[:], 2 * PAIRS)[:, :, 0:1], 0.0))
            step(G.memset(rk_w[:], 0.0))
            pool.wait_ge(consts_in, 96)
            for g in range(2):
                step(G.tensor_copy(halves(rk_w, g)[:, :, g], halves(vecs, g)[:, C_RK:C_RK + PAIRS]))

            with pool.Fori(1, N_IN // 2) as i:
                for p in range(2):
                    split_w(i, p)

            def need(name, n):
                if n > 0:
                    pool.wait_ge(done[name], n)

            def TT(o, a, b, op=ALU.mult):
                return G.tensor_tensor(o, a, b, op)

            def channels(c):
                return spread(vecs[:, c:c + PAIRS], P)

            pool.wait_ge(z_ok, N_SHIFT)
            for i in range(2):
                for tns in (phi[i], psi[i], state[i]):
                    o = G.memset(tns[:], 0.0)
            o.then_inc(done["zero"], 1)

            def tanh(t):
                need("at", t)
                TT(kk[:], zT[:, RK0:RK0 + PAIRS, tile(t)], channels(C_KK)).then_inc(done["kx"], 1)

            def li(t):
                need("LT", 2 * t + 2)
                TT(LT[1][:], LT[1][:], across(ident[:], PAIRS), ALU.add).then_inc(done["LI1"], 1)
                need("LI1", t + 1)
                TT(XT[1][:], LT[1][:], across(level[0][:], PAIRS)).then_inc(done["XT1_1"], 1)
                need("QT", t)
                TT(per_chunk(rq[:]), per_chunk(rt[:]), spread(pm[t % 2][:], CHUNK)).then_inc(done["rq"], 1)

            def cum(t):
                need("ssm", t + 1)
                TT(rn8[:], rn8[:], neg_half[:], ALU.pow).then_inc(done["rn"], 1)
                need("aa1", t + 1)
                G.tensor_scalar(aa[:], aa[:], 0.5, 0.5, ALU.mult, ALU.add).then_inc(done["aa2"], 1)

            def gs_(t):
                need("gs", t + 1)
                G.tensor_scalar(gs[t % 2][:], gs[t % 2][:], 0.5, 0.5, ALU.mult, ALU.add).then_inc(done["gg"], 1)

            def exps(t):
                need("dm", t + 1)
                need("cs", t + 1)
                TT(xw[:], dm[:], xw[:], ALU.subtract).then_inc(done["dp"], 1)
                need("pm", t + 1)
                need("pe", t + 1)
                TT(pc[t % 2][:], pm[t % 2][:], pe_[t % 2][:]).then_inc(done["pc"], 1)

            def dpe(t):
                need("kk", t + 1)
                need("t2", t + 1)
                TT(aa[:], aa[:], kk[:]).then_inc(done["kka"], 1)

            def abk(t):
                need("kka", t + 1)
                need("e2", t + 1)
                if t:
                    wait_full(pool, "mrk1", t - 1)
                TT(bt[:], aa[:], e2[:]).then_inc(done["bt"], 1)
                need("e1", t + 1)
                TT(rt[:], zT[:, R0:R0 + PAIRS, tile(t)], e1[:]).then_inc(done["rt"], 1)

            def hats(t):
                need("bt", t + 1)
                need("pe", t + 1)
                TT(per_chunk(dm[:]), per_chunk(bt[:]), spread(pe_[t % 2][:], CHUNK)).then_inc(done["bh"], 1)
                need("rt", t + 1)
                need("k2", t + 1)
                TT(e1[:], zT[:, R0:R0 + PAIRS, tile(t)], k2[:]).then_inc(done["rk"], 1)

            def mrk_m(t):
                for g in range(2):
                    need("MrkR", 2 * t + g + 1)
                    TT(MrkT[g][:], MrkT[g][:], across(incl[:], PAIRS)).then_inc(done["MrkT"], 1)

            def z5(t):
                wait_full(pool, f"y0_{LEVELS - 1}", t)
                need("pc", t + 1)
                TT(diag, across(ident64[:], 2 * PAIRS), spread(pc[t % 2][:], HEAD)).then_inc(done["diag"], 1)

            def bv_(t):
                need("V_tok", t + 1)
                need("bonus", t + 1)
                need("yn3", t)
                TT(bv[:], V_tok[t % 2][:], spread(bonus[t % 2][:], HEAD)).then_inc(done["bv"], 1)
                need("bv", t + 1)
                TT(bv[:], bv[:], view(lnb_s[:], HEADS), ALU.add).then_inc(done["bvb"], 1)

            def var(t):
                need("rs", t + 1)
                TT(rstd8[:], var8[:], neg_half[:], ALU.pow).then_inc(done["rstd"], 1)

            run({"tanh": tanh, "li": li, "cum": cum, "gs": gs_, "exps": exps, "dpe": dpe, "abk": abk, "hats": hats,
                 "mrk_m": mrk_m, f"z{LEVELS - 1}": z5, "bv": bv_, "var": var})

            split_w(N_IN // 2, 0)
            split_w(N_IN // 2, 1)
            for k in range(KT):
                pool.wait_ge(m_hi_ok, k + 1)
                TT(m_lo[:, k, :], zT[:, k if k < PAIRS else R0 + k - PAIRS, :], m_hi[:, k, :].bitcast(F32), ALU.subtract)\
                    .then_inc(m_lo_ok, 1)
            for j in range(N_OUT):
                n = N_IN + j + 2
                split_w(n // 2, n % 2)
            for k in range(KT):
                pool.wait_ge(m_hi_ok, KT + k + 1)
                TT(m_lo[:, k, :], h3[k % 2][:], m_hi[:, k, :].bitcast(F32), ALU.subtract).then_inc(m_lo_ok, 1)

            def group(g, last=False):
                with pool.Fori(0, 4) as i:
                    for p in range(2):
                        split_w(U_UP // 2 + 8 * g + i + 1, p)
                        pool.wait_ge(m_hi_ok, 2 * KT + 8 * g + 2 * i + p + 1)
                        c = bass.ds(2 * i + p, 1)
                        TT(u_lo[:, c, :], u_f[p][:].unsqueeze(1), u_hi[:, c, :].bitcast(F32), ALU.subtract)\
                            .then_inc(m_lo_ok, 1)
                with pool.Fori(0, 3 if last else 4) as i:
                    for p in range(2):
                        split_w(U_UP // 2 + 8 * g + 4 + i + 1, p)

            with pool.Fori(0, GROUPS - 1) as g:
                group(g)
            group(GROUPS - 1, last=True)
            for i in range(TILES):
                root(rs5[:, i:i + 1], fin_rs, 2 * i + 2, fin_root)

        @block_.vector
        def _(dve):
            V = nc.vector

            def need(name, n):
                if n > 0:
                    dve.wait_ge(done[name], n)

            dve.wait_ge(consts_in, 16)
            def scale_x(i):
                dve.wait_ge(x_sq, i + 1)
                c = slice(i, i + 1)
                V.tensor_scalar(rs1[:, c], ss1[:, c], 1.0 / D, RMS_EPS, ALU.mult, ALU.add).then_inc(x_rs, 1)
                dve.wait_ge(x_root, i + 1)
                V.tensor_scalar(xs[i % 2][:], xs[i % 2][:], rs1[:, c], None, ALU.mult).then_inc(x_n, 1)

            def gain_h(i):
                for j in range(2):
                    n = 2 * i + j
                    dve.wait_ge(tr_full, n + 1)
                    if i:
                        dve.wait_ge(h_lo_ok, n - 1)
                    V.tensor_tensor(h_raw[j][:], view(ps[4 + n % 4][:], 4),
                                    spread(vecs[:, C_G1 + 4 * j:C_G1 + 4 * j + 4], P), ALU.mult)\
                        .then_inc(h_raw_ok, 1)

            for i in range(TILES):
                scale_x(i)
                if i:
                    gain_h(i - 1)
            gain_h(TILES - 1)

            def shift(m):
                for p in range(2):
                    n = 2 * m + p
                    zn = zT[:, bass.ds(n, 1), :]
                    before, now = z_tmp[p][:, 0:SEQ].unsqueeze(1), z_tmp[p][:, 1:].unsqueeze(1)
                    dve.wait_ge(act_read, 2 * n + 2)
                    V.tensor_tensor(zn, before, now, ALU.subtract).then_inc(z_diff, 1)
                    dve.wait_ge(z_diff, n - R0 + 1)
                    V.scalar_tensor_tensor(out=zn, in0=zn, scalar=vecs[:, bass.ds(n - R0 + C_MU, 1)], in1=now,
                                           op0=ALU.mult, op1=ALU.add).then_inc(z_ok, 1)

            dve.wait_ge(z_zero, 2)
            with dve.Fori(R0 // 2, N_IN // 2) as i:
                shift(i)

            def TT(o, a, b, op=ALU.mult):
                return V.tensor_tensor(o, a, b, op)

            def channels(c):
                return spread(vecs[:, c:c + PAIRS], P)

            dve.wait_ge(z_ok, N_SHIFT)
            dve.wait_ge(consts_in, 96)
            dve.wait_ge(done["zero"], 1)

            def lora(t):
                wait_full(dve, "lora_w", t)
                TT(xw[:], view(bank("lora_w")[:], PAIRS), channels(C_W0), ALU.add).then_inc(done["xw0"], 1)
                wait_full(dve, "lora_a", t)
                need("bt", t)
                TT(aa[:], view(bank("lora_a")[:], PAIRS), channels(C_A0), ALU.add).then_inc(done["aa0"], 1)

            def ssq(t):
                wait_full(dve, "ss", t)
                if t:
                    wait_full(dve, "rnT", t - 1)
                V.tensor_scalar(rn8[:], bank("ss")[:, 0:HEADS], L2_EPS ** 2, None, ALU.max).then_inc(done["ssm"], 1)

            def cum(t):
                need("xw1", t + 1)
                V.tensor_scalar(xw[:], xw[:], 0.5, 0.5, ALU.mult, ALU.add).then_inc(done["xw2"], 1)
                need("xw2", t + 1)
                if t:
                    wait_full(dve, "tr_a", t - 1)
                V.tensor_tensor_scan(cs[:].rearrange("p a b -> p (a b)"), keep[:], xw[:].rearrange("p a b -> p (a b)"),
                                     0.0, ALU.mult, ALU.add).then_inc(done["cs"], 1)

            def mid(t):
                need("cs", t + 1)
                if t:
                    wait_full(dve, "tr_b", t - 1)
                TT(per_chunk(dm[:]), per_chunk(cs[:]),
                   per_chunk(cs[:])[:, :, CHUNK // 2 - 1:CHUNK // 2].to_broadcast([P, 2 * PAIRS, CHUNK]), ALU.subtract)\
                    .then_inc(done["dm"], 1)

            def rx(t):
                need("kx", t + 1)
                wait_full(dve, "rx", t)
                TT(kk[:], kk[:], view(bank("rx")[:], PAIRS)).then_inc(done["kk"], 1)
                need("aa2", t + 1)
                V.scalar_tensor_tensor(out=k2[:], in0=aa[:], scalar=-1.0, in1=channels(C_KA),
                                       op0=ALU.add, op1=ALU.mult).then_inc(done["t2"], 1)
                need("t2", t + 1)
                V.scalar_tensor_tensor(out=k2[:], in0=k2[:], scalar=1.0, in1=zT[:, RK0:RK0 + PAIRS, tile(t)],
                                       op0=ALU.add, op1=ALU.mult).then_inc(done["k2"], 1)

            def abk(t):
                need("k2", t + 1)
                need("e2", t + 1)
                if t:
                    wait_full(dve, "mrk1", t - 1)
                TT(kt[:], k2[:], e2[:]).then_inc(done["kt"], 1)
                need("kk", t + 1)
                need("dpe", t + 1)
                V.scalar_tensor_tensor(out=at[:], in0=kk[:], scalar=-1.0, in1=xw[:],
                                       op0=ALU.mult, op1=ALU.mult).then_inc(done["at"], 1)

            def hats(t):
                b = t % 2
                need("at", t + 1)
                need("pm", t + 1)
                TT(per_chunk(cs[:]), per_chunk(at[:]), spread(pm[b][:], CHUNK)).then_inc(done["ah"], 1)
                need("kt", t + 1)
                need("pe", t + 1)
                need("bt", t + 1)
                TT(per_chunk(e2[:]), per_chunk(kt[:]), spread(pe_[b][:], CHUNK)).then_inc(done["kh"], 1)

            def scores(groups):
                def biased(t):
                    lo = P if t == 0 else 0
                    if t:
                        wait_full(dve, "oT", t - 1)
                    need("rden", t)
                    for g, name in groups:
                        wait_full(dve, name, t)
                        for i in range(2):
                            head = 2 * (g // 2) + i + PAIRS * (g % 2)
                            slope = 2.0 ** -(head + 1)
                            V.scalar_tensor_tensor(out=sc[g][:, i, lo:], in0=dist[:, lo:], scalar=-slope / SCALE,
                                                   in1=bank(name)[:, 2 * P * i + lo:2 * P * (i + 1)],
                                                   op0=ALU.mult, op1=ALU.add).then_inc(done["sc"], 1)
                        need("sc", 8 * t + 2 * g + 2)
                        V.tensor_reduce(mx[:, slot(g, 0):slot(g, 1) + 1:2], sc[g][:, :, lo:], AX.X, ALU.max)\
                            .then_inc(done["mx"], 1)
                return biased

            sc_b = scores([(2, "sc01"), (3, "sc11")])

            def sc_max(t):
                sc_b(t)
                need("mx", 4 * t + 4)
                V.scalar_tensor_tensor(out=mx[:], in0=mx[:], scalar=SCALE, in1=sink_s[:], op0=ALU.mult, op1=ALU.max)\
                    .then_inc(done["m"], 1)
                need("m", t + 1)
                TT(es[:], sink_s[:], mx[:], ALU.subtract).then_inc(done["dsink"], 1)
                need("p", 8 * t)
                V.tensor_scalar(nm[:], mx[:], -1.0, None, ALU.mult).then_inc(done["nm"], 1)

            def den_(t):
                need("es", t + 1)
                need("p", 8 * t + 8)
                TT(den[:], es[:], sums[:], ALU.add).then_inc(done["den"], 1)
                need("den", t + 1)
                V.reciprocal(den[:], den[:]).then_inc(done["rden"], 1)

            def o_(t):
                wait_full(dve, "o", t)
                need("rden", t + 1)
                TT(view(sc[0][:].rearrange("p a b -> p (a b)"), HEADS), view(bank("o")[:], HEADS), spread(den[:], HEAD))\
                    .then_inc(done["o"], 1)

            def masked(name, dst, mask, key):
                def evacuate(t):
                    if t and name == "mrb":
                        wait_full(dve, "yy", t - 1)
                    for g in range(2):
                        n = f"{name}{g}"
                        wait_full(dve, n, t)
                        TT(dst[g][:], view(bank(n)[:], PAIRS), across(mask[:], PAIRS)).then_inc(done[key], 1)
                return evacuate

            def li(t):
                need("LT", 2 * t + 1)
                TT(LT[0][:], LT[0][:], across(ident[:], PAIRS), ALU.add).then_inc(done["LI0"], 1)
                need("LI0", t + 1)
                TT(XT[0][:], LT[0][:], across(level[0][:], PAIRS)).then_inc(done["XT1_0"], 1)

            def y(k):
                def level_y(t):
                    for g in range(2):
                        n = f"y{g}_{k}"
                        wait_full(dve, n, t)
                        TT(IY[g][:], view(bank(n)[:], PAIRS), across(level[k][:], PAIRS)).then_inc(done["IY"], 1)
                return level_y

            def rq_(t):
                wait_full(dve, "rq", t)
                need("rq", t + 1)
                TT(QT[:], view(bank("rq")[:], PAIRS), rq[:], ALU.add).then_inc(done["QT"], 1)

            def c_(t):
                need("diag", t + 1)
                dg = diag.rearrange("p (a c) d -> p a c d", c=CHUNKS)
                for c in range(CHUNKS):
                    need("psi", 4 * t + 2 * c + 2)
                    for g in range(2):
                        TT(halves(phi[c], g)[:, :, HEAD * g:HEAD * (g + 1)],
                           halves(view(bank(f"c{c}")[:], PAIRS), g)[:, :, 0:HEAD], halves(dg, g)[:, :, c, :],
                           ALU.add).then_inc(done["phi"], 1)

            def advance(c):
                def new_state(t):
                    wait_full(dve, f"st{c}", t)
                    need("psi", 4 * t + 2 * c + 2)
                    if c:
                        wait_full(dve, "yy", t)
                    elif t:
                        wait_full(dve, "st1", t - 1)
                    TT(state[1 - c][:], view(bank(f"st{c}")[:], PAIRS), psi[c][:], ALU.add).then_inc(done["state"], 1)
                return new_state

            yh = view(yc[:].rearrange("p a b -> p (a b)"), HEADS)

            def mu_(t):
                wait_full(dve, "yy", t)
                V.tensor_reduce(mu8[:], view(bank("yy")[:], HEADS), AX.X, ALU.add).then_inc(done["mu"], 1)
                need("mu", t + 1)
                if t:
                    wait_full(dve, "outT", t - 1)
                V.scalar_tensor_tensor(out=yh, in0=spread(mu8[:], HEAD), scalar=-1.0 / HEAD,
                                       in1=view(bank("yy")[:], HEADS), op0=ALU.mult, op1=ALU.add).then_inc(done["yc"], 1)

            def var_(t):
                need("ysq", t + 1)
                V.tensor_reduce(var8[:], view(y_sq[:].rearrange("p a b -> p (a b)"), HEADS), AX.X, ALU.add)\
                    .then_inc(done["var"], 1)
                need("var", t + 1)
                V.tensor_scalar(var8[:], var8[:], 1.0 / HEAD, GN_EPS, ALU.mult, ALU.add).then_inc(done["rs"], 1)

            def yn(t):
                need("rstd", t + 1)
                TT(yh, yh, spread(rstd8[:], HEAD)).then_inc(done["yn1"], 1)
                need("yn1", t + 1)
                TT(yc[:], yc[:], view(lnw_s[:], PAIRS)).then_inc(done["yn2"], 1)

            def gate_(t):
                need("yn2", t + 1)
                need("bvb", t + 1)
                TT(yh, yh, bv[:], ALU.add).then_inc(done["yn3"], 1)
                need("yn3", t + 1)
                wait_full(dve, "gate", t)
                TT(yc[:], yc[:], view(bank("gate")[:], PAIRS)).then_inc(done["yn5"], 1)

            run({"lora": lora, "ssq": ssq, "cum": cum, "mid": mid, "rx": rx, "abk": abk, "hats": hats,
                 "sc_a": scores([(0, "sc00"), (1, "sc10")]), "sc_b": sc_max, "den": den_, "o": o_,
                 "lab": masked("lab", LT, strict, "LT"), "lak": masked("lak", LakT, strict, "LakT"),
                 "mrb": masked("mrb", MrbT, incl, "MrbT"), "li": li, "rq": rq_, "c": c_, "st0": advance(0),
                 "st1": advance(1), "mu": mu_, "var": var_, "yn": yn, "gate": gate_}
                | {f"y{k}": y(k) for k in range(1, LEVELS)})

            for f in range(2 * TILES):
                i, j = divmod(f, 2)
                dve.wait_ge(tr_full, 2 * TILES + f + 1)
                V.tensor_copy(x2[:, 4 * j:4 * j + 4, tile(i)], view(ps[4 + f % 4][:], 4)).then_inc(x2_in, 1)
            dve.wait_ge(x2_in, 2 * TILES)

            for j in range(N_OUT):
                for h in range(2):
                    n = N_IN + j
                    dve.wait_ge(proj_full, 2 * n + h + 1)
                    o = x2[:, j, h * HALF:(h + 1) * HALF]
                    V.tensor_tensor(o, o, ps[2 * (n % 2) + h][:], ALU.add).then_inc(dve_read, 1)
                dve.wait_ge(x2_sq, j + 1)
                if j:
                    dve.wait_ge(x2_acc, j)
                    V.tensor_tensor(acc3[:], acc3[:], sq3[j % 2][:], ALU.add).then_inc(x2_acc, 1)
                else:
                    V.tensor_copy(acc3[:], sq3[0][:]).then_inc(x2_acc, 1)
            for h in range(2):
                c = slice(h * HALF, (h + 1) * HALF)
                dve.wait_ge(ss3_full, h + 1)
                V.tensor_scalar(rs3[:, c], ps[4 + h][:], 1.0 / D, RMS_EPS, ALU.mult, ALU.add).then_inc(rs3_ok, 1)
            dve.wait_ge(rs3_ok, 3)
            V.reciprocal(rs3[:], rs3[:]).then_inc(rs3_ok, 1)
            dve.wait_ge(rs3_ok, 4)
            for k in range(KT):
                if k >= 2:
                    dve.wait_ge(m_lo_ok, KT + k - 1)
                V.scalar_tensor_tensor(out=h3[k % 2][:], in0=x2[:, k, :], scalar=vecs[:, C_G2 + k:C_G2 + k + 1],
                                       in1=rs3[:], op0=ALU.mult, op1=ALU.mult).then_inc(h3_raw, 1)

            with dve.Fori(0, GROUPS) as g:
                with dve.Fori(0, 4) as i:
                    for p in range(2):
                        e = 8 * g + 2 * i + p
                        dve.wait_ge(act_read, 2 * (N_IN + e) + 2)
                        dve.wait_ge(m_lo_ok, 2 * KT + e - 1)
                        V.tensor_tensor(u_f[p][:], u_r[p][:], u_r[p][:], ALU.mult).then_inc(u_sq, 1)
                with dve.Fori(0, 4) as i:
                    for p in range(2):
                        n = U_UP + 16 * g + 8 + 2 * i + p
                        for h in range(2):
                            dve.wait_ge(proj_full, 2 * n + h + 1)
                            o = x2[:, bass.ds(2 * i + p, 1), h * HALF:(h + 1) * HALF]
                            V.tensor_tensor(o, o, ps[2 * p + h][:].unsqueeze(1), ALU.add)\
                                .then_inc(dve_read, 1)

            dve.wait_ge(fin_in, 16)
            for i in range(TILES):
                c = slice(i, i + 1)
                dve.wait_ge(fin_sq, 2 * i + 2)
                V.tensor_tensor(rs5[:, c], ss5[:, 2 * i:2 * i + 1], ss5[:, 2 * i + 1:2 * i + 2], ALU.add).then_inc(fin_rs, 1)
                dve.wait_ge(fin_rs, 2 * i + 1)
                V.tensor_scalar(rs5[:, c], rs5[:, c], 1.0 / D, RMS_EPS, ALU.mult, ALU.add).then_inc(fin_rs, 1)
                dve.wait_ge(fin_root, i + 1)
                for j in range(2):
                    f = 4 * TILES + 2 * i + j
                    V.scalar_tensor_tensor(out=o_s[i][:, j * HALF:(j + 1) * HALF], in0=ps[4 + f % 4][:],
                                           scalar=rs5[:, c], in1=fg_s[:, j * HALF:(j + 1) * HALF],
                                           op0=ALU.mult, op1=ALU.mult).then_inc(fin_y, 1)

        @block_.tensor
        def _(pe):
            M = nc.tensor.matmul

            def need(name, n):
                if n > 0:
                    pe.wait_ge(done[name], n)

            def turn(read, source, i):
                for j in range(2):
                    f = 2 * i + j
                    if f >= 4:
                        pe.wait_ge(read, f - 3)
                    for k in range(4):
                        o = nc.tensor.transpose(ps[4 + f % 4][:, k * P:(k + 1) * P], source(4 * j + k), ident[:])
                    o.then_inc(tr_full, 1)

            def unit(m, p, hi, lo):
                n = 2 * m + p
                pe.wait_ge(w_hi_ok, n + 1)
                pe.wait_ge(w_lo_ok, n + 1)
                for k in range(KT):
                    for s, (w, a) in enumerate(((w_hi, hi), (w_hi, lo), (w_lo, hi))):
                        for h in range(2):
                            o = M(ps[2 * p + h][:], w[p][:, k, :], a[:, k, h * HALF:(h + 1) * HALF],
                                  start=k == 0 and s == 0, stop=k == KT - 1 and s == 2)
                            if k == KT - 1 and s == 2:
                                o.then_inc(proj_full, 1)

            pe.wait_ge(mask_step, 3)
            for i in range(TILES):
                pe.wait_ge(x_n, i + 1)
                turn(h_raw_ok, lambda k: xs[i % 2][:, k * P:(k + 1) * P], i)
            pe.wait_ge(h_hi_ok, 2 * TILES)
            pe.wait_ge(h_lo_ok, 2 * TILES)
            unit(0, 0, h_hi, h_lo)
            unit(0, 1, h_hi, h_lo)
            with pe.Fori(1, N_IN // 2) as i:
                for p in range(2):
                    pe.wait_ge(act_read, 4 * i + 2 * p - 2)
                    unit(i, p, h_hi, h_lo)

            pe.wait_ge(h_raw_ok, 2 * TILES)
            pe.wait_ge(act_read, 2 * N_IN)
            pe.wait_ge(z_ok, N_SHIFT)
            pe.wait_ge(consts_in, 96)
            pe.wait_ge(done["zero"], 1)

            def four(name, t, f):
                wait_bank(pe, name, t)
                for a in range(PAIRS):
                    o = f(bank(name)[:, a * P:(a + 1) * P], a)
                o.then_inc(filled(name), 1)

            def heads(name, t, f):
                wait_bank(pe, name, t)
                for h in range(HEADS):
                    o = f(bank(name)[:, h * HEAD:(h + 1) * HEAD], h, *divmod(h, 2))
                o.then_inc(filled(name), 1)

            def product(to, w, m):
                return M(to, w, m, start=True, stop=True)

            def turned(to, src):
                return nc.tensor.transpose(to, src, ident[:])

            def lora(t):
                need("tw", t + 1)
                four("lora_w", t, lambda to, a: product(to, w2a2_s[0:64, a * P:(a + 1) * P], tw[0:64, :]))
                four("lora_a", t, lambda to, a: product(to, w2a2_s[64:P, a * P:(a + 1) * P], zT[64:P, RWA, tile(t)]))

            def ssq(t):
                need("ksq", t + 1)
                wait_bank(pe, "ss", t)
                for a in range(PAIRS):
                    o = product(bank("ss")[:, 2 * a:2 * a + 2], k2[:, a, :], pair_sel[:])
                o.then_inc(filled("ss"), 1)

            def norm_T(t):
                need("rn", t + 1)
                wait_bank(pe, "rnT", t)
                turned(bank("rnT")[0:HEADS, 0:P], rn8[:]).then_inc(filled("rnT"), 1)

            def rx(t):
                need("rnT", t + 1)
                four("rx", t, lambda to, a: product(to, head_up[0:HEADS, a * P:(a + 1) * P], rn_T))

            def tr_ab(t):
                need("ah", t + 1)
                four("tr_a", t, lambda to, a: turned(to, cs[:, a, :]))
                need("bh", t + 1)
                four("tr_b", t, lambda to, a: turned(to, dm[:, a, :]))

            def tr_kv(t):
                need("kh", t + 1)
                four("tr_k", t, lambda to, a: turned(to, e2[:, a, :]))
                four("tr_v", t, lambda to, a: turned(to, zT[:, RV0 + a, tile(t)]))
                need("rk", t + 1)
                wait_bank(pe, "bonus", t)
                for a in range(PAIRS):
                    o = product(bank("bonus")[:, 2 * a:2 * a + 2], e1[:, a, :], rk_w[:, a, :])
                o.then_inc(filled("bonus"), 1)
                wait_bank(pe, "vt", t)
                turned(bank("vt")[:, 0:P], zT[:, V0, tile(t)]).then_inc(filled("vt"), 1)

            def attend(groups):
                def queries_keys(t):
                    lo = P if t == 0 else 0
                    for g, name in groups:
                        wait_bank(pe, name, t)
                        par = g % 2
                        for i in range(2):
                            o = product(bank(name)[:, 2 * P * i + lo:2 * P * (i + 1)],
                                        halves(zT, par)[:, Q0 + 2 * (g // 2) + i, tile(t)],
                                        halves(zT, par)[:, K0, t * P - P + lo:t * P + P])
                        o.then_inc(filled(name), 1)
                return queries_keys

            def probs_T(t):
                for g, name in enumerate(("pt00", "pt10", "pt01", "pt11")):
                    need("p", 8 * t + 2 * g + 2)
                    wait_bank(pe, name, t)
                    for i in range(2):
                        for k in range(1 if t == 0 else 0, 2):
                            q = 2 * i + k
                            o = turned(bank(name)[:, q * P:(q + 1) * P], sc[g][:, i, k * P:(k + 1) * P])
                    o.then_inc(filled(name), 1)

            def o_(t):
                wait_bank(pe, "o", t)
                need("va_tok", t + 1)
                for g in range(4):
                    need("pT", 4 * t + g + 1)
                    for i in range(2):
                        c = slot(g, i)
                        kv = g % 2
                        for k in range(1 if t == 0 else 0, 2):
                            o = M(bank("o")[:, c * HEAD:(c + 1) * HEAD], sc[g][:, i, k * P:(k + 1) * P],
                                  va_tok[(t - 1 + k) % 2][:, kv * HEAD:(kv + 1) * HEAD],
                                  start=k == 0 or t == 0, stop=k == 1)
                o.then_inc(filled("o"), 1)

            def o_T(t):
                need("o", t + 1)
                o_tok = view(sc[0][:].rearrange("p a b -> p (a b)"), PAIRS)
                four("oT", t, lambda to, a: turned(to, o_tok[:, a, :]))

            def scores(name, keys, queries, *ready):
                def keys_queries(t):
                    for r in ready:
                        need(r, t + 1)
                    for g in range(2):
                        four(f"{name}{g}", t, lambda to, a: product(to, halves(keys, g)[:, a, :], halves(queries, g)[:, a, :]))
                return keys_queries

            def xt(t):
                for g in range(2):
                    need(f"XT1_{g}", t + 1)
                    four(f"xt{g}", t, lambda to, a: turned(to, XT[g][:, a, :]))

            def lv(t):
                need("LakT", 2 * t + 2)
                need("V_tok", t + 1)
                heads("lv", t, lambda to, h, a, g: product(to, LakT[g][:, a, :], V_tok[t % 2][:, h, :]))

            turns = 2 * (LEVELS - 1)

            def y(k):
                def level_y(t):
                    for g in range(2):
                        if k == 1:
                            need(f"LI{g}", t + 1)
                        need("X", turns * t + 2 * (k - 1) + g + 1)
                        four(f"y{g}_{k}", t, lambda to, a: product(to, LT[g][:, a, :], X[g][:, a, :]))
                return level_y

            def z(k):
                def level_z(t):
                    for g in range(2):
                        need("IY", turns * t + 2 * (k - 1) + g + 1)
                        if k > 1:
                            need("XT", turns * t + 2 * (k - 2) + g + 1)
                        if f"z{g}_{k}" in BANK:
                            four(f"z{g}_{k}", t, lambda to, a: product(to, XT[g][:, a, :], IY[g][:, a, :]))
                    for g in range(2):
                        four(f"zt{g}_{k}", t, lambda to, a: product(to, IY[g][:, a, :], XT[g][:, a, :]))
                return level_z

            def wg(t):
                need("XT", turns * (t + 1))
                need("A_tok", t + 1)
                heads("w", t, lambda to, h, a, g: product(to, XT[g][:, a, :], A_tok[t % 2][:, h, :]))
                need("LV", t + 1)
                heads("g", t, lambda to, h, a, g: product(to, XT[g][:, a, :], LV[:, h, :]))

            def rq_(t):
                need("W", t + 1)
                need("MrbT", 2 * t + 2)
                wait_bank(pe, "rq", t)
                for h in range(HEADS):
                    a, g = divmod(h, 2)
                    o = product(halves(bank("rq"), g)[:, a * P:(a + 1) * P], W_s[:, h, :], MrbT[g][:, a, :])
                o.then_inc(filled("rq"), 1)

            def c_(t):
                b = t % 2
                need("G", t + 1)
                need("B_tok", t + 1)
                need("K_tok", t + 1)
                for c in range(CHUNKS):
                    wait_bank(pe, f"c{c}", t)
                    for h in range(HEADS):
                        a, g = divmod(h, 2)
                        to = halves(bank(f"c{c}"), g)[:, a * P:(a + 1) * P]
                        row = slice(c * CHUNK, (c + 1) * CHUNK)
                        product(to[:, 0:HEAD], W_s[row, h, :], B_tok[b][row, h, :])
                        M(to[:, HEAD:], B_tok[b][row, h, :], G_s[row, h, :], start=True, stop=False)
                        o = M(to[:, HEAD:], K_tok[b][row, h, :], V_tok[b][row, h, :], start=False, stop=True)
                    o.then_inc(filled(f"c{c}"), 1)

            def advance(c):
                def next_state(t):
                    need("phi", 4 * t + 2 * c + 2)
                    need("state", 2 * t + c)
                    four(f"st{c}", t, lambda to, a: product(to, phi[c][:, a, :], state[c][:, a, :]))
                return next_state

            def yy(t):
                b = t % 2
                need("QT", t + 1)
                need("MrkT", 2 * t + 2)
                need("state", 2 * t + 1)
                wait_bank(pe, "yy", t)
                for a in range(PAIRS):
                    for c in range(CHUNKS):
                        row = slice(c * CHUNK, (c + 1) * CHUNK)
                        M(bank("yy")[row, a * P:(a + 1) * P], QT[:, a, row], state[c][:, a, :], start=True, stop=False,
                          skip_group_check=True)
                    for g in range(2):
                        h = 2 * a + g
                        to = bank("yy")[:, h * HEAD:(h + 1) * HEAD]
                        M(to, MrbT[g][:, a, :], G_s[:, h, :], start=False, stop=False, skip_group_check=True)
                        o = M(to, MrkT[g][:, a, :], V_tok[b][:, h, :], start=False, stop=g == 1, skip_group_check=True)
                o.then_inc(filled("yy"), 1)

            def gate_(t):
                need("gg", t + 1)
                wait_bank(pe, "gate", t)
                product(bank("gate")[:], gs[t % 2][:], g2_s[:]).then_inc(filled("gate"), 1)

            def out_T(t):
                need("yn5", t + 1)
                four("outT", t, lambda to, a: turned(to, yc[:, a, :]))

            run({"lora": lora, "ssq": ssq, "rnT": norm_T, "rx": rx, "tr_ab": tr_ab, "tr_kv": tr_kv,
                 "sc_a": attend([(0, "sc00"), (1, "sc10")]), "sc_b": attend([(2, "sc01"), (3, "sc11")]),
                 "pt": probs_T, "o": o_, "oT": o_T,
                 "lab": scores("lab", bt, at, "bt", "at"), "lak": scores("lak", kt, at, "kt"),
                 "mrb": scores("mrb", bt, rt, "rt"), "mrk": scores("mrk", kt, rt),
                 "xt": xt, "lv": lv, "wg": wg, "rq": rq_, "c": c_, "st0": advance(0), "st1": advance(1),
                 "yy": yy, "gate": gate_, "outT": out_T}
                | {f"y{k}": y(k) for k in range(1, LEVELS)} | {f"z{k}": z(k) for k in range(1, LEVELS)})

            for uses in BANK_USES.values():
                wait_read(pe, *uses[-1])
            for i in range(TILES):
                pe.wait_ge(x_in[i % 2], 16 * (TILES // 2 + i // 2 + 1))
                turn(x2_in, lambda k: xs3[i % 2][:, k * P:(k + 1) * P], i)
            pe.wait_ge(m_hi_ok, KT)
            pe.wait_ge(m_lo_ok, KT)
            unit(N_IN // 2, 0, m_hi, m_lo)
            unit(N_IN // 2, 1, m_hi, m_lo)
            with pe.Fori(1, N_OUT // 2) as i:
                for p in range(2):
                    pe.wait_ge(dve_read, 4 * i + 2 * p - 2)
                    unit(N_IN // 2 + i, p, m_hi, m_lo)
            pe.wait_ge(x2_acc, N_OUT)
            pe.wait_ge(x2_in, 2 * TILES)
            for h in range(2):
                M(ps[4 + h][:], ones[:], acc3[:, h * HALF:(h + 1) * HALF], start=True, stop=True).then_inc(ss3_full, 1)
            pe.wait_ge(m_hi_ok, 2 * KT)
            pe.wait_ge(m_lo_ok, 2 * KT)
            with pe.Fori(0, GROUPS) as g:
                with pe.Fori(0, 4) as i:
                    for p in range(2):
                        pe.wait_ge(dve_read, 2 * (N_OUT + 8 * g) - 2 * (1 - p))
                        pe.wait_ge(act_read, 2 * (N_IN + 8 * g + 2 * i + p - 1))
                        unit(U_UP // 2 + 8 * g + i, p, m_hi, m_lo)
                with pe.Fori(0, 4) as i:
                    for p in range(2):
                        pe.wait_ge(m_hi_ok, 2 * KT + 8 * g + 8)
                        pe.wait_ge(m_lo_ok, 2 * KT + 8 * g + 8)
                        pe.wait_ge(act_read, 2 * (N_IN + 8 * g + 8) - 2 * (1 - p))
                        pe.wait_ge(dve_read, 2 * (N_OUT + 8 * g + 2 * i + p - 1))
                        unit(U_UP // 2 + 8 * g + 4 + i, p, u_hi, u_lo)
            pe.wait_ge(dve_read, 2 * N_OUT * (1 + GROUPS))
            for i in range(TILES):
                turn(fin_y, lambda k: x2[:, k, tile(i)], i)


def kernel(x, attn_norm_g, w_in, attn_sinks, rwkv_mu, w0, w2, a0, a2, g2, k_k, k_a, r_k,
           ln_x_w, ln_x_b, w_out, mlp_norm_g, w_up, w_down, final_norm_g):
    import numpy as np
    import concourse.bacc as bacc
    from concourse.bass_utils import run_bass_kernel_spmd as run

    def arr(a):
        return np.ascontiguousarray(a)

    def blocks(v):
        return np.asarray(v).reshape(-1, P).T

    def units(w):
        n = w.shape[1] // P
        return w.reshape(KT, P, n, P).transpose(2, 1, 0, 3).reshape(n, P, KT * P)

    wi = np.asarray(w_in)[0]
    q = wi[:, :512].reshape(D, 2, 4, HEAD).transpose(0, 2, 1, 3).reshape(D, 512)
    wo = np.asarray(w_out)[0]
    o = wo[:512].reshape(2, 4, HEAD, D).transpose(1, 0, 2, 3).reshape(512, D)
    wu, wd = np.asarray(w_up)[0], np.asarray(w_down)[0]
    parts = [units(np.concatenate([q, wi[:, 512:]], 1)), units(np.concatenate([o, wo[512:]], 0))]
    for g in range(GROUPS):
        parts += [units(wu[:, g * 1024:(g + 1) * 1024]), units(wd[g * 1024:(g + 1) * 1024])]
    vec = np.concatenate([blocks(v) for v in (rwkv_mu, w0, a0, k_k, k_a, r_k, attn_norm_g, mlp_norm_g)], 1)
    ins = {
        "x": arr(x),
        "w_all": arr(np.concatenate(parts, 0)),
        "vec": arr(vec),
        "sinks": arr(np.asarray(attn_sinks).reshape(2, 4).T.reshape(1, HEADS)),
        "w2a2": arr(np.concatenate([np.asarray(w2)[0], np.asarray(a2)[0]], 0)),
        "g2": arr(np.asarray(g2)[0]),
        "ln_w": arr(ln_x_w), "ln_b": arr(ln_x_b),
        "fin_g": arr(np.asarray(final_norm_g).reshape(1, D)),
    }
    nc = bacc.Bacc("TRN2", target_bir_lowering=False, num_devices=1)
    aps = [nc.dram_tensor(f"in_{n}", a.shape, F32, kind="ExternalInput").ap() for n, a in ins.items()]
    out = nc.dram_tensor("out_0", x.shape, F32, kind="ExternalOutput").ap()
    build(nc, *aps, out)
    r = run(nc, [{f"in_{n}": a for n, a in ins.items()}], core_ids=[0])
    return r.results[0]["out_0"]
```

```python
from contextlib import ExitStack
import math

import concourse.bass as bass
from concourse import mybir

F32 = mybir.dt.float32
F32R = mybir.dt.float32r
ALU = mybir.AluOpType
ACT = mybir.ActivationFunctionType
AX = mybir.AxisListType

P = 128
SEQ = 1024
D = 1024
KT = D // P
EARLY = 3
LOW_POOL, LOW_V = (0, 4, 6), (1, 2, 3, 5, 7)
HEAD = 64
HEADS = 8
KV = 2
PAIRS = HEADS // 2
CHUNK = 64
TILES = SEQ // P
CHUNKS = P // CHUNK
HALF = 512
D_FF = 4 * D
R0, RK0, RV0, RWA, RG = 0, 4, 8, 12, 13
Q0, K0, V0 = 14, 18, 19
N_IN = 20
N_SHIFT = Q0
N_OUT = 8
GROUPS = 4
UNITS = N_IN + N_OUT + GROUPS * 16
RMS_EPS = 1e-6
GN_EPS = 64e-5
L2_EPS = 1e-12
LOG_DECAY = math.exp(-0.5)
SCALE = HEAD ** -0.5
FAR = 1.0e32
LEVELS = CHUNK.bit_length() - 1

C_MU, C_W0, C_A0, C_KK, C_KA, C_RK = 0, 14, 18, 22, 26, 30
C_G1, C_G2, C_GF, N_VEC = 34, 42, 50, 58

SCHEDULE = [
    ("lab", 0), ("yy0", -1), ("li", 0), ("lora", 1), ("yy1", -1), ("lak", 0), ("yy2", -1), ("st1", -1), ("yy3", -1),
    ("mrb", 0),
    ("mu", -1), ("sig", 1), ("ssq", 1), ("mrb_m", 0), ("mrk", 0), ("ysq", -1), ("bv", -1),
    ("xt", 0), ("mrk_e", 0), ("pt_a", 0), ("lv", 0), ("pt_b", 0),
    ("y1", 0), ("o_a", 0), ("cum", 1), ("var", -1), ("z1", 0), ("o_b", 0),
    ("y2", 0), ("tx2", 0), ("rnT", 1), ("o", 0), ("mid", 1), ("mrk_m", 0), ("yn", -1), ("z2", 0),
    ("y3", 0), ("tx3", 0), ("oT", 0), ("rx", 1), ("gate", -1), ("yg", -1), ("exps", 1), ("gs", 1), ("z3", 0),
    ("y4", 0), ("tx4", 0), ("dpe", 1), ("sc_a", 1), ("abk", 1), ("z4", 0),
    ("y5", 0), ("tx5", 0), ("sc_b", 1), ("hats", 1), ("z5", 0),
    ("outT", -1), ("tr_v", 1), ("wg", 0), ("bonus", 1), ("tanh", 2), ("rq", 0), ("c_a", 0), ("tr_ab", 1),
    ("c", 0), ("tr_k", 1), ("st0", 0), ("p", 1), ("den", 1),
]
AFTER = {"mrk_m": 0, "z2": 1, "y3": 2, "z3": 3, "y4": 4, "z4": 5, "y5": 6, "wg": 7}
FIRST = [
    ("proj", Q0), ("shifted", 0), ("tanh", 0), ("lora", 0), ("sig", 0), ("proj", Q0 + 1), ("ssq", 0), ("cum", 0),
    ("proj", Q0 + 2), ("rnT", 0), ("mid", 0), ("exps", 0), ("proj", Q0 + 3), ("rx", 0), ("dpe", 0), ("proj", K0),
    ("proj", V0), ("mix", 0), ("abk", 0), ("tr_v", 0), ("sc_a", 0), ("hats", 0), ("sc_b", 0), ("bonus", 0),
    ("tr_ab", 0), ("tanh", 1), ("tr_k", 0), ("gs", 0), ("zero", 0), ("p", 0), ("den", 0),
]
END = TILES - 1
LAST = [
    ("split_a", 0), ("yy0", END), ("st1", END), ("yy1", END), ("gate", END), ("yy2", END), ("yy3", END), ("bv", END),
    ("mu", END), ("ysq", END), ("var", END), ("yn", END), ("yg", END), ("out_a", 0), ("outT", END), ("out_b", 0),
]
ORDER = list(FIRST)
for _i in range(TILES):
    for _step, _lag in SCHEDULE:
        if 0 <= _i + _lag < TILES:
            ORDER.append((_step, _i + _lag))
        if _i == TILES - 1 and _step in AFTER:
            ORDER.append(("res", AFTER[_step]))
ORDER += LAST

MAKES = {
    "lora": [("lora_w", 6), ("lora_a", 7)], "ssq": [("ss", 6)], "rnT": [("rnT", 6)], "rx": [("rx", 6)],
    "tr_ab": [("tr_a", 6), ("tr_b", 7)], "tr_k": [("tr_k", 6)], "bonus": [("bonus", 7)], "tr_v": [("tr_v", 6), ("vt", 7)],
    "sc_a": [("sc00", 6), ("sc10", 7)], "sc_b": [("sc01", 6), ("sc11", 7)],
    "pt_a": [("pt00", 6), ("pt10", 7)], "pt_b": [("pt01", 6), ("pt11", 7)], "o_a": [("o", 6)], "oT": [("oT", 7)],
    "lab": [("lab0", 0), ("lab1", 1)], "lak": [("lak0", 4), ("lak1", 5)],
    "mrb": [("mrb0", 0), ("mrb1", 1)], "mrk": [("mrk0", 4), ("mrk1", 5)],
    "xt": [("xt0", 0), ("xt1", 1)], "lv": [("lv", 4)],
    "wg": [("wg0", 2), ("wg1", 3)], "rq": [("rq", 0)], "c_a": [("c0", 4)], "c": [("c1", 5)],
    "res": [("res_a", 6), ("res_b", 7)],
    "st0": [("st0", 2)], "st1": [("st1", 2)], "yy0": [("yy", 3)], "gate": [("gate", 7)], "outT": [("outT", 7)],
}
for _k in range(1, LEVELS):
    MAKES[f"y{_k}"] = [(f"y{_g}_{_k}", _g) for _g in range(2)]
    MAKES[f"tx{_k}"] = [(f"tx{_g}_{_k}", 4 + _g) for _g in range(2)]
    MAKES[f"z{_k}"] = [(f"z{_g}_{_k}", 2 + _g) for _g in range(2)]
del MAKES["tx1"]
BANK = {name: b for makes in MAKES.values() for name, b in makes}
BANK_USES = {b: [(name, t) for step, t in ORDER for name, to in MAKES.get(step, ()) if to == b] for b in range(8)}
USE = {use: i for uses in BANK_USES.values() for i, use in enumerate(uses)}

READER = {
    "lora_w": ("xw0", 1, 1), "lora_a": ("aa0", 1, 1), "ss": ("ssm", 1, 1), "rnT": ("rnT", 1, 1), "rx": ("kk", 1, 1),
    "bonus": ("bonus", 1, 1), "res_a": ("res", 2, 1), "res_b": ("res", 2, 2),
    "tr_a": ("A_tok", 1, 1), "tr_b": ("B_tok", 1, 1), "tr_k": ("K_tok", 1, 1), "tr_v": ("V_tok", 1, 1),
    "vt": ("va_tok", 1, 1), "o": ("o", 1, 1), "oT": ("oT", 1, 1), "lv": ("LV", 1, 1), "wg0": ("WG0", 1, 1),
    "wg1": ("WG1", 1, 1), "rq": ("QT", 1, 1), "yy": ("yc", 1, 1), "gate": ("yn5", 1, 1), "outT": ("rw", 1, 1),
}
for _i, _n in enumerate(("00", "10", "01", "11")):
    READER["sc" + _n] = ("sc", 8, 2 * _i + 2)
    READER["pt" + _n] = ("pT", 4, _i + 1)
for _g in range(2):
    READER[f"lab{_g}"] = ("LT", 2, _g + 1)
    READER[f"lak{_g}"] = ("LakT", 2, _g + 1)
    READER[f"mrb{_g}"] = ("MrbT", 2, _g + 1)
    READER[f"mrk{_g}"] = ("MrkR", 2, _g + 1)
    READER[f"xt{_g}"] = ("X", 2 * (LEVELS - 1), _g + 1)
    READER[f"c{_g}"] = ("phi", 4, 2 * _g + 2)
    READER[f"st{_g}"] = ("state", 2, _g + 1)
    for _k in range(1, LEVELS):
        READER[f"y{_g}_{_k}"] = ("IY", 2 * (LEVELS - 1), 2 * (_k - 1) + _g + 1)
        READER[f"z{_g}_{_k}"] = ("X", 2 * (LEVELS - 1), 2 * _k + _g + 1)
        READER[f"tx{_g}_{_k}"] = ("XT", 2 * (LEVELS - 1), 2 * (_k - 2) + _g + 1)
    READER[f"z{_g}_{LEVELS - 1}"] = ("XT", 2 * (LEVELS - 1), 2 * (LEVELS - 2) + _g + 1)



TURNS = [(i, 0) for i in range(4)] + [(i, 1) for i in range(4)] + [(i, j) for i in range(4, TILES) for j in range(2)]
TURN_BANKS = 7


def build(nc, x, w_all, vec, sinks, w2a2, g2, ln_w, ln_b, out):
    with ExitStack() as ctx:
        def sb(name, shape, dt=F32):
            return ctx.enter_context(nc.sbuf_tensor(name, shape, dt))

        vecs = sb("vecs", [P, N_VEC])
        ident = sb("ident", [P, P])
        ones = sb("ones", [P, P])
        w_raw = [sb(f"w_raw{i}", [P, KT, P]) for i in range(2)]
        neg_half = sb("neg_half", [P, 8])
        BASE = -(-nc.sbuf_base // 64) * 64
        TOP = nc.sbuf_usable_end // 64 * 64
        KB4 = 4 * SEQ

        class Region:

            def __init__(self, base, end=TOP):
                self.at, self.end = base, end

            def __call__(self, name, shape, dt=F32):
                t = nc.alloc_sbuf_tensor_at(name, shape, dt, offset=self.at)
                self.at += -(-4 * math.prod(shape[1:]) // 32) * 32
                assert self.at <= self.end, (name, self.at, self.end)
                return t

        r = Region(TOP - 4 * KB4)
        w_hi = [r(f"w_hi{i}", [P, KT, P], F32R) for i in range(2)]
        w_lo = [r(f"w_lo{i}", [P, KT, P], F32R) for i in range(2)]
        W_AT = TOP - 4 * KB4

        r = Region(BASE)
        zT = r("zT", [P, N_IN, SEQ])
        w2a2_s = r("w2a2_s", [P, 512])
        g2_s = r("g2_s", [P, 512])
        lnw_s = r("lnw_s", [P, 512])
        lnb_s = r("lnb_s", [P, 512])
        strict = r("strict", [P, P])
        incl = r("incl", [P, P])
        level = [r(f"level{k}", [P, P]) for k in range(LEVELS)]
        dist = r("dist", [P, 2 * P])
        pair_sel = r("pair_sel", [P, 2])
        head_up = r("head_up", [P, 512])
        ident64 = r("ident64", [P, HEAD])
        rk_w = r("rk_w", [P, PAIRS, 2])
        keep = r("keep", [P, 512])
        sink_s = r("sink_s", [P, HEADS])

        tw = r("tw", [P, P])
        pm = [r(f"pm{i}", [P, 2 * PAIRS]) for i in range(2)]
        pe_ = [r(f"pe{i}", [P, 2 * PAIRS]) for i in range(2)]
        pc = [r(f"pc{i}", [P, 2 * PAIRS]) for i in range(2)]
        rn8 = r("rn8", [P, HEADS])
        CONST_END = r.at

        r = Region(CONST_END, W_AT)
        xs = [r(f"xs{i}", [P, D]) for i in range(2)]
        z_tmp = [r(f"z_tmp{i}", [P, 1 + SEQ]) for i in range(2)]
        rs1b = r("rs1b", [P, SEQ])
        h_raw = [rs1b[:, j * HALF:(j + 1) * HALF].rearrange("p (k t) -> p k t", t=P) for j in range(2)]
        ss1 = r("ss1", [P, TILES])
        h_hi = r("h_hi", [P, KT, SEQ], F32R)
        h_lo = r("h_lo", [P, KT, SEQ], F32R)

        r = Region(CONST_END, CONST_END + 4 * KB4)
        block = [P, PAIRS, P]
        toks = [P, HEADS, HEAD]
        xw, aa, kk, cs, dm, e1, e2, k2 = (r(n, block) for n in ("xw", "aa", "kk", "cs", "dm", "e1", "e2", "k2"))
        rn_T = k2[0:HEADS, 0, :]
        r = Region(r.at)
        mx, nm, es, sums, den = (r(n, [P, HEADS]) for n in ("mx", "nm", "es", "sums", "den"))
        mu8, var8, rstd8 = (r(n, [P, HEADS]) for n in ("mu8", "var8", "rstd8"))
        bonus = [r(f"bonus{i}", [P, HEADS]) for i in range(2)]
        assert r.at <= BASE + 29 * KB4
        B_tok = [r(f"B_tok{i}", toks) for i in range(2)]
        K_tok = [r(f"K_tok{i}", toks) for i in range(2)]
        sc = [r(f"sc{i}", [P, 2, 2 * P]) for i in range(4)]
        X = [r(f"X{i}", block) for i in range(2)]
        XT = [r(f"XT{i}", block) for i in range(2)]
        rq = r("rq", block)
        va_tok = [r(f"va_tok{i}", [P, P]) for i in range(2)]
        assert r.at >= BASE + (29 + 2 * EARLY) * KB4
        A_LV = r("A_LV", [P, 3, HEADS, HEAD])
        A_tok, LV = [A_LV[:, i] for i in range(2)], A_LV[:, 2]
        QT = A_LV[:, 2].rearrange("p h d -> p (h d)").rearrange("p (a t) -> p a t", t=P)
        V_tok = [r(f"V_tok{i}", toks) for i in range(2)]
        gs = [r(f"gs{i}", [P, P]) for i in range(2)]
        MrbT = [r(f"MrbT{i}", block) for i in range(2)]
        MrkT = [r(f"MrkT{i}", block) for i in range(2)]
        WG = r("WG", [P, HEADS, 2, HEAD])
        W_s, G_s = WG[:, :, 0, :], WG[:, :, 1, :]
        phi = [r(f"phi{i}", block) for i in range(2)]
        psi = [r(f"psi{i}", block) for i in range(2)]
        state = [r(f"state{i}", block) for i in range(2)]
        yc, y_sq, bv = r("yc", block), r("y_sq", block), r("bv", toks)
        assert r.at <= W_AT
        r = Region(W_AT)
        at, rt, bt, kt = (r(n, block) for n in ("at", "rt", "bt", "kt"))
        LT = [r(f"LT{i}", block) for i in range(2)]
        LakT = [r(f"LakT{i}", block) for i in range(2)]
        IY = LakT
        diag = X[0][:].rearrange("p a b -> p (a b)").rearrange("p (h d) -> p h d", d=HEAD)

        r = Region(BASE)
        u_r = [r(f"u_r{i}", [P, SEQ]) for i in range(2)]
        u_f = [r(f"u_f{i}", [P, SEQ]) for i in range(2)]
        x2 = r("x2", [P, KT, SEQ])
        xs3 = [nc.alloc_sbuf_tensor_at(f"xs3_{i}", [P, D], F32, offset=r.at + i * KB4) for i in range(2)]
        acc3 = r("acc3", [P, SEQ])
        assert r.at == BASE + RG * KB4
        n_hi = r("n_hi", [P, KT, SEQ], F32R)
        n_lo = r("n_lo", [P, KT, SEQ], F32R)
        u_parts = r("u_parts", [P, KT, 2, SEQ], F32R)
        u_hi, u_lo = u_parts[:, :, 0, :], u_parts[:, :, 1, :]
        rs8 = r("rs8", [P, TILES])
        assert r.at <= W_AT
        rs3b = acc3
        sq3, h3 = u_r, u_f
        o_s = [nc.alloc_sbuf_tensor_at(f"o_s{i}", [P, D], F32, offset=BASE + (RG + i) * KB4) for i in range(TILES)]

        ps = [ctx.enter_context(nc.psum_tensor(f"bank{i}", [P, 512], F32)) for i in range(8)]

        def sem(name):
            return ctx.enter_context(nc.semaphore(name))

        consts_in = sem("consts_in")
        w_in = [sem(f"w_in{i}") for i in range(2)]
        w_hi_ok, w_lo_ok = sem("w_hi_ok"), sem("w_lo_ok")
        proj_full = sem("proj_full")
        act_read, dve_read = sem("act_read"), sem("dve_read")
        x_in = [sem(f"x_in{i}") for i in range(2)]
        x_sq, tr_full = sem("x_sq"), sem("tr_full")
        rs_mean, rs_root, rs_diag, rs_full, rs_ok = (
            sem(n) for n in ("rs_mean", "rs_root", "rs_diag", "rs_full", "rs_ok"))
        h_raw_ok, h_hi_ok = sem("h_raw_ok"), sem("h_hi_ok")
        h_lo_ok, h_lo_v = sem("h_lo_ok"), sem("h_lo_v")
        masks_ok, mask_step = sem("masks_ok"), sem("mask_step")
        z_zero, z_copied, z_diff, z_ok = sem("z_zero"), sem("z_copied"), sem("z_diff"), sem("z_ok")
        bank_full = [sem(f"bank_full{b}") for b in range(8)]
        NAMES = """tw gs gg xw0 aa0 xw1 aa1 xw2 aa2 cs dm dp dpe pm pe e1 e2 pc kx ksq ssm rn rnT kk t2 k2 at kka bt kt
            rt rk ah bh kh A_tok B_tok K_tok V_tok bonus va_tok sc mx m nm dsink es p den rden pT o oT
            LT LI0 LI1 MrbT LakT MrkR MrkT XT1_0 XT1_1 XT X IY LV WG0 WG1 rq QT diag phi psi state
            mu yc ysq var rs rstd yn1 yn2 yn3 bv bvb yn5 rw zero res""".split()
        done = {n: sem("s_" + n) for n in NAMES}
        o_hi_ok, o_lo_ok, o_lo_v = sem("o_hi_ok"), sem("o_lo_ok"), sem("o_lo_v")
        n_hi_ok, n_lo_ok = sem("n_hi_ok"), sem("n_lo_ok")
        u_hi_ok, u_lo_ok = sem("u_hi_ok"), sem("u_lo_ok")
        x2_sq, x2_acc = sem("x2_sq"), sem("x2_acc")
        ss3_full, h3_raw = sem("ss3_full"), sem("h3_raw")
        u_scaled, u_sq = sem("u_scaled"), sem("u_sq")
        fin_sq, fin_acc, fin_gain, fin_ss, fin_v, fin_a, out_sent = (
            sem(n) for n in ("fin_sq", "fin_acc", "fin_gain", "fin_ss", "fin_v", "fin_a", "out_sent"))

        xv = x.rearrange("b (t p) d -> p (b t) d", p=P)
        ov = out.rearrange("b (t p) d -> p (b t) d", p=P)
        U_UP = N_IN + N_OUT

        def bank(name):
            return ps[BANK[name]]

        def wait_read(pe, name, t):
            key, each, i = READER[name]
            pe.wait_ge(done[key], each * t + i)

        def wait_bank(pe, name, t):
            i = USE[name, t]
            if i:
                wait_read(pe, *BANK_USES[BANK[name]][i - 1])

        def wait_full(eng, name, t):
            eng.wait_ge(bank_full[BANK[name]], USE[name, t] + 1)

        def filled(name):
            return bank_full[BANK[name]]

        def tile(t):
            return slice(t * P, (t + 1) * P)

        def slot(g, i):
            return 2 * (2 * (g // 2) + i) + g % 2

        def halves(ap, g):
            return ap[HEAD * g:HEAD * (g + 1)]

        def per_chunk(ap):
            return ap.rearrange("p a (c t) -> p (a c) t", c=CHUNKS)

        def spread(ap, n):
            return ap.unsqueeze(2).to_broadcast([P, ap.shape[1], n])

        def across(ap, m):
            return ap.unsqueeze(1).to_broadcast([ap.shape[0], m, ap.shape[1]])

        def view(ap, m):
            return ap.rearrange("p (m n) -> p m n", m=m)

        def mixed(k):
            return zT[:, Q0 + k if k < PAIRS else R0 + k - PAIRS, :]

        def run(steps):
            for step, t in ORDER:
                if step in steps:
                    steps[step](t)

        block_ = ctx.enter_context(nc.Block())

        @block_.sync
        def _(sp):
            sp.dma_start(vecs[:], vec).then_inc(consts_in, 16)

            def load_x(i):
                if i >= 2:
                    sp.wait_ge(tr_full, 2 * (i - 1))
                    sp.wait_ge(x_sq, i - 1)
                sp.dma_start(xs[i % 2][:], xv[:, i, :]).then_inc(x_in[i % 2], 16)

            for i in range(2):
                load_x(i)
            for p in range(2):
                sp.dma_start(w_raw[p][:], w_all[p]).then_inc(w_in[p], 16)
            for i in range(2, TILES):
                load_x(i)
            for dst, src in ((w2a2_s, w2a2), (g2_s, g2), (lnw_s, ln_w.to_broadcast([P, 512])),
                             (lnb_s, ln_b.to_broadcast([P, 512])), (sink_s, sinks.to_broadcast([P, HEADS]))):
                sp.dma_start(dst[:], src).then_inc(consts_in, 16)

            def load_w(i):
                for p in range(2):
                    sp.wait_ge(w_hi_ok, 2 * i + p - 1)
                    sp.wait_ge(w_lo_ok, 2 * i + p - 1)
                    sp.dma_start(w_raw[p][:], w_all[2 * i + p]).then_inc(w_in[p], 16)

            with sp.Fori(1, N_IN // 2 + 1) as i:
                load_w(i)
            sp.wait_ge(done["V_tok"], TILES)
            sp.wait_ge(done["gs"], TILES)
            for i in range(TILES):
                if i >= 2:
                    wait_full(sp, "res_b", i - 2)
                sp.dma_start(xs3[i % 2][:], xv[:, i, :]).then_inc(x_in[i % 2], 16)
            with sp.Fori(N_IN // 2 + 1, UNITS // 2) as i:
                load_w(i)
            for i in range(TILES):
                sp.wait_ge(fin_v, i + 1)
                sp.wait_ge(fin_a, i + 1)
                sp.dma_start(ov[:, i, :], o_s[i][:]).then_inc(out_sent, 16)
            sp.wait_ge(out_sent, 16 * TILES)

        @block_.scalar
        def _(act):
            def A(o, i, f=ACT.Copy, **kw):
                return nc.scalar.activation(o, i, f, **kw)

            def need(name, n):
                if n > 0:
                    act.wait_ge(done[name], n)

            def split_w(m, p, first=False):
                n = 2 * m + p
                act.wait_ge(w_in[p], 16 * m + 16)
                if not first:
                    act.wait_ge(proj_full, 2 * n - 2)
                    act.wait_ge(w_lo_ok, n - 1)
                A(w_hi[p][:], w_raw[p][:]).then_inc(w_hi_ok, 1)

            def h_high(i):
                for j in range(2):
                    act.wait_ge(h_raw_ok, 2 * i + j + 1)
                    A(h_hi[:, 4 * j:4 * j + 4, tile(i)], h_raw[j][:]).then_inc(h_hi_ok, 1)

            for i in range(TILES):
                act.wait_ge(x_in[i % 2], 16 * (i // 2 + 1))
                if i:
                    act.wait_ge(x_sq, i)
                A(z_tmp[0][:, 1:], xs[i % 2][:], ACT.Square, accum_out=ss1[:, i:i + 1]).then_inc(x_sq, 1)
                if i == 0:
                    split_w(0, 0, first=True)
                    split_w(0, 1, first=True)
                else:
                    h_high(i - 1)
            h_high(TILES - 1)


            with act.Fori(1, Q0 // 2) as i:
                for p in range(2):
                    split_w(i, p)
            split_w(Q0 // 2, 0)

            def proj(n):
                if n + 1 < N_IN:
                    split_w((n + 1) // 2, (n + 1) % 2)

            def mix(_):
                act.wait_ge(dve_read, 2 * N_IN)

            def shifted(_):
                act.wait_ge(z_ok, N_SHIFT)
                act.wait_ge(consts_in, 96)

            def tanh(t):
                if t:
                    wait_full(act, "lora_w", t - 1)
                A(tw[0:64], zT[0:64, RWA, tile(t)], ACT.Tanh).then_inc(done["tw"], 1)

            def lora(t):
                need("kx", t + 1)
                need("kt", t)
                need("rk", t)
                A(k2[:], kk[:], ACT.Square).then_inc(done["ksq"], 1)

            def gs_(t):
                if t > 1:
                    wait_full(act, "gate", t - 2)
                A(gs[t % 2][:], zT[:, RG, tile(t)], ACT.Tanh, scale=0.5).then_inc(done["gs"], 1)

            def sig(t):
                need("xw0", t + 1)
                A(xw[:], xw[:], ACT.Tanh, scale=0.5).then_inc(done["xw1"], 1)
                need("aa0", t + 1)
                A(aa[:], aa[:], ACT.Tanh, scale=0.5).then_inc(done["aa1"], 1)

            def norm_T(t):
                wait_full(act, "rnT", t)
                A(rn_T, bank("rnT")[0:HEADS, 0:P]).then_inc(done["rnT"], 1)

            def exps(t):
                b = t % 2
                need("cs", t + 1)
                A(pm[b][:], per_chunk(cs[:])[:, :, CHUNK // 2 - 1], ACT.Exp, scale=-LOG_DECAY).then_inc(done["pm"], 1)
                need("dm", t + 1)
                A(pe_[b][:], per_chunk(dm[:])[:, :, CHUNK - 1], ACT.Exp, scale=-LOG_DECAY).then_inc(done["pe"], 1)
                if t:
                    wait_full(act, "tr_k", t - 1)
                    wait_full(act, "bonus", t - 1)
                A(e2[:], dm[:], ACT.Exp, scale=LOG_DECAY).then_inc(done["e2"], 1)
                A(e1[:], dm[:], ACT.Exp, scale=-LOG_DECAY).then_inc(done["e1"], 1)

            def dpe(t):
                need("dp", t + 1)
                A(xw[:], xw[:], ACT.Exp, scale=-LOG_DECAY).then_inc(done["dpe"], 1)

            def tr_ab(t):
                for name, dst, key in (("tr_a", A_tok, "A_tok"), ("tr_b", B_tok, "B_tok")):
                    wait_full(act, name, t)
                    A(dst[t % 2][:], view(bank(name)[:], HEADS)).then_inc(done[key], 1)

            def tr_k(t):
                wait_full(act, "tr_k", t)
                A(K_tok[t % 2][:], view(bank("tr_k")[:], HEADS)).then_inc(done["K_tok"], 1)

            def bonus_(t):
                if t > 1:
                    need("bv", t - 1)
                wait_full(act, "bonus", t)
                A(bonus[t % 2][:], bank("bonus")[:, 0:HEADS]).then_inc(done["bonus"], 1)

            def tr_v(t):
                b = t % 2
                if t > 1:
                    need("bv", t - 1)
                wait_full(act, "tr_v", t)
                A(V_tok[b][:], view(bank("tr_v")[:], HEADS)).then_inc(done["V_tok"], 1)
                wait_full(act, "vt", t)
                if t:
                    wait_full(act, "o", t - 1)
                A(va_tok[b][:], bank("vt")[:, 0:P]).then_inc(done["va_tok"], 1)

            def probs(t):
                lo = P if t == 0 else 0
                need("dsink", t + 1)
                A(es[:], es[:], ACT.Exp).then_inc(done["es"], 1)
                need("nm", t + 1)
                need("den", t)
                for g in range(4):
                    for i in range(2):
                        c = slot(g, i)
                        A(sc[g][:, i, lo:], sc[g][:, i, lo:], ACT.Exp, bias=nm[:, c:c + 1], scale=SCALE,
                          accum_out=sums[:, c:c + 1]).then_inc(done["p"], 1)

            def probs_T(groups):
                def turned_back(t):
                    first, by = (1, 2) if t == 0 else (0, 1)
                    for g, name in groups:
                        wait_full(act, name, t)
                        A(view(sc[g][:].rearrange("p a b -> p (a b)"), 4)[:, first::by, :],
                          view(bank(name)[:], 4)[:, first::by, :]).then_inc(done["pT"], 1)
                return turned_back

            def o_T(t):
                wait_full(act, "oT", t)
                A(zT[:, Q0:Q0 + PAIRS, tile(t)], view(bank("oT")[:], PAIRS)).then_inc(done["oT"], 1)

            def mrk(t):
                wait_full(act, "mrk0", t)
                if t:
                    wait_full(act, "yy", t - 1)
                for g in range(2):
                    wait_full(act, f"mrk{g}", t)
                    A(MrkT[g][:], view(bank(f"mrk{g}")[:], PAIRS)).then_inc(done["MrkR"], 1)

            def xt(t):
                need("phi", 4 * t)
                for g in range(2):
                    wait_full(act, f"xt{g}", t)
                    A(X[g][:], view(bank(f"xt{g}")[:], PAIRS)).then_inc(done["X"], 1)

            def lv(t):
                wait_full(act, "lv", t)
                A(LV, view(bank("lv")[:], HEADS)).then_inc(done["LV"], 1)

            def tx(k):
                def turned(t):
                    for g in range(2):
                        wait_full(act, f"tx{g}_{k}", t)
                        A(XT[g][:], view(bank(f"tx{g}_{k}")[:], PAIRS)).then_inc(done["XT"], 1)
                return turned

            def z(k):
                dst, key = (XT, "XT") if k == LEVELS - 1 else (X, "X")

                def level_z(t):
                    for g in range(2):
                        wait_full(act, f"z{g}_{k}", t)
                        A(dst[g][:], view(bank(f"z{g}_{k}")[:], PAIRS)).then_inc(done[key], 1)
                return level_z

            def wg(t):
                wait_full(act, "wg0", t)
                A(WG[:, 0:PAIRS], view(bank("wg0")[:], PAIRS).rearrange("p h (s d) -> p h s d", s=2))\
                    .then_inc(done["WG0"], 1)

            def c_(t):
                need("zero", 1)
                need("state", 2 * t)
                for c in range(CHUNKS):
                    wait_full(act, f"c{c}", t)
                    for g in range(2):
                        src = halves(view(bank(f"c{c}")[:], PAIRS), g)[:, :, HEAD:]
                        A(halves(psi[c], g)[:, :, HEAD * g:HEAD * (g + 1)], src).then_inc(done["psi"], 1)

            def ysq(t):
                need("yc", t + 1)
                need("var", t)
                A(y_sq[:], yc[:], ACT.Square).then_inc(done["ysq"], 1)

            def out_T(t):
                wait_full(act, "outT", t)
                A(zT[:, R0:R0 + PAIRS, tile(t)], view(bank("outT")[:], PAIRS)).then_inc(done["rw"], 1)

            def split_mixed(k):
                A(u_hi[:, k, :], mixed(k)).then_inc(o_hi_ok, 1)

            def split_a(_):
                wait_full(act, "st0", TILES - 1)
                need("phi", 4 * TILES)
                need("oT", TILES)
                split_w(N_IN // 2, 0)
                for k in range(EARLY):
                    split_mixed(k)

            def out_b(_):
                need("rw", TILES)
                need("state", 2 * TILES)
                for k in range(EARLY, KT):
                    split_mixed(k)
                    if k == PAIRS:
                        split_w(N_IN // 2, 1)

            run({"proj": proj, "shifted": shifted, "mix": mix, "split_a": split_a, "out_b": out_b,
                 "tanh": tanh, "lora": lora, "gs": gs_, "sig": sig, "rnT": norm_T, "exps": exps, "dpe": dpe,
                 "tr_ab": tr_ab, "tr_k": tr_k, "tr_v": tr_v, "bonus": bonus_, "p": probs, "oT": o_T, "mrk_e": mrk, "xt": xt,
                 "pt_a": probs_T([(0, "pt00"), (1, "pt10")]), "pt_b": probs_T([(2, "pt01"), (3, "pt11")]),
                 "lv": lv, "wg": wg, "c": c_, "ysq": ysq, "outT": out_T}
                | {f"z{k}": z(k) for k in range(1, LEVELS)} | {f"tx{k}": tx(k) for k in range(2, LEVELS)})

            for j in range(N_OUT):
                act.wait_ge(dve_read, 2 * (N_IN + j) + 2)
                if j >= 2:
                    act.wait_ge(n_lo_ok, j - 1)
                A(h3[j % 2][:], x2[:, j, :], scale=vecs[:, C_G2 + j:C_G2 + j + 1]).then_inc(h3_raw, 1)
                act.wait_ge(h3_raw, j + 1)
                A(n_hi[:, j, :], h3[j % 2][:]).then_inc(n_hi_ok, 1)
                if j >= 2:
                    act.wait_ge(x2_acc, j - 1)
                A(sq3[j % 2][:], x2[:, j, :], ACT.Square).then_inc(x2_sq, 1)
                n = N_IN + j + 2
                split_w(n // 2, n % 2)

            def inside(g, i, first=False):
                for p in range(2):
                    e = 8 * g + 2 * i + p
                    if first and p == 0:
                        act.wait_ge(x2_acc, N_OUT)
                    elif first:
                        act.wait_ge(rs_full, 4)
                    for h in range(2):
                        act.wait_ge(proj_full, 2 * (U_UP + 16 * g + 2 * i + p) + h + 1)
                        A(u_r[p][:, h * HALF:(h + 1) * HALF], ps[2 * p + h][:], ACT.Relu).then_inc(act_read, 1)
                    split_w(U_UP // 2 + 8 * g + i + 1, p)
                    act.wait_ge(u_scaled, e + 1)
                    if first:
                        act.wait_ge(n_lo_ok, KT)
                    else:
                        act.wait_ge(u_lo_ok, e - 1)
                    A(u_f[p][:], u_r[p][:], ACT.Square).then_inc(u_sq, 1)
                    act.wait_ge(u_sq, e + 1)
                    A(u_hi[:, bass.ds(2 * i + p, 1), :], u_f[p][:]).then_inc(u_hi_ok, 1)

            def group(g, first=False, last=False):
                if first:
                    inside(0, 0, first=True)
                with act.Fori(1 if first else 0, 4) as i:
                    inside(g, i)
                m = U_UP // 2 + 8 * g + 4
                if not last:
                    with act.Fori(0, 4) as i:
                        for p in range(2):
                            split_w(m + i + 1, p)

            group(0, first=True)
            with act.Fori(1, GROUPS - 1) as g:
                group(g)
            group(GROUPS - 1, last=True)

            for j in range(KT):
                n = UNITS - KT + j
                if n + 2 < UNITS:
                    split_w((n + 2) // 2, n % 2)
                act.wait_ge(dve_read, 2 * (N_IN + N_OUT + 8 * GROUPS - KT + j) + 2)
                if j >= 2:
                    act.wait_ge(fin_acc, j - 1)
                A(u_r[j % 2][:], x2[:, j, :], ACT.Square).then_inc(fin_sq, 1)
                A(x2[:, j, :], x2[:, j, :], scale=vecs[:, C_GF + j:C_GF + j + 1]).then_inc(fin_gain, 1)
            act.wait_ge(rs_root, 3)
            for i in range(TILES):
                s = TURNS.index((i, 1))
                act.wait_ge(tr_full, 2 * TILES + s + 1)
                A(o_s[i][:, HALF:], ps[1 + s % TURN_BANKS][:], scale=rs8[:, i:i + 1]).then_inc(fin_a, 1)

        @block_.gpsimd
        def _(pool):
            G = nc.gpsimd
            steps = [0]

            def step(ins):
                steps[0] += 1
                ins.then_inc(mask_step, 1)
                pool.wait_ge(mask_step, steps[0])

            def select(ap, pattern, base, mult, fill, op=ALU.is_ge):
                step(G.affine_select(out=ap, in_=ap, compare_op=op, fill=fill, base=base, pattern=pattern,
                                     channel_multiplier=mult))

            step(G.memset(ident[:], 0.0))
            select(ident[:], [[-1, P]], 0, 1, 1.0, ALU.not_equal)
            step(G.memset(ones[:], 1.0))
            step(G.memset(neg_half[:], -0.5))
            for p in range(2):
                G.memset(z_tmp[p][:, 0:1], 0.0).then_inc(z_zero, 1)

            def low_h(i):
                pool.wait_ge(h_hi_ok, 2 * i + 1)
                G.tensor_tensor(h_lo[:, 0:4, tile(i)], h_raw[0][:], h_hi[:, 0:4, tile(i)].bitcast(F32), ALU.subtract)\
                    .then_inc(h_lo_ok, 1)

            def split_w(m, p):
                pool.wait_ge(w_hi_ok, 2 * m + p + 1)
                G.tensor_tensor(w_lo[p][:], w_raw[p][:], w_hi[p][:].bitcast(F32), ALU.subtract).then_inc(w_lo_ok, 1)

            def chunk_masks():
                for mask, first in ((strict, -1), (incl, 0)):
                    step(G.memset(mask[:], 1.0))
                    select(view(mask[:], CHUNKS), [[CHUNK, CHUNKS], [1, CHUNK]], first, -1, 0.0)
                    select(view(mask[:], CHUNKS), [[-CHUNK, CHUNKS], [0, CHUNK]], 0, 1, 0.0)
            def level_masks():
                for k in range(LEVELS):
                    w = 1 << k
                    mk = view(level[k][:], P // (2 * w))
                    rows, cols = (0, w) if k == 0 else (w, 0)
                    step(G.memset(level[k][:], 0.0))
                    step(G.memset(mk[:, :, cols:cols + w], 1.0))
                    select(mk, [[-2 * w, P // (2 * w)], [0, 2 * w]], -rows, 1, 0.0)
                    select(mk, [[2 * w, P // (2 * w)], [0, 2 * w]], rows + w - 1, -1, 0.0)
                    step(G.tensor_tensor(level[k][:], level[k][:], ident[:], ALU.add))
            def other_constants():
                step(G.iota(dist[:], pattern=[[-1, 2 * P]], base=P, channel_multiplier=1,
                            allow_small_or_imprecise_dtypes=True))
                select(dist[:], [[-1, 2 * P]], P, 1, FAR)
                select(dist[:], [[1, 2 * P]], -1, -1, FAR)
                step(G.memset(pair_sel[:], 0.0))
                for g in range(2):
                    step(G.memset(halves(pair_sel, g)[:, g:g + 1], 1.0))
                step(G.memset(head_up[:], 1.0))
                select(view(head_up[:], HEADS), [[-1, HEADS], [0, HEAD]], 0, 1, 0.0, ALU.is_equal)
                step(G.tensor_tensor(ident64[:], ident[:, 0:HEAD], ident[:, HEAD:P], ALU.add))
                step(G.memset(keep[:], 1.0))
                step(G.memset(view(keep[:], 2 * PAIRS)[:, :, 0:1], 0.0))
                step(G.memset(rk_w[:], 0.0))
                pool.wait_ge(consts_in, 96)
                for g in range(2):
                    G.tensor_copy(halves(rk_w, g)[:, :, g], halves(vecs, g)[:, C_RK:C_RK + PAIRS])\
                        .then_inc(masks_ok, 1)
                    pool.wait_ge(masks_ok, g + 1)


            chunk_masks()
            split_w(0, 0)
            split_w(0, 1)
            def root(ap, ready, n, out_sem):
                pool.wait_ge(ready, n)
                G.tensor_tensor(ap, ap, neg_half[:, 0:ap.shape[1]], ALU.pow).then_inc(out_sem, 1)

            for i in range(TILES):
                low_h(i)
            root(ss1[:], rs_mean, 1, rs_root)
            split_w(1, 0)
            level_masks()
            split_w(1, 1)
            other_constants()
            with pool.Fori(2, Q0 // 2) as i:
                for p in range(2):
                    split_w(i, p)
            split_w(Q0 // 2, 0)

            def need(name, n):
                if n > 0:
                    pool.wait_ge(done[name], n)

            def TT(o, a, b, op=ALU.mult):
                return G.tensor_tensor(o, a, b, op)

            def channels(c):
                return spread(vecs[:, c:c + PAIRS], P)

            def proj(n):
                if n + 1 < N_IN:
                    split_w((n + 1) // 2, (n + 1) % 2)

            def mix(_):
                pool.wait_ge(dve_read, 2 * N_IN)

            def zero(_):
                for i in range(2):
                    for tns in (phi[i], psi[i], state[i]):
                        o = G.memset(tns[:], 0.0)
                o.then_inc(done["zero"], 1)

            def shifted(_):
                pool.wait_ge(z_ok, N_SHIFT)

            def tanh(t):
                need("at", t)
                TT(kk[:], zT[:, RK0:RK0 + PAIRS, tile(t)], channels(C_KK)).then_inc(done["kx"], 1)

            def li(t):
                need("LT", 2 * t + 2)
                TT(LT[1][:], LT[1][:], across(ident[:], PAIRS), ALU.add).then_inc(done["LI1"], 1)
                need("LI1", t + 1)
                TT(XT[1][:], LT[1][:], across(level[0][:], PAIRS)).then_inc(done["XT1_1"], 1)
                need("QT", t)
                TT(per_chunk(rq[:]), per_chunk(rt[:]), spread(pm[t % 2][:], CHUNK)).then_inc(done["rq"], 1)

            def cum(t):
                need("ssm", t + 1)
                TT(rn8[:], rn8[:], neg_half[:], ALU.pow).then_inc(done["rn"], 1)
                need("aa1", t + 1)
                G.tensor_scalar(aa[:], aa[:], 0.5, 0.5, ALU.mult, ALU.add).then_inc(done["aa2"], 1)

            def gs_(t):
                need("gs", t + 1)
                G.tensor_scalar(gs[t % 2][:], gs[t % 2][:], 0.5, 0.5, ALU.mult, ALU.add).then_inc(done["gg"], 1)

            def exps(t):
                need("dm", t + 1)
                need("cs", t + 1)
                TT(xw[:], dm[:], xw[:], ALU.subtract).then_inc(done["dp"], 1)
                need("pm", t + 1)
                need("pe", t + 1)
                TT(pc[t % 2][:], pm[t % 2][:], pe_[t % 2][:]).then_inc(done["pc"], 1)

            def dpe(t):
                need("kk", t + 1)
                need("t2", t + 1)
                TT(aa[:], aa[:], kk[:]).then_inc(done["kka"], 1)

            def abk(t):
                need("kka", t + 1)
                need("e2", t + 1)
                if t:
                    wait_full(pool, "mrk1", t - 1)
                TT(bt[:], aa[:], e2[:]).then_inc(done["bt"], 1)
                need("e1", t + 1)
                TT(rt[:], zT[:, R0:R0 + PAIRS, tile(t)], e1[:]).then_inc(done["rt"], 1)

            def hats(t):
                need("rt", t + 1)
                need("k2", t + 1)
                TT(e1[:], zT[:, R0:R0 + PAIRS, tile(t)], k2[:]).then_inc(done["rk"], 1)
                need("bt", t + 1)
                need("pe", t + 1)
                TT(per_chunk(dm[:]), per_chunk(bt[:]), spread(pe_[t % 2][:], CHUNK)).then_inc(done["bh"], 1)

            def mrk_m(t):
                for g in range(2):
                    need("MrkR", 2 * t + g + 1)
                    TT(MrkT[g][:], MrkT[g][:], across(incl[:], PAIRS)).then_inc(done["MrkT"], 1)

            def z5(t):
                wait_full(pool, f"tx0_{LEVELS - 1}", t)
                need("pc", t + 1)
                TT(diag, across(ident64[:], 2 * PAIRS), spread(pc[t % 2][:], HEAD)).then_inc(done["diag"], 1)

            def bv_(t):
                need("V_tok", t + 1)
                need("bonus", t + 1)
                need("yn3", t)
                TT(bv[:], V_tok[t % 2][:], spread(bonus[t % 2][:], HEAD)).then_inc(done["bv"], 1)
                need("bv", t + 1)
                TT(bv[:], bv[:], view(lnb_s[:], HEADS), ALU.add).then_inc(done["bvb"], 1)

            def var(t):
                need("rs", t + 1)
                TT(rstd8[:], var8[:], neg_half[:], ALU.pow).then_inc(done["rstd"], 1)

            def low_part(k):
                pool.wait_ge(o_hi_ok, k + 1)
                TT(u_lo[:, k, :], mixed(k), u_hi[:, k, :].bitcast(F32), ALU.subtract).then_inc(o_lo_ok, 1)

            def split_a(_):
                split_w(N_IN // 2, 0)
                low_part(0)

            def out_b(_):
                for k in LOW_POOL[1:]:
                    low_part(k)
                    if k == PAIRS:
                        split_w(N_IN // 2, 1)

            run({"proj": proj, "shifted": shifted, "mix": mix, "zero": zero, "split_a": split_a, "out_b": out_b,
                 "tanh": tanh, "li": li, "cum": cum, "gs": gs_, "exps": exps, "dpe": dpe, "abk": abk, "hats": hats,
                 "mrk_m": mrk_m, f"z{LEVELS - 1}": z5, "bv": bv_, "var": var})

            for j in range(N_OUT):
                pool.wait_ge(n_hi_ok, j + 1)
                TT(n_lo[:, j, :], h3[j % 2][:], n_hi[:, j, :].bitcast(F32), ALU.subtract).then_inc(n_lo_ok, 1)
                n = N_IN + j + 2
                split_w(n // 2, n % 2)
            root(rs8[:], rs_mean, 2, rs_root)

            def group(g, last=False):
                with pool.Fori(0, 4) as i:
                    for p in range(2):
                        split_w(U_UP // 2 + 8 * g + i + 1, p)
                        pool.wait_ge(u_hi_ok, 8 * g + 2 * i + p + 1)
                        c = bass.ds(2 * i + p, 1)
                        TT(u_lo[:, c, :], u_f[p][:].unsqueeze(1), u_hi[:, c, :].bitcast(F32), ALU.subtract)\
                            .then_inc(u_lo_ok, 1)
                with pool.Fori(0, 3 if last else 4) as i:
                    for p in range(2):
                        split_w(U_UP // 2 + 8 * g + 4 + i + 1, p)

            with pool.Fori(0, GROUPS - 1) as g:
                group(g)
            group(GROUPS - 1, last=True)
            root(rs8[:], rs_mean, 3, rs_root)

        @block_.vector
        def _(dve):
            V = nc.vector

            def need(name, n):
                if n > 0:
                    dve.wait_ge(done[name], n)

            dve.wait_ge(consts_in, 16)
            def gain(i, j):
                n = 2 * i + j
                dve.wait_ge(tr_full, n + 1)
                V.tensor_tensor(h_raw[j][:], view(ps[4 + n % 4][:], 4),
                                spread(vecs[:, C_G1 + 4 * j:C_G1 + 4 * j + 4], P), ALU.mult).then_inc(h_raw_ok, 1)

            def low_h(i):
                dve.wait_ge(h_hi_ok, 2 * i + 2)
                V.tensor_tensor(h_lo[:, 4:8, tile(i)], h_raw[1][:], h_hi[:, 4:8, tile(i)].bitcast(F32), ALU.subtract)\
                    .then_inc(h_lo_v, 1)

            for i in range(TILES):
                if i:
                    dve.wait_ge(h_lo_ok, i)
                gain(i, 0)
                if i:
                    low_h(i - 1)
                    dve.wait_ge(h_lo_v, i)
                gain(i, 1)
            low_h(TILES - 1)

            def factors(n, sums, diagonal):
                V.tensor_scalar(sums[:], sums[:], 1.0 / D, RMS_EPS, ALU.mult, ALU.add).then_inc(rs_mean, 1)
                dve.wait_ge(rs_root, n)
                V.tensor_tensor(diagonal, across(ident[:], TILES), spread(sums[:], P), ALU.mult).then_inc(rs_diag, 1)

            def copy_factors(n, dst):
                for h in range(2):
                    dve.wait_ge(rs_full, 2 * n - 1 + h)
                    V.tensor_copy(dst[:, h * HALF:(h + 1) * HALF], ps[4 + h][:]).then_inc(rs_ok, 1)

            dve.wait_ge(x_sq, TILES)
            dve.wait_ge(tr_full, 2 * TILES)
            dve.wait_ge(mask_step, 2)
            factors(1, ss1, view(xs[0][:], TILES))
            dve.wait_ge(h_lo_ok, TILES)
            dve.wait_ge(h_lo_v, TILES)
            dve.wait_ge(h_hi_ok, 2 * TILES)
            copy_factors(1, rs1b)
            dve.wait_ge(rs_ok, 2)

            def proj(n):
                for h in range(2):
                    dve.wait_ge(proj_full, 2 * n + h + 1)
                    c = slice(h * HALF, (h + 1) * HALF)
                    V.tensor_tensor(zT[:, n, c], ps[2 * (n % 2) + h][:], rs1b[:, c], ALU.mult).then_inc(dve_read, 1)

            def shift(m):
                for p in range(2):
                    n = 2 * m + p
                    for h in range(2):
                        dve.wait_ge(proj_full, 2 * n + h + 1)
                        c = slice(h * HALF, (h + 1) * HALF)
                        V.tensor_tensor(z_tmp[p][:, 1 + h * HALF:1 + (h + 1) * HALF], ps[2 * p + h][:], rs1b[:, c],
                                        ALU.mult).then_inc(dve_read, 1)
                    zn = zT[:, bass.ds(n, 1), :]
                    before, now = z_tmp[p][:, 0:SEQ].unsqueeze(1), z_tmp[p][:, 1:].unsqueeze(1)
                    dve.wait_ge(dve_read, 2 * n + 2)
                    V.tensor_tensor(zn, before, now, ALU.subtract).then_inc(z_diff, 1)
                    dve.wait_ge(z_diff, n + 1)
                    V.scalar_tensor_tensor(out=zn, in0=zn, scalar=vecs[:, bass.ds(n + C_MU, 1)], in1=now,
                                           op0=ALU.mult, op1=ALU.add).then_inc(z_ok, 1)

            dve.wait_ge(z_zero, 2)
            with dve.Fori(0, N_SHIFT // 2) as i:
                shift(i)

            def TT(o, a, b, op=ALU.mult):
                return V.tensor_tensor(o, a, b, op)

            def channels(c):
                return spread(vecs[:, c:c + PAIRS], P)

            dve.wait_ge(z_ok, N_SHIFT)
            dve.wait_ge(consts_in, 96)
            dve.wait_ge(masks_ok, 2)

            def mix(_):
                dve.wait_ge(dve_read, 2 * N_IN)

            def lora(t):
                wait_full(dve, "lora_w", t)
                TT(xw[:], view(bank("lora_w")[:], PAIRS), channels(C_W0), ALU.add).then_inc(done["xw0"], 1)
                wait_full(dve, "lora_a", t)
                need("bt", t)
                TT(aa[:], view(bank("lora_a")[:], PAIRS), channels(C_A0), ALU.add).then_inc(done["aa0"], 1)

            def ssq(t):
                wait_full(dve, "ss", t)
                if t:
                    wait_full(dve, "rnT", t - 1)
                V.tensor_scalar(rn8[:], bank("ss")[:, 0:HEADS], L2_EPS ** 2, None, ALU.max).then_inc(done["ssm"], 1)

            def cum(t):
                need("xw1", t + 1)
                V.tensor_scalar(xw[:], xw[:], 0.5, 0.5, ALU.mult, ALU.add).then_inc(done["xw2"], 1)
                need("xw2", t + 1)
                if t:
                    wait_full(dve, "tr_a", t - 1)
                V.tensor_tensor_scan(cs[:].rearrange("p a b -> p (a b)"), keep[:], xw[:].rearrange("p a b -> p (a b)"),
                                     0.0, ALU.mult, ALU.add).then_inc(done["cs"], 1)

            def mid(t):
                need("cs", t + 1)
                if t:
                    wait_full(dve, "tr_b", t - 1)
                TT(per_chunk(dm[:]), per_chunk(cs[:]),
                   per_chunk(cs[:])[:, :, CHUNK // 2 - 1:CHUNK // 2].to_broadcast([P, 2 * PAIRS, CHUNK]), ALU.subtract)\
                    .then_inc(done["dm"], 1)

            def rx(t):
                need("kx", t + 1)
                wait_full(dve, "rx", t)
                TT(kk[:], kk[:], view(bank("rx")[:], PAIRS)).then_inc(done["kk"], 1)
                need("aa2", t + 1)
                V.scalar_tensor_tensor(out=k2[:], in0=aa[:], scalar=-1.0, in1=channels(C_KA),
                                       op0=ALU.add, op1=ALU.mult).then_inc(done["t2"], 1)
                need("t2", t + 1)
                V.scalar_tensor_tensor(out=k2[:], in0=k2[:], scalar=1.0, in1=zT[:, RK0:RK0 + PAIRS, tile(t)],
                                       op0=ALU.add, op1=ALU.mult).then_inc(done["k2"], 1)

            def abk(t):
                need("k2", t + 1)
                need("e2", t + 1)
                if t:
                    wait_full(dve, "mrk1", t - 1)
                TT(kt[:], k2[:], e2[:]).then_inc(done["kt"], 1)
                need("kk", t + 1)
                need("dpe", t + 1)
                V.scalar_tensor_tensor(out=at[:], in0=kk[:], scalar=-1.0, in1=xw[:],
                                       op0=ALU.mult, op1=ALU.mult).then_inc(done["at"], 1)

            def hats(t):
                b = t % 2
                need("at", t + 1)
                need("pm", t + 1)
                TT(per_chunk(cs[:]), per_chunk(at[:]), spread(pm[b][:], CHUNK)).then_inc(done["ah"], 1)
                need("kt", t + 1)
                need("pe", t + 1)
                need("bt", t + 1)
                TT(per_chunk(e2[:]), per_chunk(kt[:]), spread(pe_[b][:], CHUNK)).then_inc(done["kh"], 1)

            def scores(groups):
                def biased(t):
                    lo = P if t == 0 else 0
                    if t:
                        wait_full(dve, "oT", t - 1)
                    need("rden", t)
                    for g, name in groups:
                        wait_full(dve, name, t)
                        for i in range(2):
                            head = 2 * (g // 2) + i + PAIRS * (g % 2)
                            slope = 2.0 ** -(head + 1)
                            V.scalar_tensor_tensor(out=sc[g][:, i, lo:], in0=dist[:, lo:], scalar=-slope / SCALE,
                                                   in1=bank(name)[:, 2 * P * i + lo:2 * P * (i + 1)],
                                                   op0=ALU.mult, op1=ALU.add).then_inc(done["sc"], 1)
                        need("sc", 8 * t + 2 * g + 2)
                        V.tensor_reduce(mx[:, slot(g, 0):slot(g, 1) + 1:2], sc[g][:, :, lo:], AX.X, ALU.max)\
                            .then_inc(done["mx"], 1)
                return biased

            sc_b = scores([(2, "sc01"), (3, "sc11")])

            def sc_max(t):
                sc_b(t)
                need("mx", 4 * t + 4)
                V.scalar_tensor_tensor(out=mx[:], in0=mx[:], scalar=SCALE, in1=sink_s[:], op0=ALU.mult, op1=ALU.max)\
                    .then_inc(done["m"], 1)
                need("m", t + 1)
                TT(es[:], sink_s[:], mx[:], ALU.subtract).then_inc(done["dsink"], 1)
                need("p", 8 * t)
                V.tensor_scalar(nm[:], mx[:], -1.0, None, ALU.mult).then_inc(done["nm"], 1)

            def den_(t):
                need("es", t + 1)
                need("p", 8 * t + 8)
                TT(den[:], es[:], sums[:], ALU.add).then_inc(done["den"], 1)
                need("den", t + 1)
                V.reciprocal(den[:], den[:]).then_inc(done["rden"], 1)

            def o_(t):
                wait_full(dve, "o", t)
                need("rden", t + 1)
                TT(view(sc[0][:].rearrange("p a b -> p (a b)"), HEADS), view(bank("o")[:], HEADS), spread(den[:], HEAD))\
                    .then_inc(done["o"], 1)

            def masked(name, dst, mask, key):
                def evacuate(t):
                    if t and name == "mrb":
                        wait_full(dve, "yy", t - 1)
                    for g in range(2):
                        n = f"{name}{g}"
                        wait_full(dve, n, t)
                        TT(dst[g][:], view(bank(n)[:], PAIRS), across(mask[:], PAIRS)).then_inc(done[key], 1)
                return evacuate

            def li(t):
                need("LT", 2 * t + 1)
                TT(LT[0][:], LT[0][:], across(ident[:], PAIRS), ALU.add).then_inc(done["LI0"], 1)
                need("LI0", t + 1)
                TT(XT[0][:], LT[0][:], across(level[0][:], PAIRS)).then_inc(done["XT1_0"], 1)

            def y(k):
                def level_y(t):
                    for g in range(2):
                        n = f"y{g}_{k}"
                        wait_full(dve, n, t)
                        TT(IY[g][:], view(bank(n)[:], PAIRS), across(level[k][:], PAIRS)).then_inc(done["IY"], 1)
                return level_y

            def wg(t):
                wait_full(dve, "wg1", t)
                V.tensor_copy(WG[:, PAIRS:], view(bank("wg1")[:], PAIRS).rearrange("p h (s d) -> p h s d", s=2))\
                    .then_inc(done["WG1"], 1)

            def rq_(t):
                wait_full(dve, "rq", t)
                need("rq", t + 1)
                TT(QT[:], view(bank("rq")[:], PAIRS), rq[:], ALU.add).then_inc(done["QT"], 1)

            def c_(t):
                need("zero", 1)
                need("diag", t + 1)
                dg = diag.rearrange("p (a c) d -> p a c d", c=CHUNKS)
                for c in range(CHUNKS):
                    need("psi", 4 * t + 2 * c + 2)
                    for g in range(2):
                        TT(halves(phi[c], g)[:, :, HEAD * g:HEAD * (g + 1)],
                           halves(view(bank(f"c{c}")[:], PAIRS), g)[:, :, 0:HEAD], halves(dg, g)[:, :, c, :],
                           ALU.add).then_inc(done["phi"], 1)

            def advance(c):
                def new_state(t):
                    wait_full(dve, f"st{c}", t)
                    need("psi", 4 * t + 2 * c + 2)
                    if c:
                        wait_full(dve, "yy", t)
                    elif t:
                        wait_full(dve, "st1", t - 1)
                    TT(state[1 - c][:], view(bank(f"st{c}")[:], PAIRS), psi[c][:], ALU.add).then_inc(done["state"], 1)
                return new_state

            yh = view(yc[:].rearrange("p a b -> p (a b)"), HEADS)

            def mu_(t):
                wait_full(dve, "yy", t)
                V.tensor_reduce(mu8[:], view(bank("yy")[:], HEADS), AX.X, ALU.add).then_inc(done["mu"], 1)
                need("mu", t + 1)
                if t:
                    wait_full(dve, "outT", t - 1)
                V.scalar_tensor_tensor(out=yh, in0=spread(mu8[:], HEAD), scalar=-1.0 / HEAD,
                                       in1=view(bank("yy")[:], HEADS), op0=ALU.mult, op1=ALU.add).then_inc(done["yc"], 1)

            def var_(t):
                need("ysq", t + 1)
                V.tensor_reduce(var8[:], view(y_sq[:].rearrange("p a b -> p (a b)"), HEADS), AX.X, ALU.add)\
                    .then_inc(done["var"], 1)
                need("var", t + 1)
                V.tensor_scalar(var8[:], var8[:], 1.0 / HEAD, GN_EPS, ALU.mult, ALU.add).then_inc(done["rs"], 1)

            def yn(t):
                need("rstd", t + 1)
                TT(yh, yh, spread(rstd8[:], HEAD)).then_inc(done["yn1"], 1)
                need("yn1", t + 1)
                TT(yc[:], yc[:], view(lnw_s[:], PAIRS)).then_inc(done["yn2"], 1)

            def gate_(t):
                need("yn2", t + 1)
                need("bvb", t + 1)
                TT(yh, yh, bv[:], ALU.add).then_inc(done["yn3"], 1)
                need("yn3", t + 1)
                wait_full(dve, "gate", t)
                TT(yc[:], yc[:], view(bank("gate")[:], PAIRS)).then_inc(done["yn5"], 1)

            def residual(i):
                need("V_tok", TILES)
                for j, name in enumerate(("res_a", "res_b")):
                    wait_full(dve, name, i)
                    V.tensor_copy(x2[:, 4 * j:4 * j + 4, tile(i)], view(bank(name)[:], 4)).then_inc(done["res"], 1)

            def low_part(k):
                dve.wait_ge(o_hi_ok, k + 1)
                TT(u_lo[:, k, :], mixed(k), u_hi[:, k, :].bitcast(F32), ALU.subtract).then_inc(o_lo_v, 1)

            def split_a(_):
                for k in LOW_V:
                    if k < EARLY:
                        low_part(k)

            def out_b(_):
                for k in LOW_V:
                    if k >= EARLY:
                        low_part(k)

            run({"proj": proj, "mix": mix, "split_a": split_a, "out_b": out_b, "yg": gate_,
                 "lora": lora, "ssq": ssq, "cum": cum, "mid": mid, "rx": rx, "res": residual, "abk": abk, "hats": hats,
                 "sc_a": scores([(0, "sc00"), (1, "sc10")]), "sc_b": sc_max, "den": den_, "o": o_,
                 "lab": masked("lab", LT, strict, "LT"), "lak": masked("lak", LakT, strict, "LakT"),
                 "mrb_m": masked("mrb", MrbT, incl, "MrbT"), "li": li, "wg": wg, "rq": rq_, "c": c_,
                 "st0": advance(0), "st1": advance(1), "mu": mu_, "var": var_, "yn": yn}
                | {f"y{k}": y(k) for k in range(1, LEVELS)})

            need("res", 2 * TILES)
            for j in range(N_OUT):
                for h in range(2):
                    n = N_IN + j
                    dve.wait_ge(proj_full, 2 * n + h + 1)
                    o = x2[:, j, h * HALF:(h + 1) * HALF]
                    V.tensor_tensor(o, o, ps[2 * (n % 2) + h][:], ALU.add).then_inc(dve_read, 1)
                dve.wait_ge(x2_sq, j + 1)
                if j:
                    dve.wait_ge(x2_acc, j)
                    V.tensor_tensor(acc3[:], acc3[:], sq3[j % 2][:], ALU.add).then_inc(x2_acc, 1)
                else:
                    V.tensor_copy(acc3[:], sq3[0][:]).then_inc(x2_acc, 1)
            dve.wait_ge(ss3_full, 1)
            V.tensor_copy(rs8[:], ps[4][:, 0:TILES]).then_inc(ss3_full, 1)
            dve.wait_ge(ss3_full, 2)
            factors(2, rs8, view(sq3[1][:], TILES))
            copy_factors(2, rs3b)
            dve.wait_ge(rs_ok, 4)

            def up(g):
                with dve.Fori(0, 4) as i:
                    for p in range(2):
                        e = 8 * g + 2 * i + p
                        dve.wait_ge(act_read, 2 * e + 2)
                        V.tensor_tensor(u_r[p][:], u_r[p][:], rs3b[:], ALU.mult).then_inc(u_scaled, 1)

            def down(g):
                with dve.Fori(0, 4) as i:
                    for p in range(2):
                        n = U_UP + 16 * g + 8 + 2 * i + p
                        for h in range(2):
                            dve.wait_ge(proj_full, 2 * n + h + 1)
                            o = x2[:, bass.ds(2 * i + p, 1), h * HALF:(h + 1) * HALF]
                            V.tensor_tensor(o, o, ps[2 * p + h][:].unsqueeze(1), ALU.add)\
                                .then_inc(dve_read, 1)

            with dve.Fori(0, GROUPS - 1) as g:
                up(g)
                down(g)
            up(GROUPS - 1)
            for j in range(KT):
                n = UNITS - KT + j
                for h in range(2):
                    dve.wait_ge(proj_full, 2 * n + h + 1)
                    o = x2[:, j, h * HALF:(h + 1) * HALF]
                    V.tensor_tensor(o, o, ps[2 * (n % 2) + h][:], ALU.add).then_inc(dve_read, 1)
                dve.wait_ge(fin_sq, j + 1)
                if j:
                    dve.wait_ge(fin_acc, j)
                    V.tensor_tensor(acc3[:], acc3[:], u_r[j % 2][:], ALU.add).then_inc(fin_acc, 1)
                else:
                    V.tensor_copy(acc3[:], u_r[0][:]).then_inc(fin_acc, 1)
            dve.wait_ge(fin_ss, 1)
            V.tensor_scalar(rs8[:], ps[0][:, 0:TILES], 1.0 / D, RMS_EPS, ALU.mult, ALU.add).then_inc(rs_mean, 1)
            dve.wait_ge(rs_root, 3)
            for i in range(TILES):
                s = TURNS.index((i, 0))
                dve.wait_ge(tr_full, 2 * TILES + s + 1)
                V.tensor_scalar(o_s[i][:, 0:HALF], ps[1 + s % TURN_BANKS][:], rs8[:, i:i + 1], None, ALU.mult)\
                    .then_inc(fin_v, 1)

        @block_.tensor
        def _(pe):
            M = nc.tensor.matmul

            def need(name, n):
                if n > 0:
                    pe.wait_ge(done[name], n)

            def turn(source, i):
                for j in range(2):
                    f = 2 * i + j
                    if f >= 4:
                        pe.wait_ge(h_raw_ok, f - 3)
                    for k in range(4):
                        o = nc.tensor.transpose(ps[4 + f % 4][:, k * P:(k + 1) * P], source(4 * j + k), ident[:])
                    o.then_inc(tr_full, 1)

            def unit(m, p, hi, lo, ready=lambda k: None, parts=((0, 1),), blocks=range(KT)):
                n = 2 * m + p
                pe.wait_ge(w_hi_ok, n + 1)
                pe.wait_ge(w_lo_ok, n + 1)
                for part in parts:
                    for k in blocks:
                        ready(k if len(part) == 2 else (k, part[0]))
                        for s, (w, a) in enumerate(((w_hi, hi), (w_hi, lo), (w_lo, hi))):
                            for h in part:
                                o = M(ps[2 * p + h][:], w[p][:, k, :], a[:, k, h * HALF:(h + 1) * HALF],
                                      start=k == 0 and s == 0, stop=k == KT - 1 and s == 2)
                                if k == KT - 1 and s == 2:
                                    o.then_inc(proj_full, 1)

            def tokens_ready(at):
                k, h = at
                if k == 0:
                    pe.wait_ge(h_hi_ok, TILES * (h + 1))
                    pe.wait_ge(h_lo_ok, TILES // 2 * (h + 1))
                    pe.wait_ge(h_lo_v, TILES // 2 * (h + 1))

            def spread_factors(n, diagonal):
                pe.wait_ge(rs_diag, n)
                for h in range(2):
                    M(ps[4 + h][:], ones[:], diagonal[:, h * HALF:(h + 1) * HALF], start=True, stop=True)\
                        .then_inc(rs_full, 1)

            pe.wait_ge(mask_step, 3)
            for i in range(TILES):
                pe.wait_ge(x_in[i % 2], 16 * (i // 2 + 1))
                turn(lambda k: xs[i % 2][:, k * P:(k + 1) * P], i)
            unit(0, 0, h_hi, h_lo, tokens_ready, parts=((0,), (1,)))
            pe.wait_ge(h_raw_ok, 2 * TILES)
            spread_factors(1, xs[0])
            unit(0, 1, h_hi, h_lo)
            with pe.Fori(1, Q0 // 2) as i:
                for p in range(2):
                    pe.wait_ge(dve_read, 4 * i + 2 * p - 2)
                    unit(i, p, h_hi, h_lo)

            def proj(n):
                pe.wait_ge(dve_read, 2 * n - 2)
                unit(n // 2, n % 2, h_hi, h_lo)

            def mix(_):
                pe.wait_ge(dve_read, 2 * N_IN)

            def shifted(_):
                pe.wait_ge(z_ok, N_SHIFT)
                pe.wait_ge(consts_in, 96)
                pe.wait_ge(masks_ok, 2)

            def four(name, t, f):
                wait_bank(pe, name, t)
                for a in range(PAIRS):
                    o = f(bank(name)[:, a * P:(a + 1) * P], a)
                o.then_inc(filled(name), 1)

            def heads(name, t, f):
                wait_bank(pe, name, t)
                for h in range(HEADS):
                    o = f(bank(name)[:, h * HEAD:(h + 1) * HEAD], h, *divmod(h, 2))
                o.then_inc(filled(name), 1)

            def product(to, w, m):
                return M(to, w, m, start=True, stop=True)

            def turned(to, src):
                return nc.tensor.transpose(to, src, ident[:])

            def lora(t):
                need("tw", t + 1)
                four("lora_w", t, lambda to, a: product(to, w2a2_s[0:64, a * P:(a + 1) * P], tw[0:64, :]))
                four("lora_a", t, lambda to, a: product(to, w2a2_s[64:P, a * P:(a + 1) * P], zT[64:P, RWA, tile(t)]))

            def ssq(t):
                need("ksq", t + 1)
                wait_bank(pe, "ss", t)
                for a in range(PAIRS):
                    o = product(bank("ss")[:, 2 * a:2 * a + 2], k2[:, a, :], pair_sel[:])
                o.then_inc(filled("ss"), 1)

            def norm_T(t):
                need("rn", t + 1)
                wait_bank(pe, "rnT", t)
                turned(bank("rnT")[0:HEADS, 0:P], rn8[:]).then_inc(filled("rnT"), 1)

            def rx(t):
                need("rnT", t + 1)
                four("rx", t, lambda to, a: product(to, head_up[0:HEADS, a * P:(a + 1) * P], rn_T))

            def tr_ab(t):
                need("ah", t + 1)
                four("tr_a", t, lambda to, a: turned(to, cs[:, a, :]))
                need("bh", t + 1)
                four("tr_b", t, lambda to, a: turned(to, dm[:, a, :]))

            def tr_k(t):
                need("kh", t + 1)
                four("tr_k", t, lambda to, a: turned(to, e2[:, a, :]))

            def bonus_(t):
                need("rk", t + 1)
                wait_bank(pe, "bonus", t)
                for a in range(PAIRS):
                    o = product(bank("bonus")[:, 2 * a:2 * a + 2], e1[:, a, :], rk_w[:, a, :])
                o.then_inc(filled("bonus"), 1)

            def tr_v(t):
                four("tr_v", t, lambda to, a: turned(to, zT[:, RV0 + a, tile(t)]))
                wait_bank(pe, "vt", t)
                turned(bank("vt")[:, 0:P], zT[:, V0, tile(t)]).then_inc(filled("vt"), 1)

            def attend(groups):
                def queries_keys(t):
                    lo = P if t == 0 else 0
                    for g, name in groups:
                        wait_bank(pe, name, t)
                        par = g % 2
                        for i in range(2):
                            o = product(bank(name)[:, 2 * P * i + lo:2 * P * (i + 1)],
                                        halves(zT, par)[:, Q0 + 2 * (g // 2) + i, tile(t)],
                                        halves(zT, par)[:, K0, t * P - P + lo:t * P + P])
                        o.then_inc(filled(name), 1)
                return queries_keys

            def probs_T(groups):
                def turn_probs(t):
                    for g, name in groups:
                        need("p", 8 * t + 2 * g + 2)
                        wait_bank(pe, name, t)
                        for i in range(2):
                            for k in range(1 if t == 0 else 0, 2):
                                q = 2 * i + k
                                o = turned(bank(name)[:, q * P:(q + 1) * P], sc[g][:, i, k * P:(k + 1) * P])
                        o.then_inc(filled(name), 1)
                return turn_probs

            def weighted(groups):
                def heads_of(t):
                    if 0 in groups:
                        wait_bank(pe, "o", t)
                        need("va_tok", t + 1)
                    for g in groups:
                        need("pT", 4 * t + g + 1)
                        for i in range(2):
                            c = slot(g, i)
                            kv = g % 2
                            for k in range(1 if t == 0 else 0, 2):
                                o = M(bank("o")[:, c * HEAD:(c + 1) * HEAD], sc[g][:, i, k * P:(k + 1) * P],
                                      va_tok[(t - 1 + k) % 2][:, kv * HEAD:(kv + 1) * HEAD],
                                      start=k == 0 or t == 0, stop=k == 1)
                    if 3 in groups:
                        o.then_inc(filled("o"), 1)
                return heads_of

            def o_T(t):
                need("o", t + 1)
                o_tok = view(sc[0][:].rearrange("p a b -> p (a b)"), PAIRS)
                four("oT", t, lambda to, a: turned(to, o_tok[:, a, :]))

            def scores(name, keys, queries, *ready):
                def keys_queries(t):
                    for r in ready:
                        need(r, t + 1)
                    for g in range(2):
                        wait_bank(pe, f"{name}{g}", t)
                    for a in range(PAIRS):
                        for g in range(2):
                            o = product(bank(f"{name}{g}")[:, a * P:(a + 1) * P], halves(keys, g)[:, a, :],
                                        halves(queries, g)[:, a, :])
                            if a == PAIRS - 1:
                                o.then_inc(filled(f"{name}{g}"), 1)
                return keys_queries

            def xt(t):
                for g in range(2):
                    need(f"XT1_{g}", t + 1)
                    four(f"xt{g}", t, lambda to, a: turned(to, XT[g][:, a, :]))

            def lv(t):
                need("LakT", 2 * t + 2)
                need("V_tok", t + 1)
                heads("lv", t, lambda to, h, a, g: product(to, LakT[g][:, a, :], V_tok[t % 2][:, h, :]))

            turns = 2 * (LEVELS - 1)

            def y(k):
                def level_y(t):
                    for g in range(2):
                        if k == 1:
                            need(f"LI{g}", t + 1)
                        need("X", turns * t + 2 * (k - 1) + g + 1)
                        four(f"y{g}_{k}", t, lambda to, a: product(to, LT[g][:, a, :], X[g][:, a, :]))
                return level_y

            def tx(k):
                def turn_x(t):
                    for g in range(2):
                        four(f"tx{g}_{k}", t, lambda to, a: turned(to, X[g][:, a, :]))
                return turn_x

            def z(k):
                def level_z(t):
                    for g in range(2):
                        need("IY", turns * t + 2 * (k - 1) + g + 1)
                        if k > 1:
                            need("XT", turns * t + 2 * (k - 2) + g + 1)
                        if k < LEVELS - 1:
                            four(f"z{g}_{k}", t, lambda to, a: product(to, XT[g][:, a, :], IY[g][:, a, :]))
                        else:
                            four(f"z{g}_{k}", t, lambda to, a: product(to, IY[g][:, a, :], XT[g][:, a, :]))
                return level_z

            def wg(t):
                need("XT", turns * (t + 1))
                need("A_tok", t + 1)
                need("LV", t + 1)
                b = t % 2
                for i in range(2):
                    four(f"wg{i}", t, lambda to, j: product(
                        to, XT[j % 2][:, (PAIRS * i + j) // 2, :], A_LV[:, b::2 - b, PAIRS * i + j, :]))

            def rq_(t):
                need("WG0", t + 1)
                need("MrbT", 2 * t + 2)
                wait_bank(pe, "rq", t)
                for h in range(HEADS):
                    if h == PAIRS:
                        need("WG1", t + 1)
                    a, g = divmod(h, 2)
                    o = product(halves(bank("rq"), g)[:, a * P:(a + 1) * P], W_s[:, h, :], MrbT[g][:, a, :])
                o.then_inc(filled("rq"), 1)

            def transition(c):
                def over_chunk(t):
                    b = t % 2
                    need("B_tok", t + 1)
                    need("K_tok", t + 1)
                    wait_bank(pe, f"c{c}", t)
                    for h in range(HEADS):
                        a, g = divmod(h, 2)
                        to = halves(bank(f"c{c}"), g)[:, a * P:(a + 1) * P]
                        row = slice(c * CHUNK, (c + 1) * CHUNK)
                        product(to[:, 0:HEAD], W_s[row, h, :], B_tok[b][row, h, :])
                        M(to[:, HEAD:], B_tok[b][row, h, :], G_s[row, h, :], start=True, stop=False)
                        o = M(to[:, HEAD:], K_tok[b][row, h, :], V_tok[b][row, h, :], start=False, stop=True)
                    o.then_inc(filled(f"c{c}"), 1)
                return over_chunk

            def advance(c):
                def next_state(t):
                    need("zero", 1)
                    need("phi", 4 * t + 2 * c + 2)
                    need("state", 2 * t + c)
                    four(f"st{c}", t, lambda to, a: product(to, phi[c][:, a, :], state[c][:, a, :]))
                return next_state

            def yy(a):
                def outputs(t):
                    b = t % 2
                    if a == 0:
                        need("QT", t + 1)
                        need("MrkT", 2 * t + 2)
                        need("state", 2 * t + 1)
                        wait_bank(pe, "yy", t)
                    for c in range(CHUNKS):
                        row = slice(c * CHUNK, (c + 1) * CHUNK)
                        M(bank("yy")[row, a * P:(a + 1) * P], QT[:, a, row], state[c][:, a, :], start=True, stop=False,
                          skip_group_check=True)
                    for g in range(2):
                        h = 2 * a + g
                        to = bank("yy")[:, h * HEAD:(h + 1) * HEAD]
                        M(to, MrbT[g][:, a, :], G_s[:, h, :], start=False, stop=False, skip_group_check=True)
                        o = M(to, MrkT[g][:, a, :], V_tok[b][:, h, :], start=False, stop=g == 1, skip_group_check=True)
                    if a == PAIRS - 1:
                        o.then_inc(filled("yy"), 1)
                return outputs

            def gate_(t):
                need("gg", t + 1)
                wait_bank(pe, "gate", t)
                product(bank("gate")[:], gs[t % 2][:], g2_s[:]).then_inc(filled("gate"), 1)

            def out_T(t):
                need("yn5", t + 1)
                four("outT", t, lambda to, a: turned(to, yc[:, a, :]))

            def residual(i):
                pe.wait_ge(x_in[i % 2], 16 * (TILES // 2 + i // 2 + 1))
                for j, name in enumerate(("res_a", "res_b")):
                    four(name, i, lambda to, a: turned(to, xs3[i % 2][:, (4 * j + a) * P:(4 * j + a + 1) * P]))

            def mixed_ready(k):
                if k in LOW_V:
                    pe.wait_ge(o_lo_v, LOW_V.index(k) + 1)
                else:
                    pe.wait_ge(o_lo_ok, LOW_POOL.index(k) + 1)

            def out_a(_):
                for b in range(2):
                    wait_read(pe, *BANK_USES[b][-1])
                unit(N_IN // 2, 0, u_hi, u_lo, mixed_ready, blocks=range(EARLY))

            def out_b(_):
                unit(N_IN // 2, 0, u_hi, u_lo, mixed_ready, blocks=range(EARLY, KT))

            run({"proj": proj, "shifted": shifted, "mix": mix, "out_a": out_a, "out_b": out_b,
                 "lora": lora, "ssq": ssq, "res": residual, "rnT": norm_T, "rx": rx,
                 "tr_ab": tr_ab, "tr_k": tr_k, "tr_v": tr_v, "bonus": bonus_,
                 "sc_a": attend([(0, "sc00"), (1, "sc10")]), "sc_b": attend([(2, "sc01"), (3, "sc11")]),
                 "pt_a": probs_T([(0, "pt00"), (1, "pt10")]), "pt_b": probs_T([(2, "pt01"), (3, "pt11")]),
                 "o_a": weighted((0, 1)), "o_b": weighted((2, 3)), "oT": o_T,
                 "lab": scores("lab", bt, at, "bt", "at"), "lak": scores("lak", kt, at, "kt"),
                 "mrb": scores("mrb", bt, rt, "rt"), "mrk": scores("mrk", kt, rt),
                 "xt": xt, "lv": lv, "wg": wg, "rq": rq_, "c_a": transition(0), "c": transition(1),
                 "st0": advance(0), "st1": advance(1), "gate": gate_, "outT": out_T}
                | {f"yy{a}": yy(a) for a in range(PAIRS)}
                | {f"y{k}": y(k) for k in range(1, LEVELS)} | {f"z{k}": z(k) for k in range(1, LEVELS)}
                | {f"tx{k}": tx(k) for k in range(2, LEVELS)})

            for uses in BANK_USES.values():
                wait_read(pe, *uses[-1])
            unit(N_IN // 2, 1, u_hi, u_lo)
            with pe.Fori(1, N_OUT // 2) as i:
                for p in range(2):
                    pe.wait_ge(dve_read, 2 * N_IN + 4 * i + 2 * p - 2)
                    unit(N_IN // 2 + i, p, u_hi, u_lo)

            def block_ready(k):
                pe.wait_ge(n_lo_ok, k + 1)

            def up(g, first=False):
                for p in range(2):
                    pe.wait_ge(dve_read, 2 * (N_IN + N_OUT + 8 * g) - 2 * (1 - p))
                    if first:
                        unit(U_UP // 2, p, n_hi, n_lo, block_ready)
                        if p == 0:
                            pe.wait_ge(x2_acc, N_OUT)
                            for i in range(TILES):
                                o = M(ps[4][:, i:i + 1], acc3[:, tile(i)], ones[:, 0:1], start=True, stop=True)
                            o.then_inc(ss3_full, 1)
                        else:
                            spread_factors(2, sq3[1])
                    else:
                        unit(U_UP // 2 + 8 * g, p, n_hi, n_lo)
                with pe.Fori(1, 4) as i:
                    for p in range(2):
                        pe.wait_ge(act_read, 2 * (8 * g + 2 * i + p - 1))
                        unit(U_UP // 2 + 8 * g + i, p, n_hi, n_lo)

            def down(g):
                def inside_ready(k):
                    if k == 0 or k == KT - 1:
                        pe.wait_ge(u_lo_ok, 8 * g + (KT if k else KT - 1))

                with pe.Fori(0, 4) as i:
                    for p in range(2):
                        pe.wait_ge(act_read, 2 * (8 * g + 8) - 2 * (1 - p))
                        pe.wait_ge(dve_read, 2 * (N_IN + N_OUT + 8 * g + 2 * i + p - 1))
                        unit(U_UP // 2 + 8 * g + 4 + i, p, u_hi, u_lo, inside_ready)

            up(0, first=True)
            down(0)
            with pe.Fori(1, GROUPS) as g:
                up(g)
                down(g)
            pe.wait_ge(dve_read, 2 * (N_IN + N_OUT + 8 * GROUPS))
            pe.wait_ge(fin_gain, PAIRS)
            for s, (i, j) in enumerate(TURNS):
                if s == 4:
                    pe.wait_ge(fin_acc, KT)
                    for c in range(TILES):
                        o = M(ps[0][:, c:c + 1], acc3[:, tile(c)], ones[:, 0:1], start=True, stop=True)
                    o.then_inc(fin_ss, 1)
                    pe.wait_ge(fin_gain, KT)
                if s >= TURN_BANKS:
                    before, half = TURNS[s - TURN_BANKS]
                    pe.wait_ge(fin_a if half else fin_v, before + 1)
                to = ps[1 + s % TURN_BANKS]
                for k in range(4):
                    o = nc.tensor.transpose(to[:, k * P:(k + 1) * P], x2[:, 4 * j + k, tile(i)], ident[:])
                o.then_inc(tr_full, 1)


def kernel(x, attn_norm_g, w_in, attn_sinks, rwkv_mu, w0, w2, a0, a2, g2, k_k, k_a, r_k,
           ln_x_w, ln_x_b, w_out, mlp_norm_g, w_up, w_down, final_norm_g):
    import numpy as np
    import concourse.bacc as bacc
    from concourse.bass_utils import run_bass_kernel_spmd as run

    def arr(a):
        return np.ascontiguousarray(a)

    def blocks(v):
        return np.asarray(v).reshape(-1, P).T

    def units(w):
        n = w.shape[1] // P
        return w.reshape(KT, P, n, P).transpose(2, 1, 0, 3).reshape(n, P, KT * P)

    wi = np.asarray(w_in)[0]
    q = wi[:, :512].reshape(D, 2, 4, HEAD).transpose(0, 2, 1, 3).reshape(D, 512)
    wo = np.asarray(w_out)[0]
    o = wo[:512].reshape(2, 4, HEAD, D).transpose(1, 0, 2, 3).reshape(512, D)
    wu, wd = np.asarray(w_up)[0], np.asarray(w_down)[0]
    parts = [units(np.concatenate([wi[:, 768:], q, wi[:, 512:768]], 1)), units(np.concatenate([o, wo[512:]], 0))]
    for g in range(GROUPS):
        parts += [units(wu[:, g * 1024:(g + 1) * 1024]), units(wd[g * 1024:(g + 1) * 1024])]
    vec = np.concatenate([blocks(v) for v in (rwkv_mu, w0, a0, k_k, k_a, r_k, attn_norm_g, mlp_norm_g,
                                       final_norm_g)], 1)
    ins = {
        "x": arr(x),
        "w_all": arr(np.concatenate(parts, 0)),
        "vec": arr(vec),
        "sinks": arr(np.asarray(attn_sinks).reshape(2, 4).T.reshape(1, HEADS)),
        "w2a2": arr(np.concatenate([np.asarray(w2)[0], np.asarray(a2)[0]], 0)),
        "g2": arr(np.asarray(g2)[0]),
        "ln_w": arr(ln_x_w), "ln_b": arr(ln_x_b),
    }
    nc = bacc.Bacc("TRN2", target_bir_lowering=False, num_devices=1)
    aps = [nc.dram_tensor(f"in_{n}", a.shape, F32, kind="ExternalInput").ap() for n, a in ins.items()]
    out = nc.dram_tensor("out_0", x.shape, F32, kind="ExternalOutput").ap()
    build(nc, *aps, out)
    r = run(nc, [{f"in_{n}": a for n, a in ins.items()}], core_ids=[0])
    return r.results[0]["out_0"]
```
